# Optimizing a Trainium2 kernel written in Bass

```python
import jax
import jax.numpy as jnp
from jax import lax
import numpy as np
import math
import jax, jax.numpy as jnp

D_MODEL = 1024
BATCH = 1
SEQ = 1024
DEPTH = 1

GRID_W = 64
CTX_LEN = 256
HEAD_DIM = 64
ATTN_WIDTH = D_MODEL // 2
N_Q_HEADS = ATTN_WIDTH // HEAD_DIM
N_KV_HEADS = N_Q_HEADS // 4
Q_PER_KV = N_Q_HEADS // N_KV_HEADS
KV_WIDTH = N_KV_HEADS * HEAD_DIM
WINDOW = 128
BLOCK = 128
ROPE_BASE = 10000.0
RWKV_WIDTH = D_MODEL // 2
RWKV_HEAD_DIM = 64
RWKV_HEADS = RWKV_WIDTH // RWKV_HEAD_DIM
DECAY_LORA = 32
ICLR_LORA = 32
GATE_LORA = 96
RWKV_IN_WIDTH = 3 * RWKV_WIDTH + DECAY_LORA + ICLR_LORA + GATE_LORA
SHORT_CONV = 3
N_BRANCHES = 2
IN_WIDTH = ATTN_WIDTH + 2 * KV_WIDTH + RWKV_IN_WIDTH + N_BRANCHES * D_MODEL
D_FF = 4 * D_MODEL
N_MOD = 6
NORM_EPS = 1e-6
LNX_EPS = 1e-5 * RWKV_HEAD_DIM
IN_SPLITS = [ATTN_WIDTH, ATTN_WIDTH + KV_WIDTH, ATTN_WIDTH + 2 * KV_WIDTH,
             ATTN_WIDTH + 2 * KV_WIDTH + RWKV_IN_WIDTH]
RW_SPLITS = [RWKV_WIDTH, 2 * RWKV_WIDTH, 3 * RWKV_WIDTH,
             3 * RWKV_WIDTH + DECAY_LORA, 3 * RWKV_WIDTH + DECAY_LORA + ICLR_LORA]


def rmsnorm(x, g):
    xf = x.astype(jnp.float32)
    y = xf * lax.rsqrt(jnp.mean(xf * xf, axis=-1, keepdims=True) + NORM_EPS)
    return (y * g.astype(jnp.float32)).astype(x.dtype)

def modulate(h, shift, scale):
    return h * (1 + scale) + shift

def axial_rope_tables(rows):
    n_freq = HEAD_DIM // 4
    inv_freq = jnp.power(ROPE_BASE, -jnp.arange(n_freq, dtype=jnp.float32) / n_freq)
    row = jnp.repeat(jnp.arange(rows, dtype=jnp.float32), GRID_W)
    col = jnp.tile(jnp.arange(GRID_W, dtype=jnp.float32), rows)
    ang = jnp.concatenate([row[:, None] * inv_freq, col[:, None] * inv_freq], axis=-1)
    return jnp.cos(ang), jnp.sin(ang)

def apply_rope(x, cos, sin):
    half = x.shape[-1] // 2
    x1, x2 = x[..., :half], x[..., half:]
    c = cos[:, None, :].astype(x.dtype)
    s = sin[:, None, :].astype(x.dtype)
    return jnp.concatenate([x1 * c - x2 * s, x1 * s + x2 * c], axis=-1)

def sink_column(sink, lead_shape):
    s = sink.astype(jnp.float32).reshape(N_KV_HEADS, Q_PER_KV)
    return jnp.broadcast_to(s[:, :, None, None], lead_shape + (1,))

def latent_window_attention(q, k, v, kc, vc, sink):
    B, L, _, dh = q.shape
    Lc = kc.shape[1]
    nb = L // BLOCK
    scale = dh ** -0.5
    qb = q.reshape(B, nb, BLOCK, N_KV_HEADS, Q_PER_KV, dh)
    pad = ((0, 0), (BLOCK, BLOCK), (0, 0), (0, 0))

    def band(t):
        tb = jnp.pad(t, pad).reshape(B, nb + 2, BLOCK, N_KV_HEADS, dh)
        return jnp.concatenate([tb[:, :-2], tb[:, 1:-1], tb[:, 2:]], axis=2)

    kb, vb = band(k), band(v)
    s_loc = jnp.einsum('bnqgrd,bnkgd->bngrqk', qb, kb).astype(jnp.float32) * scale
    s_ctx = jnp.einsum('bnqgrd,bcgd->bngrqc', qb, kc).astype(jnp.float32) * scale
    blk = jnp.arange(nb)[:, None, None]
    qi = jnp.arange(BLOCK)[None, :, None]
    kj = jnp.arange(3 * BLOCK)[None, None, :]
    i_pos = blk * BLOCK + qi
    j_pos = blk * BLOCK - BLOCK + kj
    valid = (jnp.abs(i_pos - j_pos) <= WINDOW) & (j_pos >= 0) & (j_pos < L)
    s_loc = jnp.where(valid[None, :, None, None], s_loc, -jnp.inf)
    s_sink = jnp.broadcast_to(sink.astype(jnp.float32).reshape(N_KV_HEADS, Q_PER_KV)[None, None, :, :, None, None],
                              s_loc.shape[:-1] + (1,))
    p = jax.nn.softmax(jnp.concatenate([s_loc, s_ctx, s_sink], axis=-1), axis=-1)
    p_loc = p[..., :3 * BLOCK].astype(v.dtype)
    p_ctx = p[..., 3 * BLOCK:3 * BLOCK + Lc].astype(v.dtype)
    o = (jnp.einsum('bngrqk,bnkgd->bnqgrd', p_loc, vb)
         + jnp.einsum('bngrqc,bcgd->bnqgrd', p_ctx, vc))
    return o.reshape(B, L, N_Q_HEADS * dh)

def context_attention(qc, kc, vc, sink):
    B, Lc, _, dh = qc.shape
    qg = qc.reshape(B, Lc, N_KV_HEADS, Q_PER_KV, dh)
    s = jnp.einsum('bqgrd,bkgd->bgrqk', qg, kc).astype(jnp.float32) * dh ** -0.5
    s_sink = sink_column(sink, s.shape[1:-1])[None]
    s_sink = jnp.broadcast_to(s_sink, s.shape[:-1] + (1,))
    p = jax.nn.softmax(jnp.concatenate([s, s_sink], axis=-1), axis=-1)
    o = jnp.einsum('bgrqk,bkgd->bqgrd', p[..., :Lc].astype(vc.dtype), vc)
    return o.reshape(B, Lc, N_Q_HEADS * dh)

def short_conv(u, w):
    L = u.shape[1]
    half = SHORT_CONV // 2
    up = jnp.pad(u, ((0, 0), (half, half), (0, 0)))
    return sum(up[:, t:t + L] * w[t] for t in range(SHORT_CONV))

def rwkv_prepare(u, decay_w0, decay_w2, iclr_a0, iclr_a2, k_k, k_a):
    B, L, _ = u.shape
    r, k, v, hw, ha, hg = jnp.split(u, RW_SPLITS, axis=-1)

    def heads(t):
        return t.astype(jnp.float32).reshape(B, L, RWKV_HEADS, RWKV_HEAD_DIM)

    kk = heads(k * k_k)
    kk = kk * lax.rsqrt(jnp.maximum(jnp.sum(kk * kk, axis=-1, keepdims=True), 1e-24))
    dirs = []
    for d in range(2):
        w_log = -jax.nn.softplus(-(decay_w0[d] + jnp.tanh(hw) @ decay_w2[d])) - 0.5
        a = jax.nn.sigmoid(iclr_a0[d] + ha @ iclr_a2[d])
        decay = jnp.exp(-jnp.exp(heads(w_log)))
        k_d = heads(k * (1 + (a - 1) * k_a))
        dirs.append((decay, kk * heads(a), k_d))
    return heads(r), heads(v), hg, kk, dirs

def wkv7_scan(S0, r, decay, kk, b, k, v, reverse, emit):
    xs = tuple(jnp.moveaxis(t, 1, 0) for t in (r, decay, kk, b, k, v))

    def step(S, inp):
        r_t, w_t, kk_t, b_t, k_t, v_t = inp
        sa = jnp.einsum('bhvk,bhk->bhv', S, -kk_t)
        S = S * w_t[:, :, None, :] + sa[..., None] * b_t[:, :, None, :] + v_t[..., None] * k_t[:, :, None, :]
        y = jnp.einsum('bhvk,bhk->bhv', S, r_t) if emit else None
        return S, y

    S, ys = lax.scan(step, S0, xs, reverse=reverse)
    return S, (jnp.moveaxis(ys, 0, 1) if emit else None)

def rwkv_output(y, r, v, hg, dirs, gate_g2, r_k, lnx_w, lnx_b):
    B, L = y.shape[:2]
    mu = jnp.mean(y, axis=-1, keepdims=True)
    var = jnp.mean(jnp.square(y - mu), axis=-1, keepdims=True)
    yn = (y - mu) * lax.rsqrt(var + LNX_EPS)
    k_sum = dirs[0][2] + dirs[1][2]
    bonus = jnp.sum(r * k_sum * r_k.astype(jnp.float32), axis=-1, keepdims=True) * v
    out = (yn.reshape(B, L, RWKV_WIDTH) * lnx_w + lnx_b + bonus.reshape(B, L, RWKV_WIDTH)).astype(hg.dtype)
    g = jax.nn.sigmoid(hg) @ gate_g2
    return out * g

def merge_branches(ya, yr, gate_logits, w_branch_attn, w_branch_rwkv, w_out):
    ga, gr = jnp.split(jax.nn.sigmoid(gate_logits), N_BRANCHES, axis=-1)
    return (ga * (ya @ w_branch_attn) + gr * (yr @ w_branch_rwkv)) @ w_out

def sq_relu_mlp(h, w_up, w_down):
    return jnp.square(jax.nn.relu(h @ w_up)) @ w_down

def trunk_layer(x, xc, c, c_ctx, cos, sin, w_ada, b_ada, norm1_g, w_in, sink, conv_w,
                decay_w0, decay_w2, iclr_a0, iclr_a2, gate_g2, k_k, k_a, r_k, lnx_w, lnx_b,
                w_branch_attn, w_branch_rwkv, w_out, norm2_g, w_mlp_up, w_mlp_down, update_ctx):
    B, L, D = x.shape
    Lc = xc.shape[1]
    mod = (jax.nn.silu(c) @ w_ada + b_ada).reshape(B, 1, N_MOD, D)
    shift1, scale1, gate1, shift2, scale2, gate2 = [mod[:, :, i] for i in range(N_MOD)]
    modc = (jax.nn.silu(c_ctx) @ w_ada + b_ada).reshape(N_MOD, D)

    h = modulate(rmsnorm(x, norm1_g), shift1, scale1)
    hc = modulate(rmsnorm(xc, norm1_g), modc[0], modc[1])
    q, k, v, rw, gl = jnp.split(h @ w_in, IN_SPLITS, axis=-1)
    qc, kc, vc, rwc, glc = jnp.split(hc @ w_in, IN_SPLITS, axis=-1)

    q = apply_rope(q.reshape(B, L, N_Q_HEADS, HEAD_DIM), cos, sin)
    k = apply_rope(k.reshape(B, L, N_KV_HEADS, HEAD_DIM), cos, sin)
    v = v.reshape(B, L, N_KV_HEADS, HEAD_DIM)
    kc = kc.reshape(B, Lc, N_KV_HEADS, HEAD_DIM)
    vc = vc.reshape(B, Lc, N_KV_HEADS, HEAD_DIM)
    ya = latent_window_attention(q, k, v, kc, vc, sink)

    r_l, v_l, hg_l, kk_l, dirs_l = rwkv_prepare(short_conv(rw, conv_w), decay_w0, decay_w2,
                                               iclr_a0, iclr_a2, k_k, k_a)
    r_c, v_c, hg_c, kk_c, dirs_c = rwkv_prepare(short_conv(rwc, conv_w), decay_w0, decay_w2,
                                               iclr_a0, iclr_a2, k_k, k_a)
    S0 = jnp.zeros((B, RWKV_HEADS, RWKV_HEAD_DIM, RWKV_HEAD_DIM), jnp.float32)
    y_lat = []
    y_ctx = []
    for d, rev in enumerate((False, True)):
        dec_c, b_c, k_c = dirs_c[d]
        S_ctx, yc_d = wkv7_scan(S0, r_c, dec_c, kk_c, b_c, k_c, v_c, rev, update_ctx)
        dec_l, b_l, k_l = dirs_l[d]
        _, y_d = wkv7_scan(S_ctx, r_l, dec_l, kk_l, b_l, k_l, v_l, rev, True)
        y_lat.append(y_d)
        y_ctx.append(yc_d)
    yr = rwkv_output(y_lat[0] + y_lat[1], r_l, v_l, hg_l, dirs_l, gate_g2, r_k, lnx_w, lnx_b)

    x = x + gate1 * merge_branches(ya, yr, gl, w_branch_attn, w_branch_rwkv, w_out)
    x = x + gate2 * sq_relu_mlp(modulate(rmsnorm(x, norm2_g), shift2, scale2), w_mlp_up, w_mlp_down)

    if update_ctx:
        yac = context_attention(qc.reshape(B, Lc, N_Q_HEADS, HEAD_DIM), kc, vc, sink)
        yrc = rwkv_output(y_ctx[0] + y_ctx[1], r_c, v_c, hg_c, dirs_c, gate_g2, r_k, lnx_w, lnx_b)
        xc = xc + modc[2] * merge_branches(yac, yrc, glc, w_branch_attn, w_branch_rwkv, w_out)
        xc = xc + modc[5] * sq_relu_mlp(modulate(rmsnorm(xc, norm2_g), modc[3], modc[4]), w_mlp_up, w_mlp_down)
    return x, xc

def first_inputs(seed: int = 0) -> dict:
    key = jax.random.key(seed)
    ks = iter(jax.random.split(key, 32))

    def nrm(shape, s):
        return jax.random.normal(next(ks), shape, jnp.float32) * s

    D = D_MODEL
    L = DEPTH
    conv_base = jnp.asarray([0.25, 1.0, 0.25], jnp.float32)[None, :, None]
    return {
        "x": nrm((BATCH, SEQ, D), 1.0),
        "c": nrm((BATCH, D), 1.0),
        "ctx": nrm((BATCH, CTX_LEN, D), 1.0),
        "c_ctx": nrm((D,), 1.0),
        "w_ada": nrm((L, D, N_MOD * D), 0.5 * D ** -0.5),
        "b_ada": nrm((L, N_MOD * D), 0.02),
        "norm1_g": 1.0 + nrm((L, D), 0.05),
        "w_in": nrm((L, D, IN_WIDTH), D ** -0.5),
        "sink": nrm((L, N_Q_HEADS), 0.5),
        "conv_w": conv_base + nrm((L, SHORT_CONV, RWKV_IN_WIDTH), 0.05),
        "decay_w0": nrm((L, 2, RWKV_WIDTH), 0.5),
        "decay_w2": nrm((L, 2, DECAY_LORA, RWKV_WIDTH), DECAY_LORA ** -0.5),
        "iclr_a0": nrm((L, 2, RWKV_WIDTH), 0.5),
        "iclr_a2": nrm((L, 2, ICLR_LORA, RWKV_WIDTH), ICLR_LORA ** -0.5),
        "gate_g2": nrm((L, GATE_LORA, RWKV_WIDTH), GATE_LORA ** -0.5),
        "k_k": 1.0 + nrm((L, RWKV_WIDTH), 0.1),
        "k_a": 1.0 + nrm((L, RWKV_WIDTH), 0.1),
        "r_k": nrm((L, RWKV_HEADS, RWKV_HEAD_DIM), 0.1),
        "lnx_w": 1.0 + nrm((L, RWKV_WIDTH), 0.05),
        "lnx_b": nrm((L, RWKV_WIDTH), 0.02),
        "w_branch_attn": nrm((L, ATTN_WIDTH, D), ATTN_WIDTH ** -0.5),
        "w_branch_rwkv": nrm((L, RWKV_WIDTH, D), RWKV_WIDTH ** -0.5),
        "w_out": nrm((L, D, D), D ** -0.5),
        "norm2_g": 1.0 + nrm((L, D), 0.05),
        "w_mlp_up": nrm((L, D, D_FF), D ** -0.5),
        "w_mlp_down": nrm((L, D_FF, D), D_FF ** -0.5),
        "norm_f_g": 1.0 + nrm((D,), 0.05),
    }

def first_block(x, c, ctx, c_ctx, w_ada, b_ada, norm1_g, w_in, sink, conv_w, decay_w0, decay_w2,
              iclr_a0, iclr_a2, gate_g2, k_k, k_a, r_k, lnx_w, lnx_b, w_branch_attn, w_branch_rwkv,
              w_out, norm2_g, w_mlp_up, w_mlp_down, norm_f_g):
    rows = x.shape[1] // GRID_W
    cos, sin = axial_rope_tables(rows)
    xc = ctx
    for l in range(DEPTH):
        x, xc = trunk_layer(x, xc, c, c_ctx, cos, sin, w_ada[l], b_ada[l], norm1_g[l], w_in[l], sink[l],
                            conv_w[l], decay_w0[l], decay_w2[l], iclr_a0[l], iclr_a2[l], gate_g2[l],
                            k_k[l], k_a[l], r_k[l], lnx_w[l], lnx_b[l], w_branch_attn[l], w_branch_rwkv[l],
                            w_out[l], norm2_g[l], w_mlp_up[l], w_mlp_down[l], update_ctx=(l < DEPTH - 1))
    return rmsnorm(x, norm_f_g)


DEPTH_2 = 2

MEM_LEN = 256
N_MIX_HEADS = D_MODEL // HEAD_DIM
N_MEM_HEADS = 4
N_TOK_HEADS = N_MIX_HEADS - N_MEM_HEADS
TOK_WIDTH = N_TOK_HEADS * HEAD_DIM
MEM_WIDTH = N_MEM_HEADS * HEAD_DIM
MIX_WIDTH = TOK_WIDTH + MEM_WIDTH
Q_LORA = 384
KV_LORA = 256
QK_NOPE = 64
QK_ROPE = 32
V_DIM = HEAD_DIM
QK_DIM = QK_NOPE + QK_ROPE
ROPE_THETA = 10000.0
Q_BLOCK = 128
CONV_W = 4
LRU_C = 8.0
N_LRU_BLOCKS = N_TOK_HEADS
LRU_BLOCK = TOK_WIDTH // N_LRU_BLOCKS
ALPHA = (2.0 * DEPTH_2) ** 0.25
BETA = (8.0 * DEPTH_2) ** -0.25
N_MLA = (DEPTH_2 + 1) // 2
N_LRU = DEPTH_2 // 2
MLA_IN = Q_LORA + KV_LORA + QK_ROPE + MIX_WIDTH + MEM_WIDTH
LRU_IN = TOK_WIDTH + MIX_WIDTH + MEM_WIDTH


def _split(t, sizes):
    idx = np.cumsum(sizes)[:-1].tolist()
    return jnp.split(t, idx, axis=-1)

def rms_norm(t, g):
    t32 = t.astype(jnp.float32)
    t32 = t32 * lax.rsqrt(jnp.mean(t32 * t32, axis=-1, keepdims=True) + NORM_EPS)
    return (t32 * g.astype(jnp.float32)).astype(t.dtype)

def layer_norm(t, g, b):
    t32 = t.astype(jnp.float32)
    mu = jnp.mean(t32, axis=-1, keepdims=True)
    var = jnp.mean(jnp.square(t32 - mu), axis=-1, keepdims=True)
    y = (t32 - mu) * lax.rsqrt(var + NORM_EPS)
    return (y * g.astype(jnp.float32) + b.astype(jnp.float32)).astype(t.dtype)

def apply_rope_2(t, positions):
    half = t.shape[-1] // 2
    inv_freq = ROPE_THETA ** (-jnp.arange(half, dtype=jnp.float32) / half)
    ang = positions.astype(jnp.float32)[..., None] * inv_freq
    cos = jnp.cos(ang)[:, :, None, :].astype(t.dtype)
    sin = jnp.sin(ang)[:, :, None, :].astype(t.dtype)
    t1, t2 = t[..., :half], t[..., half:]
    return jnp.concatenate([t1 * cos - t2 * sin, t1 * sin + t2 * cos], axis=-1)

def causal_attention(q, k, v):
    b, s, h, d = q.shape
    nb = s // Q_BLOCK
    scale = 1.0 / math.sqrt(d)
    qb = q.reshape(b, nb, Q_BLOCK, h, d).transpose(1, 0, 2, 3, 4)
    k_pos = jnp.arange(s)

    def one_block(args):
        q_blk, blk = args
        sc = jnp.einsum('bqhd,bkhd->bhqk', q_blk, k,
                        preferred_element_type=jnp.float32) * scale
        q_pos = blk * Q_BLOCK + jnp.arange(Q_BLOCK)
        mask = k_pos[None, :] <= q_pos[:, None]
        sc = jnp.where(mask[None, None], sc, -jnp.inf)
        p = jax.nn.softmax(sc, axis=-1).astype(v.dtype)
        return jnp.einsum('bhqk,bkhd->bqhd', p, v)

    out = lax.map(one_block, (qb, jnp.arange(nb)))
    return out.transpose(1, 0, 2, 3, 4).reshape(b, s, h, v.shape[-1])

def memory_attention(q, mem_k, mem_v):
    sc = jnp.einsum('bshd,bmhd->bhsm', q, mem_k,
                    preferred_element_type=jnp.float32) / math.sqrt(HEAD_DIM)
    p = jax.nn.softmax(sc, axis=-1).astype(mem_v.dtype)
    return jnp.einsum('bhsm,bmhd->bshd', p, mem_v)

def _lin_rec_combine(left, right):
    a1, b1 = left
    a2, b2 = right
    return a1 * a2, a2 * b1 + b2

def rg_lru_branch(u, conv_w, conv_b, w_r, b_r, w_i, b_i, lam):
    b, s, w = u.shape
    u_pad = jnp.pad(u, ((0, 0), (CONV_W - 1, 0), (0, 0)))
    xc = conv_b + u_pad[:, 0:s] * conv_w[0]
    for tap in range(1, CONV_W):
        xc = xc + u_pad[:, tap:tap + s] * conv_w[tap]
    xb = xc.reshape(b, s, N_LRU_BLOCKS, LRU_BLOCK)
    r = jax.nn.sigmoid(jnp.einsum('bsgi,gij->bsgj', xb, w_r).reshape(b, s, w) + b_r)
    i = jax.nn.sigmoid(jnp.einsum('bsgi,gij->bsgj', xb, w_i).reshape(b, s, w) + b_i)
    log_a = (-LRU_C * jax.nn.softplus(-lam.astype(jnp.float32))) * r.astype(jnp.float32)
    a = jnp.exp(log_a)
    gated_x = jnp.sqrt(-jnp.expm1(2.0 * log_a)) * (i * xc).astype(jnp.float32)
    _, hs = lax.associative_scan(_lin_rec_combine, (a, gated_x), axis=1)
    return hs.astype(u.dtype)

def second_inputs(seed: int = 0) -> dict:
    key = jax.random.key(seed)
    ks = jax.random.split(key, 24)
    f32 = jnp.float32
    nrm = lambda k, shape, s: jax.random.normal(k, shape, f32) * s
    x = nrm(ks[0], (BATCH, SEQ, D_MODEL), 1.0)
    mem = nrm(ks[1], (BATCH, MEM_LEN, D_MODEL), 1.0)
    offset = jax.random.randint(ks[2], (BATCH, 1), 0, 4096, dtype=jnp.int32)
    positions = (offset + jnp.arange(SEQ, dtype=jnp.int32)[None, :]).astype(jnp.int32)
    mla_w_in = nrm(ks[3], (N_MLA, D_MODEL, MLA_IN), D_MODEL ** -0.5)
    mla_q_norm = 1.0 + nrm(ks[4], (N_MLA, Q_LORA), 0.01)
    mla_w_uq = nrm(ks[5], (N_MLA, Q_LORA, N_TOK_HEADS * QK_DIM), Q_LORA ** -0.5)
    mla_kv_norm = 1.0 + nrm(ks[6], (N_MLA, KV_LORA), 0.01)
    mla_w_ukv = nrm(ks[7], (N_MLA, KV_LORA, N_TOK_HEADS * (QK_NOPE + V_DIM)), KV_LORA ** -0.5)
    lru_w_in = nrm(ks[8], (N_LRU, D_MODEL, LRU_IN), D_MODEL ** -0.5)
    lru_conv_w = nrm(ks[9], (N_LRU, CONV_W, TOK_WIDTH), CONV_W ** -0.5)
    lru_conv_b = nrm(ks[10], (N_LRU, TOK_WIDTH), 0.01)
    lru_w_rgate = nrm(ks[11], (N_LRU, N_LRU_BLOCKS, LRU_BLOCK, LRU_BLOCK), LRU_BLOCK ** -0.5)
    lru_b_rgate = nrm(ks[12], (N_LRU, TOK_WIDTH), 0.01)
    lru_w_igate = nrm(ks[13], (N_LRU, N_LRU_BLOCKS, LRU_BLOCK, LRU_BLOCK), LRU_BLOCK ** -0.5)
    lru_b_igate = nrm(ks[14], (N_LRU, TOK_WIDTH), 0.01)
    a_c = jax.random.uniform(ks[15], (N_LRU, TOK_WIDTH), f32, 0.9, 0.999)
    a0 = a_c ** (1.0 / LRU_C)
    lru_lambda = jnp.log(a0) - jnp.log1p(-a0)
    w_mem_kv = nrm(ks[16], (DEPTH_2, D_MODEL, 2 * MEM_WIDTH), D_MODEL ** -0.5)
    w_out = nrm(ks[17], (DEPTH_2, MIX_WIDTH, D_MODEL), BETA * MIX_WIDTH ** -0.5)
    ln_g = 1.0 + nrm(ks[18], (DEPTH_2, D_MODEL), 0.01)
    ln_b = nrm(ks[19], (DEPTH_2, D_MODEL), 0.01)
    return {"x": x, "mem": mem, "positions": positions,
            "mla_w_in": mla_w_in, "mla_q_norm": mla_q_norm, "mla_w_uq": mla_w_uq,
            "mla_kv_norm": mla_kv_norm, "mla_w_ukv": mla_w_ukv,
            "lru_w_in": lru_w_in, "lru_conv_w": lru_conv_w, "lru_conv_b": lru_conv_b,
            "lru_w_rgate": lru_w_rgate, "lru_b_rgate": lru_b_rgate,
            "lru_w_igate": lru_w_igate, "lru_b_igate": lru_b_igate, "lru_lambda": lru_lambda,
            "w_mem_kv": w_mem_kv, "w_out": w_out, "ln_g": ln_g, "ln_b": ln_b}

def second_block(x, mem, positions, mla_w_in, mla_q_norm, mla_w_uq, mla_kv_norm, mla_w_ukv,
              lru_w_in, lru_conv_w, lru_conv_b, lru_w_rgate, lru_b_rgate,
              lru_w_igate, lru_b_igate, lru_lambda, w_mem_kv, w_out, ln_g, ln_b):
    b, s, _ = x.shape
    h = x
    for layer in range(DEPTH_2):
        j = layer // 2
        if layer % 2 == 0:
            z = h @ mla_w_in[j]
            c_q, c_kv, k_r, gate, q_mem = _split(
                z, [Q_LORA, KV_LORA, QK_ROPE, MIX_WIDTH, MEM_WIDTH])
            q = (rms_norm(c_q, mla_q_norm[j]) @ mla_w_uq[j]).reshape(b, s, N_TOK_HEADS, QK_DIM)
            q = jnp.concatenate([q[..., :QK_NOPE], apply_rope_2(q[..., QK_NOPE:], positions)], axis=-1)
            kv = (rms_norm(c_kv, mla_kv_norm[j]) @ mla_w_ukv[j]).reshape(
                b, s, N_TOK_HEADS, QK_NOPE + V_DIM)
            k_nope, v = kv[..., :QK_NOPE], kv[..., QK_NOPE:]
            k_rope = apply_rope_2(k_r[:, :, None, :], positions)
            k = jnp.concatenate(
                [k_nope, jnp.broadcast_to(k_rope, (b, s, N_TOK_HEADS, QK_ROPE))], axis=-1)
            tok = causal_attention(q, k, v).reshape(b, s, TOK_WIDTH)
        else:
            z = h @ lru_w_in[j]
            u, gate, q_mem = _split(z, [TOK_WIDTH, MIX_WIDTH, MEM_WIDTH])
            tok = rg_lru_branch(u, lru_conv_w[j], lru_conv_b[j], lru_w_rgate[j], lru_b_rgate[j],
                                lru_w_igate[j], lru_b_igate[j], lru_lambda[j])
        mem_kv = (mem @ w_mem_kv[layer]).reshape(b, MEM_LEN, 2, N_MEM_HEADS, HEAD_DIM)
        mem_out = memory_attention(q_mem.reshape(b, s, N_MEM_HEADS, HEAD_DIM),
                                   mem_kv[:, :, 0], mem_kv[:, :, 1]).reshape(b, s, MEM_WIDTH)
        y = jnp.concatenate([tok, mem_out], axis=-1) * jax.nn.silu(gate)
        h = layer_norm(ALPHA * h + y @ w_out[layer], ln_g[layer], ln_b[layer])
    return h


def setup_inputs(seed=0):
    out = dict(first_inputs(seed))
    for name, value in second_inputs(seed + 1).items():
        if name != "x":
            out[name + "_2"] = value
    return out


def reference(
    x, c, ctx, c_ctx, w_ada, b_ada, norm1_g, w_in, sink, conv_w, decay_w0, decay_w2, iclr_a0,
    iclr_a2, gate_g2, k_k, k_a, r_k, lnx_w, lnx_b, w_branch_attn, w_branch_rwkv, w_out, norm2_g,
    w_mlp_up, w_mlp_down, norm_f_g, mem_2, positions_2, mla_w_in_2, mla_q_norm_2, mla_w_uq_2,
    mla_kv_norm_2, mla_w_ukv_2, lru_w_in_2, lru_conv_w_2, lru_conv_b_2, lru_w_rgate_2,
    lru_b_rgate_2, lru_w_igate_2, lru_b_igate_2, lru_lambda_2, w_mem_kv_2, w_out_2, ln_g_2,
    ln_b_2,
):
    x = first_block(
        x, c, ctx, c_ctx, w_ada, b_ada, norm1_g, w_in, sink, conv_w, decay_w0, decay_w2,
        iclr_a0, iclr_a2, gate_g2, k_k, k_a, r_k, lnx_w, lnx_b, w_branch_attn, w_branch_rwkv,
        w_out, norm2_g, w_mlp_up, w_mlp_down, norm_f_g,
    )
    return second_block(
        x, mem_2, positions_2, mla_w_in_2, mla_q_norm_2, mla_w_uq_2, mla_kv_norm_2, mla_w_ukv_2,
        lru_w_in_2, lru_conv_w_2, lru_conv_b_2, lru_w_rgate_2, lru_b_rgate_2, lru_w_igate_2,
        lru_b_igate_2, lru_lambda_2, w_mem_kv_2, w_out_2, ln_g_2, ln_b_2,
    )


_drawn_inputs = setup_inputs


def setup_inputs(seed=0):
    import zlib

    import numpy as np

    out = dict(_drawn_inputs(seed))
    spreads = {}
    factors = {'ctx': 4.648,
     'norm1_g': 3.715,
     'sink': 8.0,
     'decay_w0': 3.457,
     'decay_w2': 3.744,
     'k_k': 8.0,
     'k_a': 3.039,
     'lnx_w': 8.0,
     'lnx_b': 8.0,
     'mem_2': 3.66,
     'mla_q_norm_2': 8.0,
     'mla_w_uq_2': 3.113,
     'mla_kv_norm_2': 8.0,
     'lru_conv_b_2': 6.287,
     'lru_b_rgate_2': 64.0,
     'lru_b_igate_2': 64.0,
     'w_mem_kv_2': 3.545,
     'ln_g_2': 4.005,
     'ln_b_2': 3.443}
    for name, (base, spread) in spreads.items():
        noise = np.random.default_rng([zlib.crc32(name.encode()), seed]).standard_normal(out[name].shape)
        drawn = base * np.exp(spread * noise) if base else spread * noise
        out[name] = jnp.asarray(drawn.astype(out[name].dtype))
    for name, factor in factors.items():
        out[name] = (out[name] * factor).astype(out[name].dtype)
    return out
```

```python
from contextlib import ExitStack, contextmanager

import numpy as np

import concourse.bass as bass
from concourse import mybir

F32 = mybir.dt.float32
I32 = mybir.dt.int32
ALU = mybir.AluOpType
ACT = mybir.ActivationFunctionType
AX_X = mybir.AxisListType.X

P = 128
D = 1024
KD = D // P
T = 1024
CT = 256
ALL = CT + T
HD = 64
NQ, NKV = 8, 2
AW = NQ * HD
RW = 512
PAIRS = RW // P
DL, IL, GL = 32, 32, 96
GRID_W = 64
DFF = 4096
CH = 128
LEVELS = 6
EPS = 1e-6
LNX_EPS = 1e-5 * HD
QL, KVL, QKN, QKR = 384, 256, 64, 32
QKD = QKN + QKR
TH, MH = 12, 4
TW = TH * HD
MIX = D
ALPHA = (2.0 * 2) ** 0.25
NEG = -1e30

C_Q, C_K, C_V, C_R = 0, AW, AW + 128, AW + 256
C_HW = C_R + 3 * RW
C_HA, C_HG = C_HW + DL, C_HW + DL + IL
C_G = C_HG + GL

SLOT = 8192
SLOTS = 6


def turns(eng, n):
    if n >= 4 and n % 2 == 0:
        with eng.Fori(0, n // 2) as i:
            for j in range(2):
                yield i * 2 + j, j, i
    else:
        for t in range(n):
            yield t, t % 2, t // 2


def rows(ap, t, width=P):
    return ap[bass.ds(t * width, width), :]


def chunks(n, size=512):
    return [(a, min(size, n - a)) for a in range(0, n, size)]



CONST = {}
_at = 0
for _n, _w in [("ident", 128), ("rot", 128), ("ones", 128), ("headsum", 128), ("rot_mla", 96),
               ("causal", 128), ("freq", 1), ("cutmask", 1)]:
    CONST[_n] = (_at, _w)
    _at += _w
CONST_W = _at


def shape_constants():
    c = np.zeros((P, CONST_W), np.float32)

    def put(name, a):
        at, w = CONST[name]
        c[:a.shape[0], at:at + w] = a

    put("ident", np.eye(P))
    rot = np.zeros((P, P))
    for h in range(2):
        for j in range(32):
            rot[64 * h + 32 + j, 64 * h + j] = -1.0
            rot[64 * h + j, 64 * h + 32 + j] = 1.0
    put("rot", rot)
    put("ones", np.ones((P, P)))
    put("headsum", np.kron(np.eye(2), np.ones((HD, HD))))
    rot = np.zeros((QKD, QKD))
    for j in range(16):
        rot[QKN + 16 + j, QKN + j] = -1.0
        rot[QKN + j, QKN + 16 + j] = 1.0
    put("rot_mla", rot)
    i = np.arange(P)
    put("causal", np.where(i[None, :] <= i[:, None], 0.0, NEG))
    half = QKR // 2
    freq = np.power(np.float32(10000.0), -np.arange(half, dtype=np.float32) / half)
    put("freq", np.concatenate([np.zeros(QKN), freq, freq])[:, None])
    n_freq = HD // 4
    inv = np.power(np.float32(10000.0), -np.arange(n_freq, dtype=np.float32) / n_freq).astype(np.float32)
    row = np.repeat(np.arange(T // GRID_W, dtype=np.float32), GRID_W)
    col = np.tile(np.arange(GRID_W, dtype=np.float32), T // GRID_W)
    ang = np.concatenate([row[:, None] * inv, col[:, None] * inv], axis=-1).T
    axial = np.stack([np.tile(np.cos(ang), (4, 1)), np.tile(np.sin(ang), (4, 1))]).astype(np.float32)
    left = np.where(i[None, :] >= i[:, None], 0.0, NEG)
    right = np.where(i[None, :] <= i[:, None], 0.0, NEG)
    none = np.full((P, P), NEG)
    band = np.zeros((T // P, P, 3 * P), np.float32)
    for b in range(T // P):
        band[b, :, :P] = left if b else none
        band[b, :, 2 * P:] = right if b < T // P - 1 else none
    before = (i[:, None] < i[None, :]).astype(np.int32)
    upto = (i[:, None] <= i[None, :]).astype(np.int32)
    keep = np.stack([np.concatenate([before, upto], 1), np.concatenate([before.T, upto.T], 1)])
    corner = np.zeros((2, LEVELS + 1, P, P), np.float32)
    for lv in range(LEVELS + 1):
        b = 2 << lv
        m = (i[:, None] // b == i[None, :] // b) & (i[:, None] % b >= b // 2) & (i[None, :] % b < b // 2)
        corner[0, lv], corner[1, lv] = m, m.T
    corner = np.ascontiguousarray(corner.transpose(2, 0, 1, 3)).reshape(P, -1)
    starts = np.ones((P, ALL), np.float32)
    starts[:, ::CH] = 0.0
    return {"k_mats": c, "k_axial": axial, "k_band": band, "k_keep": keep.astype(np.int32),
            "k_corner": corner, "k_starts": starts}


PARAM_ROWS = {}
_PARAMS = [("b_ada", 48), ("norm1_g", 8), ("norm2_g", 8), ("norm_f_g", 8),
           ("conv0", 14), ("conv1", 14), ("conv2", 14),
           ("decay_w0", 8), ("k_k", 4), ("k_a", 4), ("r_k", 4), ("c_rows", 8), ("cc_rows", 8),
           ("iclr_a0", 8), ("lnx_w", 4), ("lnx_b", 4), ("lru_conv", 24), ("lru_conv_b", 6),
           ("lru_b_r", 6), ("lru_b_i", 6), ("lru_lambda", 6), ("ln_g", 16), ("ln_b", 16),
           ("q_norm", 3), ("kv_norm", 2)]
_at = 0
for _n, _w in _PARAMS:
    if _at // P != (_at + _w - 1) // P:
        _at = -(-_at // P) * P
    PARAM_ROWS[_n] = _at
    _at += _w
PARAM_TILES = -(-_at // P)


class Core:

    def __init__(self, nc, ctx, ins, out):
        self.nc, self.ins, self.out = nc, ins, out
        self.ctx = ctx
        self.arena = ctx.enter_context(nc.sbuf_tensor("arena", [P, SLOTS * SLOT], F32))
        self.mats = ctx.enter_context(nc.sbuf_tensor("mats", [P, CONST_W], F32))
        self.params = ctx.enter_context(nc.sbuf_tensor("params", [P, PARAM_TILES * P], F32))
        self.mod = ctx.enter_context(nc.sbuf_tensor("mod", [P, 48, 2], F32))
        self.gain = ctx.enter_context(nc.sbuf_tensor("gain", [P, 3, KD], F32))
        self.small = ctx.enter_context(nc.sbuf_tensor("small", [P, 64], F32))
        self.psum = ctx.enter_context(nc.psum_tensor("psum", [P, 8, 512], F32))
        self.stages, self.held = 0, None
        self.stored, self.stores = ctx.enter_context(nc.semaphore("stored")), 0

    @contextmanager
    def stage(self):
        self.stages += 1
        with ExitStack() as self.held:
            self.used = []
            yield
            with self.nc.Block() as block:
                @block.sync
                def _(sp):
                    for s in self.used:
                        sp.sem_clear(s)

    def storing(self, n):
        at, self.stores = self.stores, self.stores + 16 * n
        return self.stored, at

    def sem(self, name):
        self.used.append(self.held.enter_context(self.nc.semaphore(f"{name}_{self.stages}")))
        return self.used[-1]

    def pair(self, name):
        return [self.sem(f"{name}{j}") for j in range(2)]

    def mat(self, name, parts=P):
        at, w = CONST[name]
        return self.mats[0:parts, at:at + w]

    def slot(self, first, *shape, at=0, parts=P):
        n = int(np.prod(shape))
        v = self.arena[0:parts, int(first * SLOT) + at:int(first * SLOT) + at + n]
        if len(shape) == 2:
            v = v.rearrange("p (a b) -> p a b", a=shape[0])
        elif len(shape) == 3:
            v = v.rearrange("p (a b c) -> p a b c", a=shape[0], b=shape[1])
        elif len(shape) == 4:
            v = v.rearrange("p (a b c d) -> p a b c d", a=shape[0], b=shape[1], c=shape[2])
        return v

    def par(self, name, j=0, parts=P):
        at = PARAM_ROWS[name] + j
        return self.params[0:parts, at:at + 1]

    def scratch(self, name, *shape):
        return self.nc.dram_tensor(name, list(shape), F32).ap()


def setup(C):
    nc, ins = C.nc, C.ins
    raw = C.slot(0, PARAM_TILES, P)
    loaded, cleared, turned = C.sem("loaded"), C.sem("cleared"), C.sem("turned")
    n_loads = [0]
    with nc.Block() as block:
        @block.gpsimd
        def _(pool):
            nc.gpsimd.memset(raw, 0.0).then_inc(cleared, 1)

        @block.sync
        def _(sp):
            sp.dma_start(C.mats[:, :], ins["k_mats"]).then_inc(loaded, 16)
            sp.dma_start(C.small[:, 0:NQ], ins["sink"].broadcast_to([P, NQ])).then_inc(loaded, 16)
            n_loads[0] = 2
            sp.wait_ge(cleared, 1)

            def put(name, j, ap):
                at = PARAM_ROWS[name] + j
                sp.dma_start(raw[at % P:at % P + ap.shape[0], at // P, 0:ap.shape[1]], ap).then_inc(loaded, 16)
                n_loads[0] += 1

            def vec(name, ap, j=0):
                put(name, j, ap.rearrange("(a b) -> a b", b=P))

            vec("b_ada", ins["b_ada"][0, :])
            for n in ("norm1_g", "norm2_g", "k_k", "k_a", "lnx_w", "lnx_b"):
                vec(n, ins[n][0, :])
            vec("norm_f_g", ins["norm_f_g"])
            for t in range(3):
                w = ins["conv_w"][0, t, :]
                vec(f"conv{t}", w[0:3 * RW])
                put(f"conv{t}", 12, w[3 * RW:3 * RW + DL + IL].rearrange("(a b) -> a b", a=1))
                put(f"conv{t}", 13, w[3 * RW + DL + IL:3 * RW + DL + IL + GL].rearrange("(a b) -> a b", a=1))
            for d in range(2):
                vec("decay_w0", ins["decay_w0"][0, d, :], 4 * d)
                vec("iclr_a0", ins["iclr_a0"][0, d, :], 4 * d)
                vec("ln_g", ins["ln_g_2"][d, :], 8 * d)
                vec("ln_b", ins["ln_b_2"][d, :], 8 * d)
            vec("r_k", ins["r_k"][0, :, :].rearrange("h d -> (h d)"))
            vec("c_rows", ins["c"][0, :])
            vec("cc_rows", ins["c_ctx"])
            for t in range(4):
                vec("lru_conv", ins["lru_conv_w_2"][0, t, :], 6 * t)
            vec("lru_conv_b", ins["lru_conv_b_2"][0, :])
            vec("lru_b_r", ins["lru_b_rgate_2"][0, :])
            vec("lru_b_i", ins["lru_b_igate_2"][0, :])
            vec("lru_lambda", ins["lru_lambda_2"][0, :])
            vec("q_norm", ins["mla_q_norm_2"][0, :])
            vec("kv_norm", ins["mla_kv_norm_2"][0, :])

        @block.tensor
        def _(pe):
            pe.wait_ge(loaded, 16 * n_loads[0])
            for t in range(PARAM_TILES):
                mm = pe.transpose(C.psum[:, 0, t * P:(t + 1) * P], raw[:, t, :], C.mat("ident"))
            mm.then_inc(turned, 1)

        @block.vector
        def _(dve):
            dve.wait_ge(turned, 1)
            nc.vector.tensor_copy(C.params[:, :], C.psum[:, 0, 0:PARAM_TILES * P])


def modulation(C):
    nc, ins = C.nc, C.ins
    WC = 512
    N = 6 * D // WC
    w = C.slot(0, 2, KD, WC)
    s = C.slot(1, 4, 2, KD)
    gate, sil = s[:, 0], C.slot(1, KD, 2, at=256)
    mm_done, s_act, s_dve, copied = (C.sem(n) for n in ("mm_done", "sig", "sil", "copied"))
    w_ready = C.pair("w_ready")
    cols = C.params[:, PARAM_ROWS["c_rows"]:PARAM_ROWS["c_rows"] + 2 * KD].rearrange("p (v k) -> p v k", v=2)
    with nc.Block() as block:
        @block.scalar
        def _(act):
            nc.scalar.activation(gate, cols, ACT.Sigmoid).then_inc(s_act, 1)

        @block.sync
        def _(sp):
            for t, j, r in turns(sp, N):
                sp.wait_ge(mm_done, t + 1)
                sp.dma_start(w[:, j], ins["w_ada"][0, :, bass.ds(t * WC, WC)]
                             .rearrange("(k p) n -> p k n", p=P)).then_inc(w_ready[j], 16)

        @block.tensor
        def _(pe):
            pe.sem_inc(mm_done, 2)
            pe.sem_inc(copied, 2)
            pe.wait_ge(s_dve, 1)
            for t, j, r in turns(pe, N):
                pe.wait_ge(w_ready[j], (r + 1) * 16)
                pe.wait_ge(copied, t + 1)
                for m in range(WC // P):
                    for k in range(KD):
                        mm = pe.matmul(C.psum[:, j, 2 * m:2 * m + 2], w[:, j, k, m * P:(m + 1) * P], sil[:, k, :],
                                       start=(k == 0), stop=(k == KD - 1))
                mm.then_inc(mm_done, 1)

        @block.vector
        def _(dve):
            dve.wait_ge(s_act, 1)
            nc.vector.tensor_tensor(sil.rearrange("p k v -> p v k"), gate, cols, ALU.mult).then_inc(s_dve, 1)
            for t, j, r in turns(dve, N):
                dve.wait_ge(mm_done, t + 3)
                nc.vector.tensor_copy(C.mod[:, bass.ds(t * 4, 4), :],
                                      C.psum[:, j, 0:8].rearrange("p (m v) -> p m v", v=2)).then_inc(copied, 1)
            dve.wait_ge(copied, N + 2)
            b = C.params[:, PARAM_ROWS["b_ada"]:PARAM_ROWS["b_ada"] + 48]
            for v in range(2):
                nc.vector.tensor_tensor(C.mod[:, :, v], C.mod[:, :, v], b, ALU.add).then_inc(s_dve, 1)
            dve.wait_ge(s_dve, 3)
            for n, (part, v, g) in enumerate([(1, 0, "norm1_g"), (1, 1, "norm1_g"), (4, 0, "norm2_g")]):
                nc.vector.scalar_tensor_tensor(
                    C.gain[:, n, :], C.mod[:, part * KD:(part + 1) * KD, v], 1.0,
                    C.params[:, PARAM_ROWS[g]:PARAM_ROWS[g] + KD], ALU.add, ALU.mult)


def turn_in(C, src, dst, n_tok, width, at, stage_slot):
    nc = C.nc
    NT, KT = n_tok // P, width // P
    QUADS = [(a, min(4, KT - a)) for a in range(0, KT, 4)]
    raw = C.slot(stage_slot, 2, width)
    x_ready, turned, copied = C.pair("x_ready"), C.sem("turned"), C.sem("copied")
    nq = len(QUADS)
    with nc.Block() as block:
        @block.sync
        def _(sp):
            for t, j, r in turns(sp, NT):
                sp.wait_ge(turned, t * nq + nq)
                sp.dma_start(raw[:, j], rows(src, t)).then_inc(x_ready[j], 16)

        @block.tensor
        def _(pe):
            pe.sem_inc(turned, 2 * nq)
            for t, j, r in turns(pe, NT):
                pe.wait_ge(x_ready[j], (r + 1) * 16)
                pe.wait_ge(copied, t * nq + nq)
                for q, (a, n) in enumerate(QUADS):
                    for k in range(n):
                        mm = pe.transpose(C.psum[:, 2 * j + q, k * P:(k + 1) * P],
                                          raw[:, j, (a + k) * P:(a + k + 1) * P], C.mat("ident"))
                    mm.then_inc(turned, 1)

        @block.scalar
        def _(act):
            act.sem_inc(copied, 2 * nq)
            for t, j, r in turns(act, NT):
                for q, (a, n) in enumerate(QUADS):
                    act.wait_ge(turned, t * nq + q + 1 + 2 * nq)
                    nc.scalar.activation(dst[:, a:a + n, bass.ds(t * P + at, P)],
                                         C.psum[:, 2 * j + q, 0:n * P].rearrange("p (k t) -> p k t", t=P),
                                         ACT.Copy).then_inc(copied, 1)


def turn_out(C, src, dst, n_tok, stage_slot):
    nc = C.nc
    NT = n_tok // P
    nat = C.slot(stage_slot, 2, D)
    blk = C.slot(stage_slot, 2, KD, P, at=2 * D)
    staged, turned, copied = (C.sem(n) for n in ("staged", "turned", "copied"))
    stored = C.pair("stored")
    with nc.Block() as block:
        @block.vector
        def _(dve):
            for t, j, r in turns(dve, NT):
                dve.wait_ge(turned, t * 2 + 2)
                nc.vector.tensor_copy(blk[:, j], src[:, :, bass.ds(t * P, P)]).then_inc(staged, 1)

        @block.tensor
        def _(pe):
            pe.sem_inc(turned, 4)
            for t, j, r in turns(pe, NT):
                pe.wait_ge(staged, t + 1)
                pe.wait_ge(copied, t * 2 + 2)
                for q in range(2):
                    for k in range(4):
                        mm = pe.transpose(C.psum[:, 2 * j + q, k * P:(k + 1) * P], blk[:, j, 4 * q + k, :],
                                          C.mat("ident"))
                    mm.then_inc(turned, 1)

        @block.scalar
        def _(act):
            act.sem_inc(copied, 4)
            act.sem_inc(stored[0], 16)
            act.sem_inc(stored[1], 16)
            for t, j, r in turns(act, NT):
                act.wait_ge(stored[j], r * 16 + 16)
                for q in range(2):
                    act.wait_ge(turned, t * 2 + q + 5)
                    nc.scalar.activation(nat[:, j, q * 512:(q + 1) * 512], C.psum[:, 2 * j + q, :],
                                         ACT.Copy).then_inc(copied, 1)

        @block.sync
        def _(sp):
            for t, j, r in turns(sp, NT):
                sp.wait_ge(copied, t * 2 + 6)
                sp.dma_start(rows(dst, t), nat[:, j]).then_inc(stored[j], 16)
            for j in range(2):
                sp.wait_ge(stored[j], NT // 2 * 16 + 16)


def norm(C, src, dst, n_tok, kt, tmp_slot, gain=None, shift=None, center=False, segs=None):
    nc = C.nc
    segs = segs or [(a, n, gain, shift) for a, n in chunks(n_tok)]
    sq = C.slot(tmp_slot, 2, 512)
    rstd = C.slot(tmp_slot, 2, 512, at=1024)
    sq_ready, sq_used, summed, mean_ready, rs, scaled, shifted = (
        C.sem(n) for n in ("sq_ready", "sq_used", "summed", "mean_ready", "rs", "scaled", "shifted"))
    NS = len(segs)
    inv = 1.0 / (kt * P)
    per = kt + 3 + (kt if center else 0)
    x = dst if center else src
    with nc.Block() as block:
        @block.scalar
        def _(act):
            n = 0
            for s, (a, w, g, sh) in enumerate(segs):
                for k in range(kt):
                    if center:
                        act.wait_ge(scaled, per * s + k + 1)
                    if n >= 2:
                        act.wait_ge(sq_used, n - 1)
                    nc.scalar.activation(sq[:, n % 2, 0:w], x[:, k, a:a + w], ACT.Square).then_inc(sq_ready, 1)
                    n += 1
                act.wait_ge(scaled, per * s + (kt if center else 0) + 2)
                nc.scalar.activation(rstd[:, s % 2, 0:w], rstd[:, s % 2, 0:w], ACT.Sqrt).then_inc(rs, 1)
                if sh is not None:
                    for k in range(kt):
                        act.wait_ge(scaled, per * s + (kt if center else 0) + 3 + k + 1)
                        nc.scalar.activation(dst[:, k, a:a + w], dst[:, k, a:a + w], ACT.Identity, bias=sh(k))

        @block.tensor
        def _(pe):
            n = 0
            for s, (a, w, g, sh) in enumerate(segs):
                if center:
                    for k in range(kt):
                        mm = pe.matmul(C.psum[:, 2 + s % 2, 0:w], C.mat("ones"), src[:, k, a:a + w],
                                       start=(k == 0), stop=(k == kt - 1))
                    mm.then_inc(mean_ready, 1)
                for k in range(kt):
                    pe.wait_ge(sq_ready, n + 1)
                    if k == 0 and s >= 2:
                        pe.wait_ge(rs, s - 1)
                    mm = pe.matmul(C.psum[:, s % 2, 0:w], C.mat("ones"), sq[:, n % 2, 0:w],
                                   start=(k == 0), stop=(k == kt - 1)).then_inc(sq_used, 1)
                    n += 1

        @block.vector
        def _(dve):
            for s, (a, w, g, sh) in enumerate(segs):
                at = per * s
                if center:
                    dve.wait_ge(mean_ready, s + 1)
                    nc.vector.tensor_scalar(rstd[:, s % 2, 0:w], C.psum[:, 2 + s % 2, 0:w], inv, None,
                                            ALU.mult).then_inc(shifted, 1)
                    dve.wait_ge(shifted, s + 1)
                    for k in range(kt):
                        nc.vector.tensor_tensor(dst[:, k, a:a + w], src[:, k, a:a + w], rstd[:, s % 2, 0:w],
                                                ALU.subtract).then_inc(scaled, 1)
                    at += kt
                dve.wait_ge(sq_used, kt * (s + 1))
                dve.wait_ge(scaled, at) if at else None
                nc.vector.tensor_scalar(rstd[:, s % 2, 0:w], C.psum[:, s % 2, 0:w], inv, EPS, ALU.mult,
                                        ALU.add).then_inc(scaled, 1)
                dve.wait_ge(scaled, at + 1)
                nc.vector.reciprocal(rstd[:, s % 2, 0:w], rstd[:, s % 2, 0:w]).then_inc(scaled, 1)
                dve.wait_ge(rs, s + 1)
                dve.sem_inc(scaled, 1)
                for k in range(kt):
                    nc.vector.scalar_tensor_tensor(dst[:, k, a:a + w], x[:, k, a:a + w], g(k),
                                                   rstd[:, s % 2, 0:w], ALU.mult, ALU.mult).then_inc(scaled, 1)


def linear(C, rhs, w, n_m, kt, n_tok, w_slot, e_slot=None, width=P, tok0=0, kind="copy", func=None,
           dram=None, res=None, mul=None, col=None, add=None, add_scale=1.0, add_res=None, w_half=None, w_cols=None):
    nc = C.nc
    pieces = chunks(n_tok)
    NN = len(pieces)
    wb = C.slot(w_slot, 2, kt, width)
    at = 2 * kt * width
    stage = C.slot(w_slot, 2, n_tok, at=at)
    at += 2 * n_tok if dram is not None or kind == "sqrelu" else 0
    if e_slot is None:
        e_slot, e_at = w_slot, at
    else:
        e_at = 0
    ext = C.slot(e_slot, 2, 2, n_tok, at=e_at)
    done, evac, sq, stage_free = (C.sem(n) for n in ("done", "evac", "tmp", "stage_free"))
    stored, before = C.storing(n_m if dram is not None else 0)
    w_ready, e_ready = C.pair("w_ready"), C.pair("e_ready")
    extras = [x for x in (mul, add) if x is not None]
    NE = len(extras)
    src_w = w_cols or (lambda t: w[:, bass.ds(t * width, width)])

    def target(t, j, a, n):
        return stage[0:width, j, a:a + n] if dram is not None else \
            res[0:width, bass.ds(t, 1), a:a + n].rearrange("p o t -> p (o t)")

    with nc.Block() as block:
        @block.sync
        def _(sp):
            for t, j, r in turns(sp, n_m):
                sp.wait_ge(done, t * NN + NN)
                sp.dma_start(wb[:, j], src_w(t).rearrange("(k p) n -> p k n", p=P)).then_inc(w_ready[j], 16)
                if NE:
                    sp.wait_ge(evac, t * NN + NN)
                for x in range(NE):
                    sp.dma_start(ext[0:width, j, x], rows(extras[x], t, width)).then_inc(e_ready[j], 16)

        @block.tensor
        def _(pe):
            pe.sem_inc(done, 2 * NN)
            for t, j, r in turns(pe, n_m):
                pe.wait_ge(w_ready[j], (r + 1) * 16)
                for c, (a, n) in enumerate(pieces):
                    pe.wait_ge(evac, t * NN + c + 1)
                    for k in range(kt):
                        mm = pe.matmul(C.psum[0:width, j * NN + c, 0:n], wb[:, j, k, :],
                                       rhs[:, k, tok0 + a:tok0 + a + n], start=(k == 0), stop=(k == kt - 1))
                    mm.then_inc(done, 1)

        if kind in ("copy", "sqrelu"):
            @block.scalar
            def _(act):
                act.sem_inc(evac, 2 * NN)
                if dram is not None:
                    act.sem_inc(stage_free, 2)
                for t, j, r in turns(act, n_m):
                    if dram is not None:
                        act.wait_ge(stage_free, t + 1)
                    for c, (a, n) in enumerate(pieces):
                        act.wait_ge(done, t * NN + c + 1 + 2 * NN)
                        if kind == "copy":
                            nc.scalar.activation(target(t, j, a, n), C.psum[0:width, j * NN + c, 0:n],
                                                 func or ACT.Copy).then_inc(evac, 1)
                        else:
                            nc.scalar.activation(stage[:, j, a:a + n], C.psum[0:width, j * NN + c, 0:n],
                                                 ACT.Relu).then_inc(evac, 1)
                            act.wait_ge(evac, t * NN + c + 1 + 2 * NN)
                            nc.scalar.activation(target(t, j, a, n), stage[:, j, a:a + n],
                                                 ACT.Square).then_inc(sq, 1)
        else:
            @block.vector
            def _(dve):
                dve.sem_inc(evac, 2 * NN)
                dve.sem_inc(sq, 1)
                if dram is not None:
                    dve.sem_inc(stage_free, 2)
                for t, j, r in turns(dve, n_m):
                    if dram is not None:
                        dve.wait_ge(stage_free, t + 1)
                    if NE:
                        dve.wait_ge(e_ready[j], (r + 1) * 16 * NE)
                    for c, (a, n) in enumerate(pieces):
                        dve.wait_ge(done, t * NN + c + 1 + 2 * NN)
                        ps, to = C.psum[0:width, j * NN + c, 0:n], target(t, j, a, n)
                        if add is not None:
                            other = ext[0:width, j, NE - 1, a:a + n]
                        elif add_res is not None:
                            other = add_res[0:width, bass.ds(t, 1), tok0 + a:tok0 + a + n].rearrange("p o t -> p (o t)")
                        if col is not None:
                            nc.vector.scalar_tensor_tensor(to, ps, C.mod[:, bass.ds(t + col, 1), 0], other,
                                                           ALU.mult, ALU.add).then_inc(evac, 1)
                        elif mul is None:
                            nc.vector.scalar_tensor_tensor(to, other, add_scale, ps, ALU.mult,
                                                           ALU.add).then_inc(evac, 1)
                        elif add is None and add_res is None:
                            nc.vector.tensor_tensor(to, ps, ext[0:width, j, 0, a:a + n], ALU.mult).then_inc(evac, 1)
                        else:
                            m = ext[0:width, j, 0, a:a + n]
                            nc.vector.tensor_tensor(m, ps, m, ALU.mult).then_inc(sq, 1)
                            dve.wait_ge(sq, t * NN + c + 2)
                            nc.vector.tensor_tensor(to, m, other, ALU.add).then_inc(evac, 1)

        if dram is not None:
            @block.gpsimd
            def _(pool):
                for t, j, r in turns(pool, n_m):
                    if kind == "sqrelu":
                        pool.wait_ge(sq, (t + 1) * NN)
                    else:
                        pool.wait_ge(evac, (t + 1) * NN + 2 * NN)
                    pool.dma_start(rows(dram, t, width), stage[0:width, j, :]).then_inc(stored, 16)
                    pool.wait_ge(stored, t * 16 + 16 + before)
                    pool.sem_inc(stage_free, 1)


def linear_tok(C, src, w, n_cols, kt, tok_tiles, w_slot, dram, w_view=None, row=lambda t: t):
    nc = C.nc
    pieces = chunks(n_cols)
    NN = len(pieces)
    wb = C.slot(w_slot, kt, n_cols)
    stage = C.slot(w_slot, 2, n_cols, at=kt * n_cols)
    w_ready, done, evac = (C.sem(n) for n in ("w_ready", "done", "evac"))
    stored = C.pair("stored")
    n_w = kt if w_view is not None else 1
    with nc.Block() as block:
        @block.sync
        def _(sp):
            if w_view is None:
                sp.dma_start(wb, w.rearrange("(k p) n -> p k n", p=P)).then_inc(w_ready, 16)
            else:
                for k in range(kt):
                    sp.dma_start(w_view(wb[:, k, :]), w(k)).then_inc(w_ready, 16)
            for t in range(tok_tiles):
                sp.wait_ge(evac, NN * (t + 1))
                sp.dma_start(rows(dram, row(t)), stage[:, t % 2, :]).then_inc(stored[t % 2], 16)
            for j in range(2):
                sp.wait_ge(stored[j], 8 * tok_tiles)

        @block.tensor
        def _(pe):
            pe.wait_ge(w_ready, 16 * n_w)
            for t in range(tok_tiles):
                for c, (a, n) in enumerate(pieces):
                    if t >= 2:
                        pe.wait_ge(evac, NN * (t - 2) + c + 1)
                    for k in range(kt):
                        mm = pe.matmul(C.psum[:, (t % 2) * NN + c, 0:n], src[:, k, t * P:(t + 1) * P],
                                       wb[:, k, a:a + n], start=(k == 0), stop=(k == kt - 1))
                    mm.then_inc(done, 1)

        @block.scalar
        def _(act):
            for t in range(tok_tiles):
                if t >= 2:
                    act.wait_ge(stored[t % 2], 16 * (t // 2))
                for c, (a, n) in enumerate(pieces):
                    act.wait_ge(done, NN * t + c + 1)
                    nc.scalar.activation(stage[:, t % 2, a:a + n], C.psum[:, (t % 2) * NN + c, 0:n],
                                         ACT.Copy).then_inc(evac, 1)


def rotate(C, src, dst, n, width, n_tok, mat, cos, sin, slot, dst_rows=None):
    nc = C.nc
    pieces = chunks(n_tok)
    NN = len(pieces)
    x = C.slot(slot, 2, n_tok, parts=width)
    y = C.slot(slot, 2, n_tok, at=2 * n_tok, parts=width)
    z = C.slot(slot, 2, n_tok, at=4 * n_tok, parts=width)
    done, seq, out_free = (C.sem(n) for n in ("done", "seq", "out_free"))
    stored, before = C.storing(n)
    x_ready = C.pair("x_ready")
    out = dst_rows or (lambda t: rows(dst, t, width))
    with nc.Block() as block:
        @block.sync
        def _(sp):
            for t, j, r in turns(sp, n):
                sp.wait_ge(seq, t * 3 * NN + 3 * NN)
                sp.dma_start(x[:, j], rows(src, t, width)).then_inc(x_ready[j], 16)

        @block.gpsimd
        def _(pool):
            for t, j, r in turns(pool, n):
                pool.wait_ge(seq, t * 3 * NN + 9 * NN)
                pool.dma_start(out(t), z[:, j]).then_inc(stored, 16)
                pool.wait_ge(stored, t * 16 + 16 + before)
                pool.sem_inc(out_free, 1)

        @block.tensor
        def _(pe):
            for t, j, r in turns(pe, n):
                pe.wait_ge(x_ready[j], (r + 1) * 16)
                pe.wait_ge(seq, t * 3 * NN + 3 * NN)
                for c, (a, m) in enumerate(pieces):
                    pe.matmul(C.psum[0:width, j * NN + c, 0:m], mat, x[:, j, a:a + m], start=True,
                              stop=True).then_inc(done, 1)

        @block.vector
        def _(dve):
            dve.sem_inc(seq, 6 * NN)
            dve.sem_inc(out_free, 2)
            for t, j, r in turns(dve, n):
                dve.wait_ge(out_free, t + 1)
                for c, (a, m) in enumerate(pieces):
                    base = t * 3 * NN + 3 * c + 6 * NN
                    dve.wait_ge(x_ready[j], (r + 1) * 16)
                    nc.vector.tensor_tensor(y[:, j, a:a + m], x[:, j, a:a + m], cos[:, a:a + m],
                                            ALU.mult).then_inc(seq, 1)
                    dve.wait_ge(done, t * NN + c + 1)
                    nc.vector.tensor_tensor(z[:, j, a:a + m], C.psum[0:width, j * NN + c, 0:m], sin[:, a:a + m],
                                            ALU.mult).then_inc(seq, 1)
                    dve.wait_ge(seq, base + 2)
                    nc.vector.tensor_tensor(z[:, j, a:a + m], z[:, j, a:a + m], y[:, j, a:a + m],
                                            ALU.add).then_inc(seq, 1)


def attention(C, n_turns, units, load, n_loads, store, scale, setup_loads=None, n_setup=0, sink=False,
              masked=False):
    nc = C.nc
    U = len(units(0))
    groups = [[(a, min(4, len(u["v"]) - a)) for a in range(0, len(u["v"]), 4)] for u in units(0)]
    first = [sum(len(x) for x in groups[:u]) for u in range(U)]
    GT = sum(len(x) for x in groups)
    assert U % 2 == 0 and GT % 2 == 0 and n_turns % 2 == 0
    prob = C.slot(5, 2, 1024)
    probT = C.slot(5, 2, 1024, at=2048)
    st = C.slot(5, 5, 2, 8, at=4096)
    names = ("fixed", "scores", "hidden", "maxed", "negmax", "exped", "probs", "turned", "tcopied", "pv", "den",
             "rden", "evac", "out_free")
    (fixed, scores, hidden, maxed, negmax, exped, probs, turned, tcopied, pv, den, rden, evac,
     out_free) = (C.sem(n) for n in names)
    loaded = C.pair("loaded")
    stored, before = C.storing(n_turns)

    def ps(u, n):
        return C.psum[:, 2 * (u % 2):2 * (u % 2) + 2, :].rearrange("p a b -> p (a b)")[:, 0:n]

    def unit_steps(eng):
        def ahead(t, j, r, u, last):
            def at(k):
                if u + k < 0:
                    return None
                if u + k < U:
                    return t, j, r, u + k
                return None if last else (t + 1, 1 - j, r + j, u + k - U)
            return at

        for u in (-2, -1):
            yield ahead(0, 0, 0, u, False)
        with eng.Fori(0, n_turns // 2 - 1) as i:
            for j in range(2):
                for u in range(U):
                    yield ahead(i * 2 + j, j, i, u, False)
        for j in range(2):
            for u in range(U):
                yield ahead(n_turns - 2 + j, j, n_turns // 2 - 1, u, j == 1)

    with nc.Block() as block:
        @block.sync
        def _(sp):
            if setup_loads:
                setup_loads(sp, fixed)
            for t, j, r in turns(sp, n_turns):
                sp.wait_ge(pv, t * U + U)
                load(sp, t, j, loaded[j])

        @block.gpsimd
        def _(pool):
            for t, j, r in turns(pool, n_turns):
                pool.wait_ge(evac, t * U + U + 2)
                store(pool, t, j).then_inc(stored, 16)
                pool.wait_ge(stored, t * 16 + 16 + before)
                pool.sem_inc(out_free, 1)

        @block.tensor
        def _(pe):
            pe.sem_inc(pv, 2 * U)
            if n_setup:
                pe.wait_ge(fixed, 16 * n_setup)

            def turn(t, j, r, u):
                pe.wait_ge(probs, t * U + u + 1)
                for g, (a, n) in enumerate(groups[u]):
                    G = first[u] + g
                    pe.wait_ge(tcopied, t * GT + G + 1)
                    for x in range(n):
                        mm = pe.transpose(C.psum[:, 4 + G % 2, x * P:(x + 1) * P],
                                          prob[:, u % 2, (a + x) * P:(a + x + 1) * P], C.mat("ident"))
                    mm.then_inc(turned, 1)

            def score(t, j, r, u):
                if u == 0:
                    pe.wait_ge(loaded[j], r * 16 * n_loads + 16 * n_loads)
                pe.wait_ge(exped, t * U + u + 1)
                unit = units(j)[u]
                for k, at in unit["k"]:
                    mm = pe.matmul(ps(u, 1024)[:, at:at + k.shape[-1]], unit["q"], k, start=True, stop=True)
                mm.then_inc(scores, 1)

            def values(t, j, r, u):
                unit = units(j)[u]
                n, r0 = len(unit["v"]), unit["at"]
                pe.wait_ge(tcopied, t * GT + first[u] + len(groups[u]) + 2)
                pe.wait_ge(evac, t * U + u + 1)
                for x, v in enumerate(unit["v"]):
                    mm = pe.matmul(C.psum[r0:r0 + HD, 6 + u % 2, 0:P], v, probT[:, u % 2, x * P:(x + 1) * P],
                                   start=(x == 0), stop=(x == n - 1))
                mm.then_inc(pv, 1)

            for at in unit_steps(pe):
                if at(0):
                    turn(*at(0))
                if at(2):
                    score(*at(2))
                if at(0):
                    values(*at(0))

        @block.vector
        def _(dve):
            dve.sem_inc(evac, 2)
            dve.sem_inc(out_free, 2)

            def largest(t, j, r, u):
                g, unit = t * U + u, units(j)[u]
                n = unit["n"]
                dve.wait_ge(scores, g + 1)
                if masked:
                    m, at, w = unit["mask"]
                    nc.vector.tensor_tensor(ps(u, 1024)[:, at:at + w], ps(u, 1024)[:, at:at + w], m,
                                            ALU.add).then_inc(hidden, 1)
                    dve.wait_ge(hidden, g + 1)
                nc.vector.reduce_max(st[:, 0, j, u:u + 1], ps(u, n), AX_X).then_inc(maxed, 1)
                dve.wait_ge(maxed, g + 1)
                if sink:
                    h = unit["sink"]
                    nc.vector.tensor_scalar(st[:, 1, j, u:u + 1], st[:, 0, j, u:u + 1], -scale,
                                            C.small[:, 8 + h:9 + h], ALU.mult, ALU.min).then_inc(negmax, 1)
                else:
                    nc.vector.tensor_scalar(st[:, 1, j, u:u + 1], st[:, 0, j, u:u + 1], -scale, None,
                                            ALU.mult).then_inc(negmax, 1)

            def divide(t, j, r, u):
                g, unit = t * U + u, units(j)[u]
                dve.wait_ge(exped, g + 3)
                total = st[:, 2, j, u:u + 1]
                if sink:
                    nc.vector.tensor_tensor(st[:, 3, j, u:u + 1], total, st[:, 3, j, u:u + 1],
                                            ALU.add).then_inc(den, 1)
                    dve.wait_ge(den, g + 1)
                    total = st[:, 3, j, u:u + 1]
                nc.vector.reciprocal(st[:, 4, j, u:u + 1], total).then_inc(rden, 1)
                dve.wait_ge(rden, g + 1)
                p = prob[:, u % 2, 0:unit["n"]]
                nc.vector.tensor_scalar(p, p, st[:, 4, j, u:u + 1], None, ALU.mult).then_inc(probs, 1)

            def leave(t, j, r, u):
                if u == 0:
                    dve.wait_ge(out_free, t + 1)
                unit = units(j)[u]
                dve.wait_ge(pv, t * U + u + 1 + 2 * U)
                r0 = unit["at"]
                nc.vector.tensor_copy(unit["out"], C.psum[r0:r0 + HD, 6 + u % 2, 0:P]).then_inc(evac, 1)

            for at in unit_steps(dve):
                if at(1):
                    divide(*at(1))
                if at(2):
                    largest(*at(2))
                if at(0):
                    leave(*at(0))

        @block.scalar
        def _(act):
            act.sem_inc(exped, 2)
            act.sem_inc(tcopied, 2)

            def expo(t, j, r, u):
                act.wait_ge(negmax, t * U + u + 1)
                nm, unit = st[:, 1, j, u:u + 1], units(j)[u]
                if sink:
                    h = unit["sink"]
                    nc.scalar.activation(st[:, 3, j, u:u + 1], C.small[:, h:h + 1], ACT.Exp, bias=nm)
                n = unit["n"]
                nc.scalar.activation(prob[:, u % 2, 0:n], ps(u, n), ACT.Exp, bias=nm, scale=scale,
                                     accum_out=st[:, 2, j, u:u + 1]).then_inc(exped, 1)

            def copy(t, j, r, u):
                for g, (a, n) in enumerate(groups[u]):
                    G = first[u] + g
                    act.wait_ge(turned, t * GT + G + 1)
                    nc.scalar.activation(probT[:, u % 2, a * P:(a + n) * P], C.psum[:, 4 + G % 2, 0:n * P],
                                         ACT.Copy).then_inc(tcopied, 1)

            for at in unit_steps(act):
                if at(0):
                    copy(*at(0))
                if at(1):
                    expo(*at(1))


KP = CT + P + T + P


def window_attention(C, qr, kr, vt, ya):
    nc = C.nc
    q = C.slot(3, 2, 4, P)
    kl = C.slot(3, 2, NKV, 3 * P, at=1024)
    kc = C.slot(3, NKV, CT, at=1024 + 1536)
    vl = C.slot(3, 2, 3, P, at=1024 + 1536 + 512)
    vc = C.slot(3, 2, P, at=1024 + 1536 + 512 + 768)
    mask = C.slot(3, 2, 3 * P, at=4096)
    out = C.slot(3, 2, 4, P, at=4096 + 768)

    def setup_loads(sp, loaded):
        for g in range(NKV):
            for e in range(2):
                sp.dma_start(kc[64 * e:64 * e + 64, g, :], kr[64 * g:64 * g + 64, 0:CT]).then_inc(loaded, 16)
        sp.dma_start(vc, vt[0:CT, :].rearrange("(a p) n -> p a n", p=P)).then_inc(loaded, 16)

    def load(sp, t, j, loaded):
        sp.dma_start(q[:, j], qr[:, bass.ds(t * P, P)].rearrange("(a p) n -> p a n", p=P)).then_inc(loaded, 16)
        for g in range(NKV):
            for e in range(2):
                sp.dma_start(kl[64 * e:64 * e + 64, j, g, :],
                             kr[64 * g:64 * g + 64, bass.ds(t * P + CT, 3 * P)]).then_inc(loaded, 16)
        sp.dma_start(vl[:, j], vt[bass.ds(t * P + CT, 3 * P), :].rearrange("(a p) n -> p a n", p=P))\
            .then_inc(loaded, 16)
        sp.dma_start(mask[:, j, :], C.ins["k_band"][bass.ds(t, 1), :, :].rearrange("o p n -> (o p) n"))\
            .then_inc(loaded, 16)

    def units(j):
        us = []
        for h in range(NQ):
            g, e = h // (NQ // NKV), h % 2
            r = slice(64 * e, 64 * e + 64)
            us.append(dict(q=q[r, j, h // 2, :], n=5 * P, sink=h, mask=(mask[:, j, :], 0, 3 * P),
                           k=[(kl[r, j, g, :], 0), (kc[r, g, 0:P], 3 * P), (kc[r, g, P:CT], 4 * P)],
                           v=[vl[:, j, x, HD * g:HD * g + HD] for x in range(3)]
                           + [vc[:, x, HD * g:HD * g + HD] for x in range(2)],
                           out=out[r, j, h // 2, :], at=64 * e))
        return us

    attention(C, T // P, units, load, 7,
              lambda e, t, j: e.dma_start(ya[:, bass.ds(t * P, P)].rearrange("(a p) n -> p a n", p=P), out[:, j]),
              float(HD) ** -0.5, setup_loads, 5, sink=True, masked=True)


def latent_attention(C, qr, kn, krope, vt, tok):
    q = C.slot(3, 2, T, parts=QKD)
    k = C.slot(3, 2, T, at=2 * T, parts=QKD)
    v = C.slot(3, 2, T // P, HD, at=4 * T)
    out = C.slot(3, 2, T, at=5 * T, parts=HD)

    def load(sp, t, j, loaded):
        sp.dma_start(q[:, j, :], rows(qr, t, QKD)).then_inc(loaded, 16)
        sp.dma_start(k[0:QKN, j, :], rows(kn, t, QKN)).then_inc(loaded, 16)
        sp.dma_start(k[QKN:QKD, j, :], krope).then_inc(loaded, 16)
        sp.dma_start(v[:, j], vt[:, bass.ds(t * HD, HD)].rearrange("(a p) n -> p a n", p=P)).then_inc(loaded, 16)

    def units(j):
        us = []
        for b in range(T // P):
            n = (b + 1) * P
            us.append(dict(q=q[:, j, b * P:(b + 1) * P], n=n, mask=(C.mat("causal"), b * P, P),
                           k=[(k[:, j, a:a + w], a) for a, w in chunks(n)],
                           v=[v[:, j, x, :] for x in range(b + 1)], out=out[:, j, b * P:(b + 1) * P], at=0))
        return us

    attention(C, TH, units, load, 4,
              lambda e, t, j: e.dma_start(rows(tok, t, HD), out[:, j]),
              float(QKD) ** -0.5, masked=True)


def memory_attention(C, qm, km, vm, mem_out):
    q = C.slot(3, 2, 2, P)
    k = C.slot(3, 2, 256, at=512)
    v = C.slot(3, 2, 256, at=1024)
    out = C.slot(3, 2, 2, P, at=1536)

    def setup_loads(sp, loaded):
        sp.dma_start(k, km.rearrange("(a p) n -> p a n", p=P)).then_inc(loaded, 16)
        sp.dma_start(v, vm.rearrange("(a p) n -> p a n", p=P)).then_inc(loaded, 16)

    def load(sp, t, j, loaded):
        sp.dma_start(q[:, j], qm[:, bass.ds(t * P, P)].rearrange("(a p) n -> p a n", p=P)).then_inc(loaded, 16)

    def units(j):
        return [dict(q=q[64 * (h % 2):64 * (h % 2) + 64, j, h // 2, :], n=256,
                     k=[(k[64 * (h % 2):64 * (h % 2) + 64, h // 2, :], 0)],
                     v=[v[:, x, HD * h:HD * h + HD] for x in range(2)],
                     out=out[64 * (h % 2):64 * (h % 2) + 64, j, h // 2, :], at=64 * (h % 2))
                for h in range(MH)]

    attention(C, T // P, units, load, 1, lambda e, t, j: e.dma_start(
        mem_out[:, bass.ds(t * P, P)].rearrange("(a p) n -> p a n", p=P), out[:, j]),
              float(HD) ** -0.5, setup_loads, 2)


KAPPA = float(np.exp(-0.5))
NCH = ALL // CH
CC = CT // CH
SEGS = [(0, CT), (CT, T)]


def rwkv_prepare(C, rw, chunked, v_chunked, bonus, gate_in):
    nc, ins = C.nc, C.ins
    W, W4 = ALL, ALL + 4
    places = iter(range(0, 5 * SLOT, W4))

    def tile(parts=P):
        return C.slot(1, 1, W, at=next(places), parts=parts)[:, 0, :]

    raw = [C.slot(1, 1, W4, at=next(places))[:, 0, :] for _ in range(3)]
    cv = [tile() for _ in range(3)]
    kraw, rn, kk, sg, cum, w, y, e1, e2, e3, a, b = (tile() for _ in range(12))
    kd = [tile(), tile()]
    outs = [[tile() for _ in range(4)] for _ in range(2)]
    tail, starts = tile(64), tile()
    used = next(places)
    w2 = C.slot(1, 2, RW, at=used, parts=64)
    gate = e1
    r_, k_, v_ = cv
    sqk = sg
    (padded, dstep, astep, pstep, wload, gate_out) = (
        C.sem(n) for n in ("padded", "dstep", "astep", "pstep", "wload", "gate_out"))
    loaded = [C.sem(f"loaded{x}") for x in range(3)]

    TAIL = [f"t{x}{s}{k}" for x in range(2) for s in range(2) for k in range(3)] + ["omka"]
    DV = [f"c{x}{s}{k}" for x in range(3) for s in range(2) for k in range(3)] + \
         ["kraw", "kmax", "krec", "kk"] + \
         [f"{n}{d}" for d in range(2) for n in ("scan", "ct", "cc", "w", "y", "b", "am", "kd", "A", "R", "B", "K")] + \
         ["ksum", "bon", "bonus"]
    AC = ["sq", "sqrt"] + [f"{n}{d}" for d in range(2) for n in ("sg", "a", "e1", "e2", "e3")]
    PEV = ["kk", "z0", "a0", "z1", "a1", "bon"]
    STORES = 10
    stored, before = C.storing(STORES * PAIRS)

    def dv(q, name):
        return len(TAIL) + q * len(DV) + DV.index(name) + 1

    def ac(q, name):
        return 2 + q * len(AC) + AC.index(name) + 1

    def pv(q, name):
        return q * len(PEV) + PEV.index(name) + 1

    def by_chunk(x):
        return x.rearrange("p (c n) -> p c n", n=CH)

    def bank(first, n=W):
        return C.psum[:, first:first + 3, :].rearrange("p a b -> p (a b)")[:, 0:n]

    with nc.Block() as block:
        @block.gpsimd
        def _(pool):
            for x in range(3):
                nc.gpsimd.memset(raw[x], 0.0).then_inc(padded, 1)
            for q in range(PAIRS):
                pool.wait_ge(dstep, dv(q, "c212"))
                pool.dma_start(v_chunked[:, :, q, :].rearrange("c p n -> p c n"), by_chunk(v_)).then_inc(stored, 16)
                for d in range(2):
                    for x, n in enumerate(("A", "R", "B", "K")):
                        pool.wait_ge(dstep, dv(q, f"{n}{d}"))
                        pool.dma_start(chunked[d, :, :, x, q, :].rearrange("c p n -> p c n"),
                                       by_chunk(outs[d][x])).then_inc(stored, 16)
                pool.wait_ge(dstep, dv(q, "bonus"))
                pool.dma_start(rows(bonus, q), rn[:, CT:W]).then_inc(stored, 16)
            pool.wait_ge(stored, 16 * STORES * PAIRS + before)

        @block.sync
        def _(sp):
            sp.dma_start(starts, ins["k_starts"]).then_inc(wload, 16)
            for d in range(2):
                sp.dma_start(w2[0:32, d, :], ins["decay_w2"][0, d, :, :]).then_inc(wload, 16)
                sp.dma_start(w2[32:64, d, :], ins["iclr_a2"][0, d, :, :]).then_inc(wload, 16)
            sp.wait_ge(padded, 3)
            for x, (r0, n) in enumerate([(3 * RW, 64), (3 * RW + 64, GL)]):
                for s, (a0, m) in enumerate(SEGS):
                    sp.dma_start(raw[x][0:n, a0 + 1 + s:a0 + 1 + s + m], rw[r0:r0 + n, a0:a0 + m])\
                      .then_inc(loaded[x], 16)
            for q in range(PAIRS):
                for x in range(3):
                    sp.wait_ge(dstep, len(TAIL) - 1 if q == 0 else dv(q - 1, f"c{x}12"))
                    for s, (a0, m) in enumerate(SEGS):
                        r0 = x * RW + q * P
                        sp.dma_start(raw[x][:, a0 + 1 + s:a0 + 1 + s + m], rw[r0:r0 + P, a0:a0 + m])\
                          .then_inc(loaded[x], 16)

        def conv(dve, x, s, k, src, dst, row, parts, step):
            a0, m = SEGS[s]
            i = src[0:parts, a0 + s + k:a0 + s + k + m]
            o = dst[0:parts, a0:a0 + m]
            c = C.par(f"conv{k}", row, parts)
            if step > 1:
                dve.wait_ge(dstep, step - 1)
            if k == 0:
                nc.vector.tensor_scalar(o, i, c, None, ALU.mult).then_inc(dstep, 1)
            else:
                nc.vector.scalar_tensor_tensor(o, i, c, o, ALU.mult, ALU.add).then_inc(dstep, 1)

        @block.vector
        def _(dve):
            n = 0
            for x in range(2):
                dve.wait_ge(loaded[x], 32)
                for s in range(2):
                    for k in range(3):
                        n += 1
                        conv(dve, x, s, k, raw[x], (tail, gate)[x], 12 + x, (64, GL)[x], n)
            nc.vector.tensor_scalar(C.omka[:, :], C.params[:, PARAM_ROWS["k_a"]:PARAM_ROWS["k_a"] + PAIRS], -1.0, 1.0,
                                    ALU.mult, ALU.add).then_inc(dstep, 1)
            dve.wait_ge(wload, 80)
            for q in range(PAIRS):
                def step(name, f, *args):
                    dve.wait_ge(dstep, dv(q, name) - 1)
                    f(*args).then_inc(dstep, 1)

                tt, ts, stt = nc.vector.tensor_tensor, nc.vector.tensor_scalar, nc.vector.scalar_tensor_tensor
                if q > 0:
                    dve.wait_ge(stored, 16 * STORES * q + before)
                for x in range(3):
                    dve.wait_ge(loaded[x], 32 * (q + 1) + (32 if x < 2 else 0))
                    for s in range(2):
                        for k in range(3):
                            conv(dve, x, s, k, raw[x], cv[x], 4 * x + q, P, dv(q, f"c{x}{s}{k}"))
                step("kraw", ts, kraw, k_, C.par("k_k", q), None, ALU.mult)
                dve.wait_ge(pstep, pv(q, "kk"))
                step("kmax", ts, rn, bank(0), 1e-24, None, ALU.max)
                step("krec", nc.vector.reciprocal, rn, rn)
                dve.wait_ge(astep, ac(q, "sqrt"))
                step("kk", tt, kk, kraw, rn, ALU.mult)
                for d in range(2):
                    cumc, wc = by_chunk(cum), by_chunk(w)
                    dve.wait_ge(astep, ac(q, f"sg{d}"))
                    step(f"scan{d}", nc.vector.tensor_tensor_scan, cum, starts, sg, 0.0, ALU.mult, ALU.add)
                    step(f"ct{d}", nc.vector.tensor_copy, C.ends[:, 0, d, q, :], cumc[:, :, CH - 1])
                    step(f"cc{d}", nc.vector.tensor_copy, C.ends[:, 1, d, q, :], cumc[:, :, CH // 2 - 1])
                    step(f"w{d}", tt, wc, cumc, cumc[:, :, CH // 2 - 1:CH // 2].broadcast_to([P, NCH, CH]),
                         ALU.subtract)
                    step(f"y{d}", tt, y, w, sg, ALU.subtract)
                    dve.wait_ge(astep, ac(q, f"a{d}"))
                    step(f"b{d}", tt, b, kk, a, ALU.mult)
                    step(f"am{d}", ts, kd[d], a, C.par("k_a", q), C.omka[:, q:q + 1], ALU.mult, ALU.add)
                    step(f"kd{d}", tt, kd[d], kd[d], k_, ALU.mult)
                    dve.wait_ge(astep, ac(q, f"e3{d}"))
                    eA, eR, eB = (e3, e2, e1) if d == 0 else (e1, e2, e3)
                    step(f"A{d}", tt, outs[d][0], kk, eA, ALU.mult)
                    step(f"R{d}", tt, outs[d][1], r_, eR, ALU.mult)
                    step(f"B{d}", tt, outs[d][2], b, eB, ALU.mult)
                    step(f"K{d}", tt, outs[d][3], kd[d], eB, ALU.mult)
                step("ksum", tt, kd[0][:, CT:W], kd[0][:, CT:W], kd[1][:, CT:W], ALU.add)
                step("bon", stt, kd[0][:, CT:W], r_[:, CT:W], C.par("r_k", q), kd[0][:, CT:W], ALU.mult, ALU.mult)
                dve.wait_ge(pstep, pv(q, "bon"))
                step("bonus", tt, rn[:, CT:W], bank(0, T), v_[:, CT:W], ALU.mult)
            E, tot, mid = C.decay, C.ends[:, 0], C.ends[:, 1]
            last = dv(PAIRS - 1, "bonus")
            dve.wait_ge(dstep, last)
            nc.vector.memset(E[:, :, :, :], 0.0).then_inc(dstep, 1)
            nc.vector.tensor_tensor(tot, tot, mid, ALU.subtract).then_inc(dstep, 1)
            dve.wait_ge(dstep, last + 2)
            nc.vector.tensor_tensor(E[:, 0, :, 0:NCH - 1], tot[:, 0, :, 0:NCH - 1], mid[:, 0, :, 1:NCH], ALU.add)\
              .then_inc(dstep, 1)
            nc.vector.tensor_tensor(E[:, 1, :, 1:NCH], tot[:, 1, :, 0:NCH - 1], mid[:, 1, :, 1:NCH], ALU.add)\
              .then_inc(dstep, 1)
            nc.vector.tensor_tensor(E[:, 1, :, 0:1], tot[:, 1, :, NCH - 1:NCH], mid[:, 1, :, 0:1], ALU.add)\
              .then_inc(dstep, 1)

        @block.scalar
        def _(act):
            act.wait_ge(dstep, 6)
            nc.scalar.activation(tail[0:32, :], tail[0:32, :], ACT.Tanh).then_inc(astep, 1)
            act.wait_ge(dstep, 12)
            nc.scalar.activation(gate[0:GL, :], gate[0:GL, :], ACT.Sigmoid).then_inc(astep, 1)
            act.wait_ge(astep, 2)
            act.dma_start(gate_in, gate[0:GL, CT:W]).then_inc(gate_out, 16)
            act.wait_ge(gate_out, 16)
            for q in range(PAIRS):
                act.wait_ge(dstep, dv(q, "kraw"))
                nc.scalar.activation(sqk, kraw, ACT.Square).then_inc(astep, 1)
                act.wait_ge(dstep, dv(q, "krec"))
                nc.scalar.activation(rn, rn, ACT.Sqrt).then_inc(astep, 1)
                for d in range(2):
                    act.wait_ge(pstep, pv(q, f"z{d}"))
                    if d == 1:
                        act.wait_ge(dstep, dv(q, "y0"))
                    nc.scalar.activation(sg, bank(3), ACT.Sigmoid, bias=C.par("decay_w0", 4 * d + q)).then_inc(astep, 1)
                    act.wait_ge(pstep, pv(q, f"a{d}"))
                    if d == 1:
                        act.wait_ge(dstep, dv(q, "kd0"))
                    nc.scalar.activation(a, bank(0), ACT.Sigmoid, bias=C.par("iclr_a0", 4 * d + q)).then_inc(astep, 1)
                    act.wait_ge(dstep, dv(q, "K0") if d else dv(q, "y0"))
                    act.wait_ge(dstep, dv(q, f"y{d}"))
                    nc.scalar.activation(e1, w, ACT.Exp, scale=KAPPA).then_inc(astep, 1)
                    nc.scalar.activation(e2, y if d else w, ACT.Exp, scale=KAPPA if d else -KAPPA).then_inc(astep, 1)
                    nc.scalar.activation(e3, y, ACT.Exp, scale=-KAPPA).then_inc(astep, 1)
            act.wait_ge(dstep, dv(PAIRS - 1, "bonus") + 5)
            nc.scalar.activation(C.decay[:, :, :, :], C.decay[:, :, :, :], ACT.Exp, scale=-KAPPA)

        @block.tensor
        def _(pe):
            def product(first, lhsT, rhs, a0=0, n=W):
                for c, (a, m) in enumerate(chunks(n)):
                    mm = pe.matmul(C.psum[:, first + c, 0:m], lhsT, rhs[:, a0 + a:a0 + a + m], start=True, stop=True)
                mm.then_inc(pstep, 1)

            pe.wait_ge(wload, 80)
            for q in range(PAIRS):
                cols = slice(q * P, (q + 1) * P)
                if q > 0:
                    pe.wait_ge(dstep, dv(q - 1, "bonus"))
                pe.wait_ge(astep, ac(q, "sq"))
                product(0, C.mat("headsum"), sqk)
                for d in range(2):
                    if q > 0 or d > 0:
                        pe.wait_ge(astep, ac(q, "sg0") if d else ac(q - 1, "sg1"))
                    product(3, w2[0:32, d, cols], tail[0:32, :])
                    pe.wait_ge(dstep, dv(q, "kmax"))
                    if d == 1:
                        pe.wait_ge(astep, ac(q, "a0"))
                    product(0, w2[32:64, d, cols], tail[32:64, :])
                pe.wait_ge(astep, ac(q, "a1"))
                pe.wait_ge(dstep, dv(q, "bon"))
                product(0, C.mat("headsum"), kd[0], CT, T)


def recurrence(C, chunked, v_chunked, yT):
    nc, ins = C.nc, C.ins
    NU = 2 * 2 * PAIRS
    at = [0]

    def tile(*shape):
        v = C.slot(1, *shape, at=at[0])
        at[0] += int(np.prod(shape))
        return v

    factors = tile(2, 2, 4 * PAIRS, CH)
    vals = tile(2, 2, PAIRS, CH)
    prods = tile(NU, 2, 2 * CH)
    XX = tile(NU, 2, CH)
    Wt = tile(NU, CH)
    toks = tile(3, 2, PAIRS, CH)
    W0s = tile(2, 2, PAIRS, HD)
    Us = tile(2, 2 * PAIRS, HD)
    S = tile(2, PAIRS, HD)
    corner = tile(2, LEVELS + 1, CH)
    keep_f = tile(2, 2 * CH)
    assert at[0] <= 4 * SLOT, at[0]
    keep = keep_f.bitcast(I32)
    names = ("consts", "cleared", "tok_turned", "tok_copied", "prod", "kept", "mprod", "m_used", "first",
             "xx", "w_ok", "zprod", "wprod", "w0p", "w0c", "up", "uc", "yp", "y_copied", "s_done", "s_new", "s_sum")
    (consts, cleared, tok_turned, tok_copied, prod, kept, mprod, m_used, first, xx, w_ok, zprod, wprod,
     w0p, w0c, up, uc, yp, y_copied, s_done, s_new, s_sum) = (C.sem(n) for n in names)
    loaded = C.pair("loaded")
    turn = C.sem("turn")
    NG = 4
    XL = (LEVELS + 1) * NG
    WL = LEVELS * NG

    def steps(eng):
        for s in range(CC):
            yield s, s, CC - 1 - s, s % 2, s // 2, None
        with eng.Fori(0, (NCH - CC) // 2) as i:
            for j in range(2):
                yield i * 2 + (j + CC), i * 2 + (j + CC), i * (-2) + (NCH - 1 - j), j, i + CC // 2, i * 2 + j

    def heads(d):
        for e in range(2):
            for q in range(PAIRS):
                yield 2 * q + e, 8 * d + 4 * e + q, q, slice(64 * e, 64 * e + 64)

    with nc.Block() as block:
        @block.gpsimd
        def _(pool):
            nc.gpsimd.memset(prods, 0.0).then_inc(cleared, 1)
            nc.gpsimd.memset(S, 0.0).then_inc(cleared, 1)

        @block.sync
        def _(sp):
            sp.dma_start(corner, ins["k_corner"].rearrange("p (a b c) -> p a b c", a=2, b=LEVELS + 1))\
              .then_inc(consts, 16)
            sp.dma_start(keep, ins["k_keep"].rearrange("d p n -> p d n")).then_inc(consts, 16)
            sp.sem_inc(s_done, 4)
            for s, fc, rc, j, m, _ in steps(sp):
                sp.wait_ge(s_done, s * 2 + 2)
                for d, c in enumerate((fc, rc)):
                    sp.dma_start(factors[:, j, d], chunked[d, bass.ds(c, 1), :, :, :, :]
                                 .rearrange("o p a q n -> (o p) (a q) n")).then_inc(loaded[j], 16)
                    sp.dma_start(vals[:, j, d], v_chunked[bass.ds(c, 1), :, :, :]
                                 .rearrange("o p q n -> (o p) q n")).then_inc(loaded[j], 16)

        @block.tensor
        def _(pe):
            for s, fc, rc, j, m, es in steps(pe):
                pe.wait_ge(loaded[j], (m + 1) * 64)
                n = 0
                for d in range(2):
                    for x in range(3):
                        pe.wait_ge(tok_copied, s * 6 + n + 1)
                        for q in range(PAIRS):
                            src = vals[:, j, d, q, :] if x == 2 else factors[:, j, d, (2 + x) * PAIRS + q, :]
                            mm = pe.transpose(C.psum[:, 6 + n % 2, q * CH:(q + 1) * CH], src, C.mat("ident"))
                        mm.then_inc(tok_turned, 1)
                        n += 1
                pe.wait_ge(s_new, s * 2 + 1)
                if es is not None:
                    pe.wait_ge(y_copied, es * 2 + 1)
                for d in range(2):
                    for h, u, q, r in heads(d):
                        pe.wait_ge(kept, s * NU + u + 1)
                        ar = factors[r, j, d, q:2 * PAIRS:PAIRS, :]
                        for x in range(2):
                            mm = pe.matmul(C.psum[:, u % 4, x * 2 * CH:(x + 1) * 2 * CH],
                                           factors[r, j, d, (2 + x) * PAIRS + q, :], ar, start=True, stop=True)
                        mm.then_inc(prod, 1)
                for g in range(NG):
                    pe.wait_ge(m_used, s * NG + g + 1)
                    for h, u, q, r in list(heads(g // 2))[4 * (g % 2):4 * (g % 2) + 4]:
                        mm = pe.matmul(C.psum[:, 4 + g % 2, (u % 4) * CH:(u % 4 + 1) * CH], factors[r, j, g // 2, q, :],
                                       factors[r, j, g // 2, 2 * PAIRS + q, :], start=True, stop=True)
                    mm.then_inc(mprod, 1)
                for lv in range(1, LEVELS + 1):
                    def corners(g):
                        pe.wait_ge(xx, s * XL + (lv - 1) * NG + g + 1)
                        pe.wait_ge(w_ok, s * WL + (lv - 1) * NG + g + 1)
                        for u in range(4 * g, 4 * g + 4):
                            mm = pe.matmul(C.psum[:, g % 2, (u % 4) * CH:(u % 4 + 1) * CH], prods[:, u, 0, 0:CH],
                                           XX[:, u, 0, :], start=True, stop=True)
                        mm.then_inc(wprod, 1)

                    def merge(g):
                        pe.wait_ge(w_ok, s * WL + (lv - 1) * NG + g + 3)
                        zb = C.psum[:, 2 + 2 * (g % 2):4 + 2 * (g % 2), :].rearrange("p a (b c) -> p (a b) c", c=CH)
                        for u in range(4 * g, 4 * g + 4):
                            if lv < LEVELS:
                                pe.matmul(zb[:, 2 * (u % 4), :], XX[:, u, 1, :], Wt[:, u, :], start=True, stop=True)
                            mm = pe.matmul(zb[:, 2 * (u % 4) + 1, :], Wt[:, u, :], XX[:, u, 1, :], start=True,
                                           stop=True)
                        mm.then_inc(zprod, 1)

                    for g in range(NG):
                        corners(g)
                        if g > 0:
                            merge(g - 1)
                    merge(NG - 1)
                pe.wait_ge(tok_copied, s * 6 + 8)
                pe.wait_ge(xx, s * XL + XL)
                for d in range(2):
                    for h, u, q, r in heads(d):
                        o = C.psum[:, 2 * d + h % 2, q * HD:(q + 1) * HD]
                        pe.matmul(o, factors[r, j, d, q, :], S[r, d, q, :], start=True, stop=False)
                        mm = pe.matmul(o, prods[:, u, 1, 0:CH],
                                       toks[:, 2, d, q, r.start:r.stop], start=False, stop=True)
                    mm.then_inc(w0p, 1)
                for d in range(2):
                    pe.wait_ge(w0c, s * 2 + d + 1)
                    for h, u, q, r in heads(d):
                        mm = pe.matmul(C.psum[:, 4 + d, h * HD:(h + 1) * HD], XX[:, u, 1, :], W0s[:, d, h % 2, q, :],
                                       start=True, stop=True)
                    mm.then_inc(up, 1)
                for d in range(2):
                    pe.wait_ge(uc, s * 2 + d + 1)
                    pe.sem_inc(turn, 1)
                    if es is not None:
                        for h, u, q, r in heads(d):
                            o = C.psum[r, d, q * CH:(q + 1) * CH]
                            pe.matmul(o, S[r, d, q, :], factors[r, j, d, PAIRS + q, :], start=True, stop=False)
                            pe.matmul(o, Us[:, d, h, :], prods[:, u, 0, CH:2 * CH], start=False, stop=False)
                            mm = pe.matmul(o, toks[:, 2, d, q, r.start:r.stop], prods[:, u, 1, CH:2 * CH],
                                           start=False, stop=True)
                        mm.then_inc(yp, 1)
                    for q in range(PAIRS):
                        o = C.psum[:, 2 + d, q * CH:(q + 1) * CH]
                        pe.matmul(o, toks[:, 0, d, q, :], Us[:, d, 2 * q:2 * q + 2, :].rearrange("p a b -> p (a b)"),
                                  start=True, stop=False)
                        mm = pe.matmul(o, toks[:, 1, d, q, :], toks[:, 2, d, q, :], start=False, stop=True)
                    mm.then_inc(s_done, 1)

        @block.scalar
        def _(act):
            act.sem_inc(tok_copied, 2)
            act.sem_inc(y_copied, 1)
            for s, fc, rc, j, m, es in steps(act):
                n = 0
                for d in range(2):
                    for x in range(3):
                        act.wait_ge(tok_turned, s * 6 + n + 1)
                        nc.scalar.activation(toks[:, x, d], C.psum[:, 6 + n % 2, :]
                                             .rearrange("p (q n) -> p q n", n=CH), ACT.Copy).then_inc(tok_copied, 1)
                        n += 1
                for d in range(2):
                    act.wait_ge(w0p, s * 2 + d + 1)
                    nc.scalar.activation(W0s[:, d], C.psum[:, 2 * d:2 * d + 2, 0:PAIRS * HD]
                                         .rearrange("p e (q v) -> p e q v", v=HD),
                                         ACT.Copy).then_inc(w0c, 1)
                for d in range(2):
                    act.wait_ge(up, s * 2 + d + 1)
                    nc.scalar.activation(Us[:, d], C.psum[:, 4 + d, :].rearrange("p (h v) -> p h v", v=HD),
                                         ACT.Copy, scale=-1.0).then_inc(uc, 1)
                if es is not None:
                    for d, c in enumerate((fc, rc)):
                        act.wait_ge(yp, es * 2 + d + 1)
                        nc.scalar.activation(yT[d][:, :, bass.ds((c - CC) * CH, CH)],
                                             C.psum[:, d, :].rearrange("p (q n) -> p q n", n=CH),
                                             ACT.Copy).then_inc(y_copied, 1)

        @block.vector
        def _(dve):
            dve.sem_inc(kept, 4)
            dve.sem_inc(m_used, 2)
            dve.sem_inc(w_ok, 2)
            dve.wait_ge(consts, 32)
            dve.wait_ge(cleared, 2)
            dve.sem_inc(s_new, 1)
            ident = C.mat("ident").unsqueeze(1).broadcast_to([P, 4, CH])
            for s, fc, rc, j, m, es in steps(dve):
                for u in range(NU):
                    dve.wait_ge(prod, s * NU + u + 1)
                    dve.sem_inc(turn, 1)
                    k2 = keep[:, u // 8, :].unsqueeze(1).broadcast_to([P, 2, 2 * CH])
                    nc.vector.copy_predicated(prods[:, u], k2, C.psum[:, u % 4, :]
                                              .rearrange("p (a b) -> p a b", a=2)).then_inc(kept, 1)
                for g in range(NG):
                    d, us = g // 2, slice(4 * g, 4 * g + 4)
                    c0 = corner[:, d, 0, :].unsqueeze(1).broadcast_to([P, 4, CH])
                    c0t = corner[:, 1 - d, 0, :].unsqueeze(1).broadcast_to([P, 4, CH])
                    dve.wait_ge(mprod, s * NG + g + 1)
                    nc.vector.tensor_tensor(XX[:, us, 0, :], C.psum[:, 4 + g % 2, :]
                                            .rearrange("p (a b) -> p a b", b=CH), c0, ALU.mult).then_inc(m_used, 1)
                    dve.wait_ge(kept, s * NU + 4 * g + 8)
                    nc.vector.tensor_tensor(XX[:, us, 1, :], prods[:, us, 0, 0:CH], c0t, ALU.mult).then_inc(first, 1)
                    dve.wait_ge(m_used, s * NG + g + 3)
                    nc.vector.tensor_tensor(XX[:, us, 0, :], ident, XX[:, us, 0, :], ALU.subtract).then_inc(first, 1)
                    dve.wait_ge(first, s * (2 * NG) + 2 * g + 1)
                    nc.vector.tensor_tensor(XX[:, us, 1, :], ident, XX[:, us, 1, :], ALU.subtract).then_inc(xx, 1)
                    dve.wait_ge(first, s * (2 * NG) + 2 * g + 2)
                for lv in range(1, LEVELS + 1):
                    def corners(g):
                        dve.wait_ge(wprod, s * WL + (lv - 1) * NG + g + 1)
                        c = corner[:, g // 2, lv, :].unsqueeze(1).broadcast_to([P, 4, CH])
                        nc.vector.tensor_tensor(Wt[:, 4 * g:4 * g + 4, :], C.psum[:, g % 2, :]
                                                .rearrange("p (a b) -> p a b", b=CH), c, ALU.mult).then_inc(w_ok, 1)

                    def merge(g):
                        dve.wait_ge(zprod, s * WL + (lv - 1) * NG + g + 1)
                        zb = C.psum[:, 2 + 2 * (g % 2):4 + 2 * (g % 2), :].rearrange("p a (b x c) -> p (a b) x c", x=2, c=CH)
                        us = slice(4 * g, 4 * g + 4)
                        x0 = 1 if lv == LEVELS else 0
                        dve.wait_ge(xx, s * XL + (lv - 1) * NG + g + 1)
                        nc.vector.tensor_tensor(XX[:, us, x0:2, :], XX[:, us, x0:2, :], zb[:, :, x0:2, :],
                                                ALU.subtract).then_inc(xx, 1)

                    for g in range(NG):
                        corners(g)
                        if g > 0:
                            merge(g - 1)
                    merge(NG - 1)
                for d, c in enumerate((fc, rc)):
                    dve.wait_ge(s_done, s * 2 + d + 1 + 4)
                    for e in range(2):
                        r = slice(64 * e, 64 * e + 64)
                        nc.vector.tensor_tensor(S[r, d], C.psum[r, 2 + d, :].rearrange("p (q n) -> p q n", n=CH)
                                                [:, :, 64 * e:64 * e + 64], S[r, d], ALU.add).then_inc(s_sum, 1)
                    dve.wait_ge(s_sum, s * 4 + 2 * d + 2)
                    dec = C.decay[:, d, :, bass.ds(c, 1)].broadcast_to([P, PAIRS, HD])
                    nc.vector.tensor_tensor(S[:, d], S[:, d], dec, ALU.mult).then_inc(s_new, 1)


def rwkv_output(C, yT, bonus, gate_in, out, slot):
    nc, ins = C.nc, C.ins
    g2 = C.slot(slot, 1, RW, parts=GL)[:, 0, :]
    sgate = C.slot(slot, 1, T, at=RW, parts=GL)[:, 0, :]
    bon = C.slot(slot, PAIRS, T, at=RW + T)
    sq = C.slot(slot + 1, 1, 512)[:, 0, :]
    rstd = C.slot(slot + 1, 1, 512, at=512)[:, 0, :]
    loaded, dstep, astep, pstep = (C.sem(n) for n in ("loaded", "dstep", "astep", "pstep"))
    DV = ["sum", "center", "eps", "rec", "scale", "bias", "gate"]
    units = [(q, a) for q in range(PAIRS) for a in range(0, T, 512)]

    def dv(n, name):
        return n * len(DV) + DV.index(name) + 1

    with nc.Block() as block:
        @block.sync
        def _(sp):
            sp.dma_start(g2, ins["gate_g2"][0, :, :]).then_inc(loaded, 16)
            sp.dma_start(sgate, gate_in).then_inc(loaded, 16)
            sp.dma_start(bon, bonus.rearrange("(q p) n -> p q n", p=P)).then_inc(loaded, 16)

        @block.tensor
        def _(pe):
            pe.wait_ge(loaded, 48)
            for n, (q, a) in enumerate(units):
                y = out[:, q, a:a + 512]
                pe.wait_ge(dstep, dv(n, "sum"))
                pe.matmul(C.psum[:, 0, :], C.mat("headsum"), y, start=True, stop=True).then_inc(pstep, 1)
                pe.matmul(C.psum[:, 2, :], g2[:, q * P:(q + 1) * P], sgate[:, a:a + 512], start=True, stop=True)
                pe.wait_ge(astep, 2 * n + 1)
                pe.matmul(C.psum[:, 1, :], C.mat("headsum"), sq, start=True, stop=True).then_inc(pstep, 1)

        @block.scalar
        def _(act):
            for n, (q, a) in enumerate(units):
                act.wait_ge(dstep, dv(n, "center"))
                nc.scalar.activation(sq, out[:, q, a:a + 512], ACT.Square).then_inc(astep, 1)
                act.wait_ge(dstep, dv(n, "rec"))
                nc.scalar.activation(rstd, rstd, ACT.Sqrt).then_inc(astep, 1)

        @block.vector
        def _(dve):
            dve.wait_ge(loaded, 48)
            for n, (q, a) in enumerate(units):
                y = out[:, q, a:a + 512]

                def step(name, f, *args):
                    if dv(n, name) > 1:
                        dve.wait_ge(dstep, dv(n, name) - 1)
                    f(*args).then_inc(dstep, 1)

                tt, ts, stt = nc.vector.tensor_tensor, nc.vector.tensor_scalar, nc.vector.scalar_tensor_tensor
                step("sum", tt, y, yT[0][:, q, a:a + 512], yT[1][:, q, a:a + 512], ALU.add)
                dve.wait_ge(pstep, 2 * n + 1)
                step("center", stt, y, C.psum[:, 0, :], -1.0 / HD, y, ALU.mult, ALU.add)
                dve.wait_ge(pstep, 2 * n + 2)
                step("eps", ts, rstd, C.psum[:, 1, :], 1.0 / HD, LNX_EPS, ALU.mult, ALU.add)
                step("rec", nc.vector.reciprocal, rstd, rstd)
                dve.wait_ge(astep, 2 * n + 2)
                step("scale", stt, y, y, C.par("lnx_w", q), rstd, ALU.mult, ALU.mult)
                step("bias", stt, y, y, C.par("lnx_b", q), bon[:, q, a:a + 512], ALU.add, ALU.add)
                step("gate", tt, y, y, C.psum[:, 2, :], ALU.mult)


def move(C, pairs):
    moved = C.sem("moved")
    with C.nc.Block() as block:
        @block.sync
        def _(sp):
            for dst, src in pairs:
                sp.dma_start(dst, src).then_inc(moved, 16)
            sp.wait_ge(moved, 16 * len(pairs))


def pad_keys(C, kraw, kr, vt):
    zero = C.slot(5, 1, P)[:, 0, :]
    cleared, stored = C.sem("cleared"), C.sem("stored")
    with C.nc.Block() as block:
        @block.gpsimd
        def _(pool):
            C.nc.gpsimd.memset(zero, 0.0).then_inc(cleared, 1)

        @block.sync
        def _(sp):
            sp.dma_start(kr[:, 0:CT], kraw[:, 0:CT]).then_inc(stored, 16)
            sp.wait_ge(cleared, 1)
            for a in (CT, CT + P + T):
                sp.dma_start(kr[:, a:a + P], zero).then_inc(stored, 16)
                sp.dma_start(vt[a:a + P, :], zero).then_inc(stored, 16)
            sp.wait_ge(stored, 80)

        @block.vector
        def _(dve):
            C.nc.vector.tensor_scalar(C.small[:, 8:8 + NQ], C.small[:, 0:NQ], -1.0, None, ALU.mult)


TWO_PI = 2.0 * np.pi
TP1 = 6.28125
TP2 = float(np.round((TWO_PI - TP1) * 2.0 ** 19) / 2.0 ** 19)
TP3 = float(TWO_PI - TP1 - TP2)
ROUND = 1.5 * 2.0 ** 23
PI_BELOW = 3.1415925


def position_tables(C, cos, sin, slot):
    nc, ins = C.nc, C.ins
    pi = C.slot(slot, 1, T, parts=QKD)[:, 0, :]
    ang, k, r = (C.slot(slot, 1, T, at=T * (1 + x), parts=QKD)[:, 0, :] for x in range(3))
    loaded, seq, done = C.sem("loaded"), C.sem("seq"), C.sem("done")
    with nc.Block() as block:
        @block.sync
        def _(sp):
            sp.dma_start(pi.bitcast(I32), ins["positions_2"].broadcast_to([QKD, T])).then_inc(loaded, 16)

        @block.vector
        def _(dve):
            n = [0]

            def step(f, *args):
                if n[0]:
                    dve.wait_ge(seq, n[0])
                f(*args).then_inc(seq, 1)
                n[0] += 1

            dve.wait_ge(loaded, 16)
            step(nc.vector.tensor_copy, ang, pi.bitcast(I32))
            step(nc.vector.tensor_scalar, ang, ang, C.mat("freq", QKD), None, ALU.mult)
            for x, (shift, out) in enumerate([(0.0, sin), (0.25, cos)]):
                step(nc.vector.tensor_scalar, k, ang, 1.0 / TWO_PI, shift, ALU.mult, ALU.add)
                step(nc.vector.tensor_scalar, k, k, ROUND, None, ALU.add)
                step(nc.vector.tensor_scalar, k, k, -ROUND, None, ALU.add)
                step(nc.vector.scalar_tensor_tensor, r, k, -TP1, ang, ALU.mult, ALU.add)
                step(nc.vector.scalar_tensor_tensor, r, k, -TP2, r, ALU.mult, ALU.add)
                step(nc.vector.scalar_tensor_tensor, r, k, -TP3, r, ALU.mult, ALU.add)
                step(nc.vector.tensor_scalar, r, r, shift * TWO_PI, PI_BELOW, ALU.add, ALU.min)
                step(nc.vector.tensor_scalar, out, r, -PI_BELOW, None, ALU.max)

        @block.scalar
        def _(act):
            act.wait_ge(seq, 18)
            nc.scalar.activation(sin, sin, ACT.Sin).then_inc(done, 1)
            nc.scalar.activation(cos, cos, ACT.Sin).then_inc(done, 1)


def silu_gate(C, y, gate, slot):
    nc = C.nc
    g = C.slot(slot, 2, T)
    s = C.slot(slot, 2, T, at=2 * T)
    loaded, sig, seq = C.pair("loaded"), C.sem("sig"), C.sem("seq")
    with nc.Block() as block:
        @block.sync
        def _(sp):
            for t in range(KD):
                if t >= 2:
                    sp.wait_ge(seq, 2 * (t - 1))
                sp.dma_start(g[:, t % 2], rows(gate, t)).then_inc(loaded[t % 2], 16)

        @block.scalar
        def _(act):
            for t in range(KD):
                act.wait_ge(loaded[t % 2], 16 * (t // 2 + 1))
                if t >= 2:
                    act.wait_ge(seq, 2 * (t - 1))
                nc.scalar.activation(s[:, t % 2], g[:, t % 2], ACT.Sigmoid).then_inc(sig, 1)

        @block.vector
        def _(dve):
            for t in range(KD):
                dve.wait_ge(loaded[t % 2], 16 * (t // 2 + 1))
                nc.vector.tensor_tensor(y[:, t, :], y[:, t, :], g[:, t % 2], ALU.mult).then_inc(seq, 1)
                dve.wait_ge(sig, t + 1)
                dve.wait_ge(seq, 2 * t + 1)
                nc.vector.tensor_tensor(y[:, t, :], y[:, t, :], s[:, t % 2], ALU.mult).then_inc(seq, 1)


def lru(C, u, y, slot):
    nc, ins = C.nc, C.ins
    NT = TW // P
    lam = C.small[:, 16:16 + NT]
    ex, sr, s2, acc, mx = (C.small[:, 22 + 6 * x:28 + 6 * x] for x in range(5))
    raw = C.slot(slot, 2, T + 4)
    xc, R, Ig, av, tv, rec = (C.slot(slot, 1, T, at=2 * (T + 4) + x * T)[:, 0, :] for x in range(6))
    blocks = C.slot(slot + 1, 2, 2, P, at=512)
    cleared, dstep, astep, pstep = (C.sem(n) for n in ("cleared", "dstep", "astep", "pstep"))
    u_ready, w_ready = C.pair("u_ready"), C.pair("w_ready")
    DV = ["c0", "c1", "c2", "c3", "neg", "one", "rec", "sq", "gx", "gx2", "scan"]
    AC = ["r", "i", "a", "t", "sqrt"]
    TERMS = 9
    N0 = 3 + 3 + 2 * TERMS + 4

    def dv(t, name):
        return N0 + t * len(DV) + DV.index(name) + 1

    def ac(t, name):
        return 1 + t * len(AC) + AC.index(name) + 1

    with nc.Block() as block:
        @block.gpsimd
        def _(pool):
            nc.gpsimd.memset(blocks, 0.0).then_inc(cleared, 1)
            nc.gpsimd.memset(raw, 0.0).then_inc(cleared, 1)

        @block.sync
        def _(sp):
            sp.wait_ge(cleared, 2)
            for t in range(NT):
                if t >= 2:
                    sp.wait_ge(dstep, dv(t - 2, "c3"))
                sp.dma_start(raw[:, t % 2, 3:3 + T], rows(u, t)).then_inc(u_ready[t % 2], 16)
                if t >= 2:
                    sp.wait_ge(pstep, t - 1)
                for x, w in enumerate(("lru_w_rgate_2", "lru_w_igate_2")):
                    for e in range(2):
                        sp.dma_start(blocks[64 * e:64 * e + 64, t % 2, x, 64 * e:64 * e + 64],
                                     ins[w][0, 2 * t + e, :, :]).then_inc(w_ready[t % 2], 16)

        @block.tensor
        def _(pe):
            for t in range(NT):
                pe.wait_ge(w_ready[t % 2], 64 * (t // 2 + 1))
                pe.wait_ge(dstep, dv(t, "c3"))
                if t > 0:
                    pe.wait_ge(astep, ac(t - 1, "i"))
                for x in range(2):
                    for c in range(2):
                        mm = pe.matmul(C.psum[:, 2 * x + c, :], blocks[:, t % 2, x, :], xc[:, c * 512:(c + 1) * 512],
                                       start=True, stop=True)
                mm.then_inc(pstep, 1)

        @block.scalar
        def _(act):
            act.wait_ge(dstep, 2)
            nc.scalar.activation(ex, mx, ACT.Exp, scale=-1.0).then_inc(astep, 1)
            act.wait_ge(dstep, N0)
            for t in range(NT):
                act.wait_ge(pstep, t + 1)
                if t > 0:
                    act.wait_ge(dstep, dv(t - 1, "scan"))
                ps = C.psum[:, 0:4, :].rearrange("p (x a) b -> p x (a b)", x=2)
                nc.scalar.activation(R, ps[:, 0, :], ACT.Sigmoid, bias=C.par("lru_b_r", t)).then_inc(astep, 1)
                nc.scalar.activation(Ig, ps[:, 1, :], ACT.Sigmoid, bias=C.par("lru_b_i", t)).then_inc(astep, 1)
                act.wait_ge(astep, ac(t, "r"))
                nc.scalar.activation(av, R, ACT.Exp, scale=lam[:, t:t + 1]).then_inc(astep, 1)
                nc.scalar.activation(tv, R, ACT.Tanh, scale=lam[:, t:t + 1]).then_inc(astep, 1)
                act.wait_ge(dstep, dv(t, "sq"))
                nc.scalar.activation(rec, rec, ACT.Sqrt).then_inc(astep, 1)

        @block.vector
        def _(dve):
            n = [0]
            tt, ts, stt = nc.vector.tensor_tensor, nc.vector.tensor_scalar, nc.vector.scalar_tensor_tensor

            def step(f, *args):
                if n[0]:
                    dve.wait_ge(dstep, n[0])
                f(*args).then_inc(dstep, 1)
                n[0] += 1

            lm = C.params[:, PARAM_ROWS["lru_lambda"]:PARAM_ROWS["lru_lambda"] + NT]
            step(ts, mx, lm, -1.0, None, ALU.mult)
            step(tt, mx, mx, lm, ALU.max)
            dve.wait_ge(astep, 1)
            step(ts, sr, ex, 2.0, None, ALU.add)
            step(nc.vector.reciprocal, sr, sr)
            step(tt, sr, sr, ex, ALU.mult)
            step(tt, s2, sr, sr, ALU.mult)
            for i in range(TERMS):
                c = 1.0 / (2 * (TERMS - 1 - i) + 1)
                step(tt, acc, acc if i else s2, s2, ALU.mult)
                step(ts, acc, acc, 1.0 if i else 0.0, c, ALU.mult, ALU.add)
            step(stt, acc, acc, 2.0, sr, ALU.mult, ALU.mult)
            step(ts, mx, lm, -1.0, 0.0, ALU.mult, ALU.max)
            step(tt, acc, acc, mx, ALU.add)
            step(ts, lam, acc, -8.0, None, ALU.mult)
            assert n[0] == N0
            for t in range(NT):
                dve.wait_ge(u_ready[t % 2], 16 * (t // 2 + 1))
                if t > 0:
                    dve.wait_ge(pstep, t)
                for k in range(4):
                    w, i = C.par("lru_conv", 6 * k + t), raw[:, t % 2, k:k + T]
                    if k == 0:
                        step(ts, xc, i, w, C.par("lru_conv_b", t), ALU.mult, ALU.add)
                    else:
                        step(stt, xc, i, w, xc, ALU.mult, ALU.add)
                dve.wait_ge(astep, ac(t, "t"))
                step(ts, tv, tv, -2.0, 2e-30, ALU.mult, ALU.max)
                step(ts, rec, tv, 0.5, 1.0, ALU.mult, ALU.add)
                step(nc.vector.reciprocal, rec, rec)
                step(tt, rec, rec, tv, ALU.mult)
                step(tt, Ig, Ig, xc, ALU.mult)
                dve.wait_ge(astep, ac(t, "sqrt"))
                step(tt, Ig, Ig, rec, ALU.mult)
                step(nc.vector.tensor_tensor_scan, y[:, t, :], av, Ig, 0.0, ALU.mult, ALU.add)


def block_kernel(nc, ins, out, stop=None):
    with ExitStack() as ctx:
        C = Core(nc, ctx, ins, out)
        C.ends = ctx.enter_context(nc.sbuf_tensor("ends", [P, 2, 2, PAIRS, NCH], F32))
        C.decay = ctx.enter_context(nc.sbuf_tensor("decay", [P, 2, PAIRS, NCH], F32))
        C.omka = ctx.enter_context(nc.sbuf_tensor("omka", [P, PAIRS], F32))
        full = C.slot
        w_in = ins["w_in"][0, :, :]

        with C.stage():
            setup(C)
        with C.stage():
            modulation(C)
        mod = lambda part, v: (lambda k: C.mod[:, part * KD + k, v:v + 1])
        gain = lambda n: (lambda k: C.gain[:, n, k:k + 1])
        par = lambda name, j=0: (lambda k: C.par(name, j + k))

        xT, cT = full(0, KD, T), full(1, KD, CT)
        hT = full(2, KD, ALL)
        with C.stage():
            turn_in(C, ins["x"][0, :, :], xT, T, D, 0, 5)
        with C.stage():
            turn_in(C, ins["ctx"][0, :, :], cT, CT, D, 0, 5)
        with C.stage():
            norm(C, cT, hT[:, :, 0:CT], CT, KD, 5, gain(1), mod(0, 1))
        with C.stage():
            norm(C, xT, hT[:, :, CT:ALL], T, KD, 5, gain(0), mod(0, 0))

        qraw, qr = C.scratch("qraw", AW, T), C.scratch("qr", AW, T)
        kraw, kr = C.scratch("kraw", P, ALL), C.scratch("kr", P, KP)
        vt = C.scratch("vt", KP, P)
        rw = C.scratch("rw", 3 * RW + DL + IL + GL, ALL)
        gates = C.scratch("gates", 2 * D, T)
        cols = lambda c0: w_in[:, c0:]
        with C.stage():
            linear(C, hT, cols(C_Q), AW // P, KD, T, 4, tok0=CT, dram=qraw)
        with C.stage():
            linear(C, hT, cols(C_K), 1, KD, ALL, 4, dram=kraw)
        with C.stage():
            linear_tok(C, hT, w_in[:, C_V:C_V + P], P, KD, ALL // P, 4, vt, row=lambda t: t + (t >= CT // P))
        with C.stage():
            linear(C, hT, cols(C_R), 3 * RW // P, KD, ALL, 4, dram=rw)
        with C.stage():
            linear(C, hT, cols(C_HW), 1, KD, ALL, 4, width=64, dram=rw[3 * RW:3 * RW + 64, :])
        with C.stage():
            linear(C, hT, cols(C_HG), 1, KD, ALL, 4, width=GL, dram=rw[3 * RW + 64:3 * RW + 64 + GL, :])
        with C.stage():
            linear(C, hT, cols(C_G), 2 * D // P, KD, T, 4, tok0=CT, dram=gates, func=ACT.Sigmoid)

        ya = C.scratch("ya", AW, T)
        axial = full(4, 2, T)
        with C.stage():
            pad_keys(C, kraw, kr, vt)
        with C.stage():
            move(C, [(axial, ins["k_axial"].rearrange("a p n -> p a n"))])
        with C.stage():
            rotate(C, qraw, qr, AW // P, P, T, C.mat("rot"), axial[:, 0, :], axial[:, 1, :], 5)
        with C.stage():
            rotate(C, kraw[:, CT:ALL], None, 1, P, T, C.mat("rot"), axial[:, 0, :], axial[:, 1, :], 5,
                   dst_rows=lambda t: kr[:, CT + P:CT + P + T])
        with C.stage():
            window_attention(C, qr, kr, vt, ya)

        chunked = C.scratch("chunked", 2, NCH, P, 4, PAIRS, CH)
        v_chunked = C.scratch("v_chunked", NCH, P, PAIRS, CH)
        bonus, gate_in = C.scratch("bonus", RW, T), C.scratch("gate_in", GL, T)
        with C.stage():
            rwkv_prepare(C, rw, chunked, v_chunked, bonus, gate_in)
        yT = [full(5, PAIRS, T), full(5, PAIRS, T, at=PAIRS * T)]
        with C.stage():
            recurrence(C, chunked, v_chunked, yT)
        yr, yaT = full(1, PAIRS, T), full(1, PAIRS, T, at=PAIRS * T)
        with C.stage():
            rwkv_output(C, yT, bonus, gate_in, yr, 2)

        with C.stage():
            move(C, [(yaT, ya.rearrange("(k p) n -> p k n", p=P))])
        part, merged, x1 = full(3, KD, T), full(4, KD, T), full(3, KD, T)
        with C.stage():
            linear(C, yaT, ins["w_branch_attn"][0, :, :], KD, AW // P, T, 2, kind="combine", mul=gates[0:D, :],
                   res=part)
        with C.stage():
            linear(C, yr, ins["w_branch_rwkv"][0, :, :], KD, RW // P, T, 2, kind="combine",
                   mul=gates[D:2 * D, :], add_res=part, res=merged)
        with C.stage():
            linear(C, merged, ins["w_out"][0, :, :], KD, KD, T, 2, kind="combine", col=2 * KD, add_res=xT, res=x1)

        x1_d, x2_d = C.scratch("x1", D, T), C.scratch("x2", D, T)
        h2 = full(4, KD, T)
        with C.stage():
            move(C, [(x1_d.rearrange("(k p) n -> p k n", p=P), x1)])
        with C.stage():
            norm(C, x1, h2, T, KD, 5, gain(2), mod(3, 0))
        hid = full(0, DFF // P, T)
        with C.stage():
            linear(C, h2, ins["w_mlp_up"][0, :, :], DFF // P, KD, T, 5, kind="sqrelu", res=hid)
        with C.stage():
            linear(C, hid, ins["w_mlp_down"][0, :, :], KD, DFF // P, T, 4, kind="combine", col=5 * KD, add=x1_d,
                   dram=x2_d)
        h = full(0, KD, T)
        with C.stage():
            move(C, [(h, x2_d.rearrange("(k p) n -> p k n", p=P))])
        with C.stage():
            norm(C, h, h, T, KD, 5, par("norm_f_g"))

        memT = full(1, KD, 256)
        km = [C.scratch(f"km{l}", 256, 256) for l in range(2)]
        vm = [C.scratch(f"vm{l}", 256, 256) for l in range(2)]
        with C.stage():
            turn_in(C, ins["mem_2"][0, :, :], memT, 256, D, 0, 5)
        for l in range(2):
            with C.stage():
                linear(C, memT, ins["w_mem_kv_2"][l, :, :], 2, KD, 256, 4, dram=km[l])
            with C.stage():
                linear_tok(C, memT, ins["w_mem_kv_2"][l, :, 256:512], 256, KD, 2, 4, vm[l])

        y2, mixed = full(1, KD, T), full(2, KD, T)
        gate = [C.scratch(f"gate{l}", D, T) for l in range(2)]
        qm = [C.scratch(f"qm{l}", 256, T) for l in range(2)]
        mem_out = [C.scratch(f"mem_out{l}", 256, T) for l in range(2)]

        def finish_layer(l):
            with C.stage():
                memory_attention(C, qm[l], km[l], vm[l], mem_out[l])
            with C.stage():
                move(C, [(y2[:, TW // P:KD, :], mem_out[l].rearrange("(k p) n -> p k n", p=P))])
            with C.stage():
                silu_gate(C, y2, gate[l], 3)
            with C.stage():
                linear(C, y2, ins["w_out_2"][l, :, :], KD, KD, T, 3, kind="combine", add_res=h, add_scale=ALPHA,
                       res=mixed)
            with C.stage():
                norm(C, mixed, h, T, KD, 5, par("ln_g", 8 * l), par("ln_b", 8 * l), center=True)

        wm = ins["mla_w_in_2"][0, :, :]
        z = full(1, 5, T)
        kr96, krot = C.scratch("kr96", QKD, T), C.scratch("krot", QKD, T)
        q96, q96r = C.scratch("q96", TH * QKD, T), C.scratch("q96r", TH * QKD, T)
        kn, v2, tok = C.scratch("kn", TH * QKN, T), C.scratch("v2", T, TW), C.scratch("tok", TW, T)
        c_g = QL + KVL + QKR
        with C.stage():
            linear(C, h, wm, 5, KD, T, 2, res=z)
        with C.stage():
            linear(C, h, wm[:, QL + KVL - QKN:], 1, KD, T, 2, width=QKD, dram=kr96)
        with C.stage():
            linear(C, h, wm[:, c_g:], KD, KD, T, 2, dram=gate[0])
        with C.stage():
            linear(C, h, wm[:, c_g + D:], 2, KD, T, 2, dram=qm[0])
        zq, zk = z[:, 0:3, :], z[:, 3:5, :]
        with C.stage():
            norm(C, zq, zq, T, 3, 5, par("q_norm"))
        with C.stage():
            norm(C, zk, zk, T, 2, 5, par("kv_norm"))
        with C.stage():
            linear(C, zq, ins["mla_w_uq_2"][0, :, :], TH, 3, T, 2, width=QKD, dram=q96)
        wkv = ins["mla_w_ukv_2"][0, :, :]
        with C.stage():
            linear(C, zk, None, TH, 2, T, 2, width=QKN, dram=kn,
                   w_cols=lambda t: wkv[:, bass.ds(t * (QKN + HD), QKN)])
        with C.stage():
            linear_tok(C, zk, lambda k: wkv[k * P:(k + 1) * P, :].rearrange("p (h c) -> p h c", c=QKN + HD)
                       [:, :, QKN:], TW, 2, T // P, 2, v2, w_view=lambda b: b.rearrange("p (h c) -> p h c", c=HD))
        cos, sin = (full(4, 1, T, at=x * T, parts=QKD)[:, 0, :] for x in range(2))
        with C.stage():
            position_tables(C, cos, sin, 5)
        with C.stage():
            rotate(C, q96, q96r, TH, QKD, T, C.mat("rot_mla", QKD), cos, sin, 5)
        with C.stage():
            rotate(C, kr96, krot, 1, QKD, T, C.mat("rot_mla", QKD), cos, sin, 5)
        with C.stage():
            latent_attention(C, q96r, kn, krot[QKN:QKD, :], v2, tok)
        with C.stage():
            move(C, [(y2[:, 0:TW // P, :], tok.rearrange("(k p) n -> p k n", p=P))])
        finish_layer(0)

        wl = ins["lru_w_in_2"][0, :, :]
        u = C.scratch("u", TW, T)
        with C.stage():
            linear(C, h, wl, TW // P, KD, T, 2, dram=u)
        with C.stage():
            linear(C, h, wl[:, TW:], KD, KD, T, 2, dram=gate[1])
        with C.stage():
            linear(C, h, wl[:, TW + D:], 2, KD, T, 2, dram=qm[1])
        with C.stage():
            lru(C, u, y2, 3)
        finish_layer(1)
        with C.stage():
            turn_out(C, h, out[0, :, :], T, 5)


_INS = ["x", "c", "ctx", "c_ctx", "w_ada", "b_ada", "norm1_g", "w_in", "sink", "conv_w", "decay_w0", "decay_w2",
        "iclr_a0", "iclr_a2", "gate_g2", "k_k", "k_a", "r_k", "lnx_w", "lnx_b", "w_branch_attn", "w_branch_rwkv",
        "w_out", "norm2_g", "w_mlp_up", "w_mlp_down", "norm_f_g", "mem_2", "positions_2", "mla_w_in_2",
        "mla_q_norm_2", "mla_w_uq_2", "mla_kv_norm_2", "mla_w_ukv_2", "lru_w_in_2", "lru_conv_w_2",
        "lru_conv_b_2", "lru_w_rgate_2", "lru_b_rgate_2", "lru_w_igate_2", "lru_b_igate_2", "lru_lambda_2",
        "w_mem_kv_2", "w_out_2", "ln_g_2", "ln_b_2"]


def kernel(**inputs):
    import concourse.bacc as bacc
    from concourse.bass_utils import run_bass_kernel_spmd as run

    nc = bacc.Bacc("TRN2", target_bir_lowering=False, num_devices=1)
    arrays, ins = {}, {}
    given = {n: np.ascontiguousarray(inputs[n]) for n in _INS}
    given.update(shape_constants())
    for name, a in given.items():
        arrays[f"in_{name}"] = a
        ins[name] = nc.dram_tensor(f"in_{name}", a.shape, mybir.dt.from_np(a.dtype), kind="ExternalInput").ap()
    out = nc.dram_tensor("out_0", (1, T, D), F32, kind="ExternalOutput").ap()
    block_kernel(nc, ins, out)
    r = run(nc, [arrays], core_ids=[0])
    return r.results[0]["out_0"]
```

```python
from contextlib import ExitStack, contextmanager

import numpy as np

import concourse.bass as bass
from concourse import mybir

F32 = mybir.dt.float32
I32 = mybir.dt.int32
F32R = mybir.dt.float32r
ALU = mybir.AluOpType
ACT = mybir.ActivationFunctionType
AX_X = mybir.AxisListType.X

P = 128
D = 1024
KD = D // P
T = 1024
CT = 256
ALL = CT + T
HD = 64
NQ, NKV = 8, 2
AW = NQ * HD
RW = 512
PAIRS = RW // P
DL, IL, GL = 32, 32, 96
GRID_W = 64
DFF = 4096
CH = 128
LEVELS = 6
EPS = 1e-6
LNX_EPS = 1e-5 * HD
QL, KVL, QKN, QKR = 384, 256, 64, 32
QKD = QKN + QKR
TH, MH = 12, 4
TW = TH * HD
MIX = D
ALPHA = (2.0 * 2) ** 0.25
NEG = -1e30

C_Q, C_K, C_V, C_R = 0, AW, AW + 128, AW + 256
C_HW = C_R + 3 * RW
C_HA, C_HG = C_HW + DL, C_HW + DL + IL
C_G = C_HG + GL

SLOT = 8192
SLOTS = 6
ARENA_AT = 16512


def turns(eng, n):
    if n >= 4 and n % 2 == 0:
        with eng.Fori(0, n // 2) as i:
            for j in range(2):
                yield i * 2 + j, j, i
    else:
        for t in range(n):
            yield t, t % 2, t // 2


def rows(ap, t, width=P):
    return ap[bass.ds(t * width, width), :]


def chunks(n, size=512):
    return [(a, min(size, n - a)) for a in range(0, n, size)]



CONST = {}
_at = 0
for _n, _w in [("ident", 128), ("rot", 128), ("ones", 128), ("headsum", 128), ("rot_mla", 96),
               ("causal", 128), ("freq", 1)]:
    CONST[_n] = (_at, _w)
    _at += _w
CONST_W = _at


def shape_constants():
    c = np.zeros((P, CONST_W), np.float32)

    def put(name, a):
        at, w = CONST[name]
        c[:a.shape[0], at:at + w] = a

    put("ident", np.eye(P))
    rot = np.zeros((P, P))
    for h in range(2):
        for j in range(32):
            rot[64 * h + 32 + j, 64 * h + j] = -1.0
            rot[64 * h + j, 64 * h + 32 + j] = 1.0
    put("rot", rot)
    put("ones", np.ones((P, P)))
    put("headsum", np.kron(np.eye(2), np.ones((HD, HD))))
    rot = np.zeros((QKD, QKD))
    for j in range(16):
        rot[QKN + 16 + j, QKN + j] = -1.0
        rot[QKN + j, QKN + 16 + j] = 1.0
    put("rot_mla", rot)
    i = np.arange(P)
    put("causal", np.where(i[None, :] <= i[:, None], 0.0, NEG))
    half = QKR // 2
    freq = np.power(np.float32(10000.0), -np.arange(half, dtype=np.float32) / half)
    put("freq", np.concatenate([np.zeros(QKN), freq, freq])[:, None])
    n_freq = HD // 4
    inv = np.power(np.float32(10000.0), -np.arange(n_freq, dtype=np.float32) / n_freq).astype(np.float32)
    row = np.repeat(np.arange(T // GRID_W, dtype=np.float32), GRID_W)
    col = np.tile(np.arange(GRID_W, dtype=np.float32), T // GRID_W)
    ang = np.concatenate([row[:, None] * inv, col[:, None] * inv], axis=-1).T
    axial = np.stack([np.tile(np.cos(ang), (4, 1)), np.tile(np.sin(ang), (4, 1))]).astype(np.float32)
    left = np.where(i[None, :] >= i[:, None], 0.0, NEG)
    right = np.where(i[None, :] <= i[:, None], 0.0, NEG)
    none = np.full((P, P), NEG)
    band = np.zeros((T // P, P, 3 * P), np.float32)
    for b in range(T // P):
        band[b, :, :P] = left if b else none
        band[b, :, 2 * P:] = right if b < T // P - 1 else none
    before = (i[:, None] < i[None, :]).astype(np.int32)
    upto = (i[:, None] <= i[None, :]).astype(np.int32)
    keep = np.stack([np.concatenate([before, upto], 1), np.concatenate([before.T, upto.T], 1)])
    corner = np.zeros((2, LEVELS + 1, P, P), np.float32)
    for lv in range(LEVELS + 1):
        b = 2 << lv
        m = (i[:, None] // b == i[None, :] // b) & (i[:, None] % b >= b // 2) & (i[None, :] % b < b // 2)
        corner[0, lv], corner[1, lv] = m, m.T
    corner = np.ascontiguousarray(corner.transpose(2, 0, 1, 3)).reshape(P, -1)
    starts = np.ones((P, ALL), np.float32)
    starts[:, ::CH] = 0.0
    return {"k_mats": c, "k_axial": axial, "k_band": band, "k_keep": keep.astype(np.int32),
            "k_corner": corner, "k_starts": starts}


PARAM_ROWS = {}
_PARAMS = [("b_ada", 48), ("norm1_g", 8), ("norm2_g", 8), ("norm_f_g", 8),
           ("conv0", 14), ("conv1", 14), ("conv2", 14),
           ("decay_w0", 8), ("k_k", 4), ("k_a", 4), ("r_k", 4), ("c_rows", 8), ("cc_rows", 8),
           ("iclr_a0", 8), ("lnx_w", 4), ("lnx_b", 4), ("lru_conv", 24), ("lru_conv_b", 6),
           ("lru_b_r", 6), ("lru_b_i", 6), ("lru_lambda", 6), ("ln_g", 16), ("ln_b", 16),
           ("q_norm", 3), ("kv_norm", 2)]
_at = 0
for _n, _w in _PARAMS:
    if _at // P != (_at + _w - 1) // P:
        _at = -(-_at // P) * P
    PARAM_ROWS[_n] = _at
    _at += _w
PARAM_TILES = -(-_at // P)


class Core:

    def __init__(self, nc, ctx, ins, out):
        self.nc, self.ins, self.out = nc, ins, out
        self.ctx = ctx
        self.arena = ctx.enter_context(nc.sbuf_tensor("arena", [P, SLOTS * SLOT], F32))
        self.places, self.joint, self.sems = {}, None, 0
        self.mats = ctx.enter_context(nc.sbuf_tensor("mats", [P, CONST_W], F32))
        self.params = ctx.enter_context(nc.sbuf_tensor("params", [P, PARAM_TILES * P], F32))
        self.mod = ctx.enter_context(nc.sbuf_tensor("mod", [P, 48, 2], F32))
        self.gain = ctx.enter_context(nc.sbuf_tensor("gain", [P, 3, KD], F32))
        self.small = ctx.enter_context(nc.sbuf_tensor("small", [P, 64], F32))
        self.psum = ctx.enter_context(nc.psum_tensor("psum", [P, 8, 512], F32))
        self.stages, self.held = 0, None
        self.stored, self.stores = ctx.enter_context(nc.semaphore("stored")), 0

    @contextmanager
    def stage(self):
        self.stages += 1
        with ExitStack() as self.held:
            self.used = []
            yield
            with self.nc.Block() as block:
                @block.sync
                def _(sp):
                    for s in self.used:
                        sp.sem_clear(s)

    @contextmanager
    def together(self):
        with self.stage():
            with self.nc.Block() as self.joint:
                yield
            self.joint = None

    @contextmanager
    def block(self):
        if self.joint is not None:
            yield self.joint
        else:
            with self.nc.Block() as block:
                yield block

    def storing(self, n):
        at, self.stores = self.stores, self.stores + 16 * n
        return self.stored, at

    def sem(self, name):
        self.sems += 1
        self.used.append(self.held.enter_context(self.nc.semaphore(f"{name}_{self.sems}")))
        return self.used[-1]

    def pair(self, name):
        return [self.sem(f"{name}{j}") for j in range(2)]

    def mat(self, name, parts=P):
        at, w = CONST[name]
        return self.mats[0:parts, at:at + w]

    def slot(self, first, *shape, at=0, parts=P):
        return self.view(F32, first, shape, at, parts)

    def slot_r(self, first, *shape, at=0, parts=P):
        return self.view(F32R, first, shape, at, parts)

    def view(self, dtype, first, shape, at, parts):
        n, at = int(np.prod(shape)), int(first * SLOT) + at
        if (at, n, dtype) not in self.places:
            self.places[at, n, dtype] = self.nc.alloc_sbuf_tensor_at(f"place{len(self.places)}", [P, n], dtype,
                                                                     offset=ARENA_AT + 4 * at)
        v = self.places[at, n, dtype][0:parts, :]
        if len(shape) == 2:
            v = v.rearrange("p (a b) -> p a b", a=shape[0])
        elif len(shape) == 3:
            v = v.rearrange("p (a b c) -> p a b c", a=shape[0], b=shape[1])
        elif len(shape) == 4:
            v = v.rearrange("p (a b c d) -> p a b c d", a=shape[0], b=shape[1], c=shape[2])
        return v

    def par(self, name, j=0, parts=P):
        at = PARAM_ROWS[name] + j
        return self.params[0:parts, at:at + 1]

    def scratch(self, name, *shape):
        return self.nc.dram_tensor(name, list(shape), F32).ap()


def setup(C):
    nc, ins = C.nc, C.ins
    raw = C.slot(0, PARAM_TILES, P)
    loaded, cleared, turned = C.sem("loaded"), C.sem("cleared"), C.sem("turned")
    n_loads = [0]
    with C.block() as block:
        @block.gpsimd
        def _(pool):
            nc.gpsimd.memset(raw, 0.0).then_inc(cleared, 1)

        @block.sync
        def _(sp):
            sp.dma_start(C.mats[:, :], ins["k_mats"]).then_inc(loaded, 16)
            sp.dma_start(C.small[:, 0:NQ], ins["sink"].broadcast_to([P, NQ])).then_inc(loaded, 16)
            n_loads[0] = 2
            sp.wait_ge(cleared, 1)

            def put(name, j, ap):
                at = PARAM_ROWS[name] + j
                sp.dma_start(raw[at % P:at % P + ap.shape[0], at // P, 0:ap.shape[1]], ap).then_inc(loaded, 16)
                n_loads[0] += 1

            def vec(name, ap, j=0):
                put(name, j, ap.rearrange("(a b) -> a b", b=P))

            vec("b_ada", ins["b_ada"][0, :])
            for n in ("norm1_g", "norm2_g", "k_k", "k_a", "lnx_w", "lnx_b"):
                vec(n, ins[n][0, :])
            vec("norm_f_g", ins["norm_f_g"])
            for t in range(3):
                w = ins["conv_w"][0, t, :]
                vec(f"conv{t}", w[0:3 * RW])
                put(f"conv{t}", 12, w[3 * RW:3 * RW + DL + IL].rearrange("(a b) -> a b", a=1))
                put(f"conv{t}", 13, w[3 * RW + DL + IL:3 * RW + DL + IL + GL].rearrange("(a b) -> a b", a=1))
            for d in range(2):
                vec("decay_w0", ins["decay_w0"][0, d, :], 4 * d)
                vec("iclr_a0", ins["iclr_a0"][0, d, :], 4 * d)
                vec("ln_g", ins["ln_g_2"][d, :], 8 * d)
                vec("ln_b", ins["ln_b_2"][d, :], 8 * d)
            vec("r_k", ins["r_k"][0, :, :].rearrange("h d -> (h d)"))
            vec("c_rows", ins["c"][0, :])
            vec("cc_rows", ins["c_ctx"])
            for t in range(4):
                vec("lru_conv", ins["lru_conv_w_2"][0, t, :], 6 * t)
            vec("lru_conv_b", ins["lru_conv_b_2"][0, :])
            vec("lru_b_r", ins["lru_b_rgate_2"][0, :])
            vec("lru_b_i", ins["lru_b_igate_2"][0, :])
            vec("lru_lambda", ins["lru_lambda_2"][0, :])
            vec("q_norm", ins["mla_q_norm_2"][0, :])
            vec("kv_norm", ins["mla_kv_norm_2"][0, :])

        @block.tensor
        def _(pe):
            pe.wait_ge(loaded, 16 * n_loads[0])
            for t in range(PARAM_TILES):
                mm = pe.transpose(C.psum[:, 0, t * P:(t + 1) * P], raw[:, t, :], C.mat("ident"))
            mm.then_inc(turned, 1)

        @block.vector
        def _(dve):
            dve.wait_ge(turned, 1)
            nc.vector.tensor_copy(C.params[:, :], C.psum[:, 0, 0:PARAM_TILES * P])


def modulation(C):
    nc, ins = C.nc, C.ins
    WC, BUFS = 512, 4
    N = 6 * D // WC
    w = C.slot(2, BUFS, KD, WC)
    s = C.slot(4, 4, 2, KD)
    gate, sil = s[:, 0], C.slot(4, KD, 2, at=256)
    mm_done, s_act, s_dve, copied = (C.sem(n) for n in ("mm_done", "sig", "sil", "copied"))
    w_ready = [C.sem(f"w_ready{j}") for j in range(BUFS)]
    cols = C.params[:, PARAM_ROWS["c_rows"]:PARAM_ROWS["c_rows"] + 2 * KD].rearrange("p (v k) -> p v k", v=2)

    def load(eng, t):
        if t >= BUFS:
            eng.wait_ge(mm_done, t - BUFS + 1)
        eng.dma_start(w[:, t % BUFS], ins["w_ada"][0, :, t * WC:(t + 1) * WC]
                      .rearrange("(k p) n -> p k n", p=P)).then_inc(w_ready[t % BUFS], 16)

    with C.block() as block:
        @block.scalar
        def _(act):
            load(act, 1)
            load(act, 3)
            nc.scalar.activation(gate, cols, ACT.Sigmoid).then_inc(s_act, 1)
            for t in range(5, N, 2):
                load(act, t)

        @block.sync
        def _(sp):
            for t in range(0, N, 2):
                load(sp, t)

        @block.tensor
        def _(pe):
            pe.wait_ge(s_dve, 1)
            for t in range(N):
                pe.wait_ge(w_ready[t % BUFS], (t // BUFS + 1) * 16)
                if t >= 2:
                    pe.wait_ge(copied, t - 1)
                for m in range(WC // P):
                    for k in range(KD):
                        mm = pe.matmul(C.psum[:, t % 2, 2 * m:2 * m + 2], w[:, t % BUFS, k, m * P:(m + 1) * P],
                                       sil[:, k, :], start=(k == 0), stop=(k == KD - 1))
                mm.then_inc(mm_done, 1)

        @block.vector
        def _(dve):
            dve.wait_ge(s_act, 1)
            nc.vector.tensor_tensor(sil.rearrange("p k v -> p v k"), gate, cols, ALU.mult).then_inc(s_dve, 1)
            for t in range(N):
                dve.wait_ge(mm_done, t + 1)
                nc.vector.tensor_copy(C.mod[:, t * 4:t * 4 + 4, :],
                                      C.psum[:, t % 2, 0:8].rearrange("p (m v) -> p m v", v=2)).then_inc(copied, 1)
            dve.wait_ge(copied, N)
            b = C.params[:, PARAM_ROWS["b_ada"]:PARAM_ROWS["b_ada"] + 48]
            for v in range(2):
                nc.vector.tensor_tensor(C.mod[:, :, v], C.mod[:, :, v], b, ALU.add).then_inc(s_dve, 1)
            dve.wait_ge(s_dve, 3)
            for n, (part, v, g) in enumerate([(1, 0, "norm1_g"), (1, 1, "norm1_g"), (4, 0, "norm2_g")]):
                nc.vector.scalar_tensor_tensor(
                    C.gain[:, n, :], C.mod[:, part * KD:(part + 1) * KD, v], 1.0,
                    C.params[:, PARAM_ROWS[g]:PARAM_ROWS[g] + KD], ALU.add, ALU.mult)


def turn_in(C, src, dst, n_tok, width, at, stage_slot):
    nc = C.nc
    NT, KT = n_tok // P, width // P
    QUADS = [(a, min(4, KT - a)) for a in range(0, KT, 4)]
    raw = C.slot(stage_slot, 2, width)
    x_ready, turned, copied = C.pair("x_ready"), C.sem("turned"), C.sem("copied")
    nq = len(QUADS)
    with C.block() as block:
        @block.sync
        def _(sp):
            for t, j, r in turns(sp, NT):
                sp.wait_ge(turned, t * nq + nq)
                sp.dma_start(raw[:, j], rows(src, t)).then_inc(x_ready[j], 16)

        @block.tensor
        def _(pe):
            pe.sem_inc(turned, 2 * nq)
            for t, j, r in turns(pe, NT):
                pe.wait_ge(x_ready[j], (r + 1) * 16)
                pe.wait_ge(copied, t * nq + nq)
                for q, (a, n) in enumerate(QUADS):
                    for k in range(n):
                        mm = pe.transpose(C.psum[:, 2 * j + q, k * P:(k + 1) * P],
                                          raw[:, j, (a + k) * P:(a + k + 1) * P], C.mat("ident"))
                    mm.then_inc(turned, 1)
            pe.wait_ge(copied, NT * nq + 2 * nq)

        @block.scalar
        def _(act):
            act.sem_inc(copied, 2 * nq)
            for t, j, r in turns(act, NT):
                for q, (a, n) in enumerate(QUADS):
                    act.wait_ge(turned, t * nq + q + 1 + 2 * nq)
                    nc.scalar.activation(dst[:, a:a + n, bass.ds(t * P + at, P)],
                                         C.psum[:, 2 * j + q, 0:n * P].rearrange("p (k t) -> p k t", t=P),
                                         ACT.Copy).then_inc(copied, 1)


def turn_out(C, src, dst, n_tok, stage_slot):
    nc = C.nc
    NT = n_tok // P
    nat = C.slot(stage_slot, 2, D)
    blk = C.slot(stage_slot, 2, KD, P, at=2 * D)
    staged, turned, copied = (C.sem(n) for n in ("staged", "turned", "copied"))
    stored = C.pair("stored")
    with C.block() as block:
        @block.vector
        def _(dve):
            for t, j, r in turns(dve, NT):
                dve.wait_ge(turned, t * 2 + 2)
                nc.vector.tensor_copy(blk[:, j], src[:, :, bass.ds(t * P, P)]).then_inc(staged, 1)

        @block.tensor
        def _(pe):
            pe.sem_inc(turned, 4)
            for t, j, r in turns(pe, NT):
                pe.wait_ge(staged, t + 1)
                pe.wait_ge(copied, t * 2 + 2)
                for q in range(2):
                    for k in range(4):
                        mm = pe.transpose(C.psum[:, 2 * j + q, k * P:(k + 1) * P], blk[:, j, 4 * q + k, :],
                                          C.mat("ident"))
                    mm.then_inc(turned, 1)

        @block.scalar
        def _(act):
            act.sem_inc(copied, 4)
            act.sem_inc(stored[0], 16)
            act.sem_inc(stored[1], 16)
            for t, j, r in turns(act, NT):
                act.wait_ge(stored[j], r * 16 + 16)
                for q in range(2):
                    act.wait_ge(turned, t * 2 + q + 5)
                    nc.scalar.activation(nat[:, j, q * 512:(q + 1) * 512], C.psum[:, 2 * j + q, :],
                                         ACT.Copy).then_inc(copied, 1)

        @block.sync
        def _(sp):
            for t, j, r in turns(sp, NT):
                sp.wait_ge(copied, t * 2 + 6)
                sp.dma_start(rows(dst, t), nat[:, j]).then_inc(stored[j], 16)
            for j in range(2):
                sp.wait_ge(stored[j], NT // 2 * 16 + 16)


def norm(C, src, dst, n_tok, kt, tmp_slot, gain=None, shift=None, center=False, segs=None):
    nc = C.nc
    segs = segs or [(a, n, gain, shift) for a, n in chunks(n_tok)]
    sq = C.slot(tmp_slot, 2, 512)
    rstd = C.slot(tmp_slot, 2, 512, at=1024)
    sq_ready, sq_used, summed, mean_ready, rs, scaled, shifted = (
        C.sem(n) for n in ("sq_ready", "sq_used", "summed", "mean_ready", "rs", "scaled", "shifted"))
    NS = len(segs)
    inv = 1.0 / (kt * P)
    per = kt + 3 + (kt if center else 0)
    x = dst if center else src
    with C.block() as block:
        @block.scalar
        def _(act):
            n = 0
            for s, (a, w, g, sh) in enumerate(segs):
                for k in range(kt):
                    if center:
                        act.wait_ge(scaled, per * s + k + 1)
                    if n >= 2:
                        act.wait_ge(sq_used, n - 1)
                    nc.scalar.activation(sq[:, n % 2, 0:w], x[:, k, a:a + w], ACT.Square).then_inc(sq_ready, 1)
                    n += 1
                act.wait_ge(scaled, per * s + (kt if center else 0) + 2)
                nc.scalar.activation(rstd[:, s % 2, 0:w], rstd[:, s % 2, 0:w], ACT.Sqrt).then_inc(rs, 1)
                if sh is not None:
                    for k in range(kt):
                        act.wait_ge(scaled, per * s + (kt if center else 0) + 3 + k + 1)
                        nc.scalar.activation(dst[:, k, a:a + w], dst[:, k, a:a + w], ACT.Identity, bias=sh(k))

        @block.tensor
        def _(pe):
            n = 0
            for s, (a, w, g, sh) in enumerate(segs):
                if center:
                    for k in range(kt):
                        mm = pe.matmul(C.psum[:, 2 + s % 2, 0:w], C.mat("ones"), src[:, k, a:a + w],
                                       start=(k == 0), stop=(k == kt - 1))
                    mm.then_inc(mean_ready, 1)
                for k in range(kt):
                    pe.wait_ge(sq_ready, n + 1)
                    if k == 0 and s >= 2:
                        pe.wait_ge(rs, s - 1)
                    mm = pe.matmul(C.psum[:, s % 2, 0:w], C.mat("ones"), sq[:, n % 2, 0:w],
                                   start=(k == 0), stop=(k == kt - 1)).then_inc(sq_used, 1)
                    n += 1
            pe.wait_ge(rs, NS)

        @block.vector
        def _(dve):
            for s, (a, w, g, sh) in enumerate(segs):
                at = per * s
                if center:
                    dve.wait_ge(mean_ready, s + 1)
                    nc.vector.tensor_scalar(rstd[:, s % 2, 0:w], C.psum[:, 2 + s % 2, 0:w], inv, None,
                                            ALU.mult).then_inc(shifted, 1)
                    dve.wait_ge(shifted, s + 1)
                    for k in range(kt):
                        nc.vector.tensor_tensor(dst[:, k, a:a + w], src[:, k, a:a + w], rstd[:, s % 2, 0:w],
                                                ALU.subtract).then_inc(scaled, 1)
                    at += kt
                dve.wait_ge(sq_used, kt * (s + 1))
                dve.wait_ge(scaled, at) if at else None
                nc.vector.tensor_scalar(rstd[:, s % 2, 0:w], C.psum[:, s % 2, 0:w], inv, EPS, ALU.mult,
                                        ALU.add).then_inc(scaled, 1)
                dve.wait_ge(scaled, at + 1)
                nc.vector.reciprocal(rstd[:, s % 2, 0:w], rstd[:, s % 2, 0:w]).then_inc(scaled, 1)
                dve.wait_ge(rs, s + 1)
                dve.sem_inc(scaled, 1)
                for k in range(kt):
                    nc.vector.scalar_tensor_tensor(dst[:, k, a:a + w], x[:, k, a:a + w], g(k),
                                                   rstd[:, s % 2, 0:w], ALU.mult, ALU.mult).then_inc(scaled, 1)


def job(w, n, hi, lo, kt, n_tok=T, tok0=0, width=P, dram=None, res=None, func=None, mul=None, add=None,
        scale=1.0, col=None, w_view=None, w_parts=1, kind=None, own=False):
    src = w_view or (lambda t, b: [(b, w[:, bass.ds(t * width, P)].rearrange("(k p) n -> p k n", p=P))])
    return dict(n=n, hi=hi, lo=lo, kt=kt, n_tok=n_tok, tok0=tok0, width=width, dram=dram, res=res, func=func,
                mul=mul, add=add, scale=scale, col=col, src=src, parts=w_parts, kind=kind, own=own)


PER = 3


def linears(C, jobs, w_slot, kind="copy", splits=()):
    nc = C.nc
    raw = C.slot(w_slot, 2, KD, P)
    w_hi, w_lo = C.slot_r(w_slot, 2, KD, P, at=2 * KD * P), C.slot_r(w_slot, 2, KD, P, at=4 * KD * P)
    width_max = max(jb["n_tok"] for jb in jobs)
    stage = C.slot(w_slot, 2, width_max, at=6 * KD * P)
    ns = sum(s[0].shape[1] for s in splits)
    done, evac, w_split, r_hi, r_lo, sq, hid, turn = (
        C.sem(n) for n in ("done", "evac", "w_split", "r_hi", "r_lo", "sq", "hid", "turn"))
    w_ready, e_ready = C.pair("w_ready"), C.pair("e_ready")
    for jb in jobs:
        jb["kind"] = jb["kind"] or kind
    n_store = sum(jb["n"] for jb in jobs if jb["dram"] is not None)
    stage_free, gated = C.sem("stage_free"), C.sem("gated")
    stored, before = C.storing(n_store)

    def tiles(eng):
        g0, s0, w0, e0 = 0, 0, [0, 0], [0, 0]
        for jb in jobs:
            t0, n = 0, jb["n"]
            if g0 == 0:
                yield jb, 0, 0, 0, 16 * jb["parts"], True, 0, 16
                w0[0], e0[0], t0, g0, n = 16 * jb["parts"], 16 if jb["mul"] is not None else 0, 1, 1, n - 1
            s_at = s0
            body = n // 2 if n // 2 >= 2 else 0
            if body:
                with eng.Fori(0, body) as i:
                    for x in range(2):
                        j = (g0 + x) % 2
                        yield (jb, i * 2 + t0 + x, i * 2 + g0 + x, j, i * (16 * jb["parts"]) + w0[j] + 16 * jb["parts"],
                               False, i * 2 + s_at + t0 + x, i * 16 + e0[j] + 16)
            for m in range(2 * body, n):
                j, i = (g0 + m) % 2, m // 2
                yield (jb, t0 + m, g0 + m, j, w0[j] + 16 * jb["parts"] * (i + 1), False, s_at + t0 + m,
                       e0[j] + 16 * (i + 1))
            for x in range(2):
                used = (n + 1 - x) // 2
                w0[(g0 + x) % 2] += 16 * jb["parts"] * used
                e0[(g0 + x) % 2] += 16 * used if jb["mul"] is not None else 0
            g0 += n
            s0 += jb["n"] if jb["dram"] is not None else 0

    def pieces(jb):
        c = chunks(jb["n_tok"])
        return [(x, a, n, PER - x if x == len(c) - 1 else 1) for x, (a, n) in enumerate(c)]

    for x, jb in enumerate(jobs):
        makers = [y["n"] for y in jobs[:x] if y["kind"] == "sqrelu"]
        jb["p0"], jb["pairs"] = sum(y["n"] for y in jobs[:x]) - sum(makers), 2 * sum(makers)

    def target(jb, t, j, a, n):
        if jb["dram"] is not None:
            return stage[0:jb["width"], j, a:a + n]
        return jb["res"][:, bass.ds(t, 1), a:a + n].rearrange("p o t -> p (o t)")

    def split_weights(eng, op):
        for jb, t, g, j, wr, first, s, e in tiles(eng):
            kt = jb["kt"]
            eng.wait_ge(w_ready[j], wr)
            eng.wait_ge(done, g * PER + PER)
            eng.sem_inc(turn, 1)
            op.tensor_copy(w_hi[:, j, 0:kt, :], raw[:, j, 0:kt, :]).then_inc(w_split, 1)
            eng.wait_ge(w_split, g * 2 + 5)
            op.tensor_tensor(w_lo[:, j, 0:kt, :], raw[:, j, 0:kt, :], w_hi[:, j, 0:kt, :].bitcast(F32),
                             ALU.subtract).then_inc(w_split, 1)
            yield jb, t, g, j, wr, first, s, e

    with C.block() as block:
        @block.sync
        def _(sp):
            for jb, t, g, j, wr, first, s, e in tiles(sp):
                sp.wait_ge(w_split, g * 2 + 2)
                for dst, src in jb["src"](t, raw[:, j, 0:jb["kt"], :]):
                    sp.dma_start(dst, src).then_inc(w_ready[j], 16)
                if jb["mul"] is not None:
                    sp.wait_ge(evac, g * PER + PER)
                    sp.dma_start(stage[:, j, 0:jb["n_tok"]], rows(jb["mul"], t)).then_inc(e_ready[j], 16)

        @block.tensor
        def _(pe):
            pe.sem_inc(done, 2 * PER)
            for jb, t, g, j, wr, first, s, e in tiles(pe):
                pe.wait_ge(w_split, g * 2 + 6)
                pe.wait_ge(evac, g * PER + PER)
                kt, at = jb["kt"], jb["tok0"]
                if jb["own"]:
                    pe.wait_ge(hid, jb["pairs"] + 4)
                for c, a, n, inc in pieces(jb):
                    ps = C.psum[:, j * PER + c, 0:n]
                    for k in range(kt):
                        if ns and first and c == 0:
                            pe.wait_ge(r_lo, k + 1)
                        hi, lo = (jb[x][:, k, at + a:at + a + n] for x in ("hi", "lo"))
                        pe.matmul(ps, w_hi[:, j, k, :], hi, start=(k == 0), stop=False)
                        pe.matmul(ps, w_hi[:, j, k, :], lo, start=False, stop=False)
                        mm = pe.matmul(ps, w_lo[:, j, k, :], hi, start=False, stop=(k == kt - 1))
                    mm.then_inc(done, inc)
                if ns and first:
                    pe.wait_ge(r_lo, ns)
            pe.wait_ge(evac, sum(jb["n"] for jb in jobs) * PER + 2 * PER)

        def split_rhs_hi(act):
            for src, hi, lo in splits:
                for k in range(src.shape[1]):
                    nc.scalar.activation(hi[:, k, :], src[:, k, :], ACT.Copy).then_inc(r_hi, 1)

        def split_rhs_lo(dve, a, b):
            for n, (src, hi, lo, k) in list(enumerate((*s, k) for s in splits for k in range(s[0].shape[1])))[a:b]:
                dve.wait_ge(r_hi, n + 1)
                nc.vector.tensor_tensor(lo[:, k, :], src[:, k, :], hi[:, k, :].bitcast(F32),
                                        ALU.subtract).then_inc(r_lo, 1)

        def pair_at(r, t, a, n):
            return r[:, bass.ds(t, 1), a:a + n].rearrange("p o t -> p (o t)")

        @block.scalar
        def _(act):
            act.sem_inc(evac, 2 * PER)
            if n_store:
                act.sem_inc(stage_free, 2)
            split_rhs_hi(act)
            for jb, t, g, j, wr, first, s, e in tiles(act):
                if jb["kind"] == "combine":
                    continue
                if jb["dram"] is not None:
                    act.wait_ge(stage_free, s + 1)
                act.wait_ge(evac, g * PER + 2 * PER)
                for c, a, n, inc in pieces(jb):
                    piece = (g - jb["p0"]) * 2 + c
                    ps = C.psum[:, j * PER + c, 0:n]
                    act.wait_ge(done, g * PER + (c + 1 if inc == 1 else PER) + 2 * PER)
                    if jb["kind"] == "copy":
                        to = target(jb, t, j, a, n)
                        nc.scalar.activation(to, ps[0:to.shape[0], :], jb["func"] or ACT.Copy).then_inc(evac, inc)
                    else:
                        act.wait_ge(hid, piece + 1)
                        nc.scalar.activation(stage[:, j, a:a + n], ps, ACT.Relu).then_inc(evac, inc)
                        act.wait_ge(sq, piece + 1)
                        nc.scalar.activation(pair_at(jb["res"][0], t, a, n), stage[:, j, a:a + n],
                                             ACT.Copy).then_inc(r_hi, 1)

        @block.vector
        def _(dve):
            dve.sem_inc(hid, 4)
            if n_store:
                dve.sem_inc(w_split, 4)
                split_rhs_lo(dve, 0, ns // 2)
                weights = split_weights(dve, nc.vector)
                next(weights)
                split_rhs_lo(dve, ns // 2, ns)
                for _ in weights:
                    pass
                return
            split_rhs_lo(dve, 0, ns)
            for jb, t, g, j, wr, first, s, e in tiles(dve):
                if jb["kind"] == "combine":
                    dve.wait_ge(evac, g * PER + 2 * PER)
                if jb["mul"] is not None:
                    dve.wait_ge(e_ready[j], e)
                for c, a, n, inc in pieces(jb):
                    piece = (g - jb["p0"]) * 2 + c
                    x, ps = stage[:, j, a:a + n], C.psum[:, j * PER + c, 0:n]
                    if jb["kind"] == "sqrelu":
                        dve.wait_ge(evac, g * PER + (c + 1 if inc == 1 else PER) + 2 * PER)
                        nc.vector.tensor_tensor(x, x, x, ALU.mult).then_inc(sq, 1)
                        dve.wait_ge(sq, piece + 1)
                        dve.wait_ge(r_hi, piece + 1 + ns)
                        hi, lo = (pair_at(r, t, a, n) for r in jb["res"])
                        nc.vector.tensor_tensor(lo, x, hi.bitcast(F32), ALU.subtract).then_inc(hid, 1)
                    else:
                        dve.wait_ge(done, g * PER + (c + 1 if inc == 1 else PER) + 2 * PER)
                        to = target(jb, t, j, a, n)
                        if jb["add"] is not None:
                            other = pair_at(jb["add"], t, a, n)
                        if jb["col"] is not None:
                            nc.vector.scalar_tensor_tensor(to, ps, C.mod[:, bass.ds(t + jb["col"], 1), 0], other,
                                                           ALU.mult, ALU.add).then_inc(evac, inc)
                        elif jb["mul"] is None:
                            nc.vector.scalar_tensor_tensor(to, other, jb["scale"], ps, ALU.mult,
                                                           ALU.add).then_inc(evac, inc)
                        elif jb["add"] is None:
                            nc.vector.tensor_tensor(to, ps, x, ALU.mult).then_inc(evac, inc)
                        else:
                            nc.vector.tensor_tensor(x, ps, x, ALU.mult).then_inc(gated, 1)
                            dve.wait_ge(gated, t * 2 + c + 1)
                            nc.vector.tensor_tensor(to, x, other, ALU.add).then_inc(evac, inc)
        @block.gpsimd
        def _(pool):
            if not n_store:
                pool.sem_inc(w_split, 4)
                for _ in split_weights(pool, nc.gpsimd):
                    pass
                return
            for jb, t, g, j, wr, first, s, e in tiles(pool):
                if jb["dram"] is not None:
                    pool.wait_ge(evac, g * PER + 3 * PER)
                    pool.dma_start(rows(jb["dram"], t, jb["width"]),
                                   stage[0:jb["width"], j, 0:jb["n_tok"]]).then_inc(stored, 16)
                    pool.wait_ge(stored, s * 16 + 16 + before)
                    pool.sem_inc(stage_free, 1)


def split(C, src, hi, lo):
    nc = C.nc
    r_hi = C.sem("r_hi")
    with C.block() as block:
        @block.scalar
        def _(act):
            for k in range(src.shape[1]):
                nc.scalar.activation(hi[:, k, :], src[:, k, :], ACT.Copy).then_inc(r_hi, 1)

        @block.vector
        def _(dve):
            for k in range(src.shape[1]):
                dve.wait_ge(r_hi, k + 1)
                nc.vector.tensor_tensor(lo[:, k, :], src[:, k, :], hi[:, k, :].bitcast(F32), ALU.subtract)


def linear_tok(C, src, w, n_cols, kt, tok_tiles, w_slot, dram, w_view=None, row=lambda t: t):
    nc = C.nc
    pieces = chunks(n_cols)
    NN = len(pieces)
    wb = C.slot(w_slot, kt, n_cols)
    stage = C.slot(w_slot, 2, n_cols, at=kt * n_cols)
    w_ready, done, evac = (C.sem(n) for n in ("w_ready", "done", "evac"))
    stored = C.pair("stored")
    n_w = kt if w_view is not None else 1
    with C.block() as block:
        @block.sync
        def _(sp):
            if w_view is None:
                sp.dma_start(wb, w.rearrange("(k p) n -> p k n", p=P)).then_inc(w_ready, 16)
            else:
                for k in range(kt):
                    sp.dma_start(w_view(wb[:, k, :]), w(k)).then_inc(w_ready, 16)
            for t in range(tok_tiles):
                sp.wait_ge(evac, NN * (t + 1))
                sp.dma_start(rows(dram, row(t)), stage[:, t % 2, :]).then_inc(stored[t % 2], 16)
            for j in range(2):
                sp.wait_ge(stored[j], 8 * tok_tiles)

        @block.tensor
        def _(pe):
            pe.wait_ge(w_ready, 16 * n_w)
            for t in range(tok_tiles):
                for c, (a, n) in enumerate(pieces):
                    if t >= 2:
                        pe.wait_ge(evac, NN * (t - 2) + c + 1)
                    for k in range(kt):
                        mm = pe.matmul(C.psum[:, (t % 2) * NN + c, 0:n], src[:, k, t * P:(t + 1) * P],
                                       wb[:, k, a:a + n], start=(k == 0), stop=(k == kt - 1))
                    mm.then_inc(done, 1)
            pe.wait_ge(evac, NN * tok_tiles)

        @block.scalar
        def _(act):
            for t in range(tok_tiles):
                if t >= 2:
                    act.wait_ge(stored[t % 2], 16 * (t // 2))
                for c, (a, n) in enumerate(pieces):
                    act.wait_ge(done, NN * t + c + 1)
                    nc.scalar.activation(stage[:, t % 2, a:a + n], C.psum[:, (t % 2) * NN + c, 0:n],
                                         ACT.Copy).then_inc(evac, 1)


def rotate(C, src, dst, n, width, n_tok, mat, cos, sin, slot, dst_rows=None):
    nc = C.nc
    pieces = chunks(n_tok)
    NN = len(pieces)
    x = C.slot(slot, 2, n_tok, parts=width)
    y = C.slot(slot, 2, n_tok, at=2 * n_tok, parts=width)
    z = C.slot(slot, 2, n_tok, at=4 * n_tok, parts=width)
    done, seq, out_free = (C.sem(n) for n in ("done", "seq", "out_free"))
    stored, before = C.storing(n)
    x_ready = C.pair("x_ready")
    out = dst_rows or (lambda t: rows(dst, t, width))
    with C.block() as block:
        @block.sync
        def _(sp):
            for t, j, r in turns(sp, n):
                sp.wait_ge(seq, t * 3 * NN + 3 * NN)
                sp.dma_start(x[:, j], rows(src, t, width)).then_inc(x_ready[j], 16)

        @block.gpsimd
        def _(pool):
            for t, j, r in turns(pool, n):
                pool.wait_ge(seq, t * 3 * NN + 9 * NN)
                pool.dma_start(out(t), z[:, j]).then_inc(stored, 16)
                pool.wait_ge(stored, t * 16 + 16 + before)
                pool.sem_inc(out_free, 1)

        @block.tensor
        def _(pe):
            for t, j, r in turns(pe, n):
                pe.wait_ge(x_ready[j], (r + 1) * 16)
                pe.wait_ge(seq, t * 3 * NN + 3 * NN)
                for c, (a, m) in enumerate(pieces):
                    pe.matmul(C.psum[0:width, j * NN + c, 0:m], mat, x[:, j, a:a + m], start=True,
                              stop=True).then_inc(done, 1)
            pe.wait_ge(seq, n * 3 * NN + 6 * NN)

        @block.vector
        def _(dve):
            dve.sem_inc(seq, 6 * NN)
            dve.sem_inc(out_free, 2)
            for t, j, r in turns(dve, n):
                dve.wait_ge(out_free, t + 1)
                for c, (a, m) in enumerate(pieces):
                    base = t * 3 * NN + 3 * c + 6 * NN
                    dve.wait_ge(x_ready[j], (r + 1) * 16)
                    nc.vector.tensor_tensor(y[:, j, a:a + m], x[:, j, a:a + m], cos[:, a:a + m],
                                            ALU.mult).then_inc(seq, 1)
                    dve.wait_ge(done, t * NN + c + 1)
                    nc.vector.tensor_tensor(z[:, j, a:a + m], C.psum[0:width, j * NN + c, 0:m], sin[:, a:a + m],
                                            ALU.mult).then_inc(seq, 1)
                    dve.wait_ge(seq, base + 2)
                    nc.vector.tensor_tensor(z[:, j, a:a + m], z[:, j, a:a + m], y[:, j, a:a + m],
                                            ALU.add).then_inc(seq, 1)


def attention(C, n_turns, units, load, n_loads, store, scale, setup_loads=None, n_setup=0, sink=False,
              masked=False):
    nc = C.nc
    U = len(units(0))
    groups = [[(a, min(4, len(u["v"]) - a)) for a in range(0, len(u["v"]), 4)] for u in units(0)]
    first = [sum(len(x) for x in groups[:u]) for u in range(U)]
    GT = sum(len(x) for x in groups)
    assert U % 2 == 0 and GT % 2 == 0 and n_turns % 2 == 0
    prob = C.slot(5, 2, 1024)
    probT = C.slot(5, 2, 1024, at=2048)
    st = C.slot(5, 5, 2, 8, at=4096)
    names = ("fixed", "scores", "hidden", "maxed", "negmax", "exped", "probs", "turned", "tcopied", "pv", "den",
             "rden", "evac", "out_free")
    (fixed, scores, hidden, maxed, negmax, exped, probs, turned, tcopied, pv, den, rden, evac,
     out_free) = (C.sem(n) for n in names)
    loaded = C.pair("loaded")
    stored, before = C.storing(n_turns)

    def ps(u, n):
        return C.psum[:, 2 * (u % 2):2 * (u % 2) + 2, :].rearrange("p a b -> p (a b)")[:, 0:n]

    def unit_steps(eng):
        def ahead(t, j, r, u, last):
            def at(k):
                if u + k < 0:
                    return None
                if u + k < U:
                    return t, j, r, u + k
                return None if last else (t + 1, 1 - j, r + j, u + k - U)
            return at

        for u in (-2, -1):
            yield ahead(0, 0, 0, u, False)
        with eng.Fori(0, n_turns // 2 - 1) as i:
            for j in range(2):
                for u in range(U):
                    yield ahead(i * 2 + j, j, i, u, False)
        for j in range(2):
            for u in range(U):
                yield ahead(n_turns - 2 + j, j, n_turns // 2 - 1, u, j == 1)

    with C.block() as block:
        @block.sync
        def _(sp):
            if setup_loads:
                setup_loads(sp, fixed)
            for t, j, r in turns(sp, n_turns):
                sp.wait_ge(pv, t * U + U)
                load(sp, t, j, loaded[j])

        @block.gpsimd
        def _(pool):
            for t, j, r in turns(pool, n_turns):
                pool.wait_ge(evac, t * U + U + 2)
                store(pool, t, j).then_inc(stored, 16)
                pool.wait_ge(stored, t * 16 + 16 + before)
                pool.sem_inc(out_free, 1)

        @block.tensor
        def _(pe):
            pe.sem_inc(pv, 2 * U)
            if n_setup:
                pe.wait_ge(fixed, 16 * n_setup)

            def turn(t, j, r, u):
                pe.wait_ge(probs, t * U + u + 1)
                for g, (a, n) in enumerate(groups[u]):
                    G = first[u] + g
                    pe.wait_ge(tcopied, t * GT + G + 1)
                    for x in range(n):
                        mm = pe.transpose(C.psum[:, 4 + G % 2, x * P:(x + 1) * P],
                                          prob[:, u % 2, (a + x) * P:(a + x + 1) * P], C.mat("ident"))
                    mm.then_inc(turned, 1)

            def score(t, j, r, u):
                if u == 0:
                    pe.wait_ge(loaded[j], r * 16 * n_loads + 16 * n_loads)
                pe.wait_ge(exped, t * U + u + 1)
                unit = units(j)[u]
                for k, at in unit["k"]:
                    mm = pe.matmul(ps(u, 1024)[:, at:at + k.shape[-1]], unit["q"], k, start=True, stop=True)
                mm.then_inc(scores, 1)

            def values(t, j, r, u):
                unit = units(j)[u]
                n, r0 = len(unit["v"]), unit["at"]
                pe.wait_ge(tcopied, t * GT + first[u] + len(groups[u]) + 2)
                pe.wait_ge(evac, t * U + u + 1)
                for x, v in enumerate(unit["v"]):
                    mm = pe.matmul(C.psum[r0:r0 + HD, 6 + u % 2, 0:P], v, probT[:, u % 2, x * P:(x + 1) * P],
                                   start=(x == 0), stop=(x == n - 1))
                mm.then_inc(pv, 1)

            for at in unit_steps(pe):
                if at(0):
                    turn(*at(0))
                if at(2):
                    score(*at(2))
                if at(0):
                    values(*at(0))

        @block.vector
        def _(dve):
            dve.sem_inc(evac, 2)
            dve.sem_inc(out_free, 2)

            def largest(t, j, r, u):
                g, unit = t * U + u, units(j)[u]
                n = unit["n"]
                dve.wait_ge(scores, g + 1)
                if masked:
                    m, at, w = unit["mask"]
                    nc.vector.tensor_tensor(ps(u, 1024)[:, at:at + w], ps(u, 1024)[:, at:at + w], m,
                                            ALU.add).then_inc(hidden, 1)
                    dve.wait_ge(hidden, g + 1)
                nc.vector.reduce_max(st[:, 0, j, u:u + 1], ps(u, n), AX_X).then_inc(maxed, 1)
                dve.wait_ge(maxed, g + 1)
                if sink:
                    h = unit["sink"]
                    nc.vector.tensor_scalar(st[:, 1, j, u:u + 1], st[:, 0, j, u:u + 1], -scale,
                                            C.small[:, 8 + h:9 + h], ALU.mult, ALU.min).then_inc(negmax, 1)
                else:
                    nc.vector.tensor_scalar(st[:, 1, j, u:u + 1], st[:, 0, j, u:u + 1], -scale, None,
                                            ALU.mult).then_inc(negmax, 1)

            def divide(t, j, r, u):
                g, unit = t * U + u, units(j)[u]
                dve.wait_ge(exped, g + 3)
                total = st[:, 2, j, u:u + 1]
                if sink:
                    nc.vector.tensor_tensor(st[:, 3, j, u:u + 1], total, st[:, 3, j, u:u + 1],
                                            ALU.add).then_inc(den, 1)
                    dve.wait_ge(den, g + 1)
                    total = st[:, 3, j, u:u + 1]
                nc.vector.reciprocal(st[:, 4, j, u:u + 1], total).then_inc(rden, 1)
                dve.wait_ge(rden, g + 1)
                p = prob[:, u % 2, 0:unit["n"]]
                nc.vector.tensor_scalar(p, p, st[:, 4, j, u:u + 1], None, ALU.mult).then_inc(probs, 1)

            def leave(t, j, r, u):
                if u == 0:
                    dve.wait_ge(out_free, t + 1)
                unit = units(j)[u]
                dve.wait_ge(pv, t * U + u + 1 + 2 * U)
                r0 = unit["at"]
                nc.vector.tensor_copy(unit["out"], C.psum[r0:r0 + HD, 6 + u % 2, 0:P]).then_inc(evac, 1)

            for at in unit_steps(dve):
                if at(1):
                    divide(*at(1))
                if at(2):
                    largest(*at(2))
                if at(0):
                    leave(*at(0))

        @block.scalar
        def _(act):
            act.sem_inc(exped, 2)
            act.sem_inc(tcopied, 2)

            def expo(t, j, r, u):
                act.wait_ge(negmax, t * U + u + 1)
                nm, unit = st[:, 1, j, u:u + 1], units(j)[u]
                if sink:
                    h = unit["sink"]
                    nc.scalar.activation(st[:, 3, j, u:u + 1], C.small[:, h:h + 1], ACT.Exp, bias=nm)
                n = unit["n"]
                nc.scalar.activation(prob[:, u % 2, 0:n], ps(u, n), ACT.Exp, bias=nm, scale=scale,
                                     accum_out=st[:, 2, j, u:u + 1]).then_inc(exped, 1)

            def copy(t, j, r, u):
                for g, (a, n) in enumerate(groups[u]):
                    G = first[u] + g
                    act.wait_ge(turned, t * GT + G + 1)
                    nc.scalar.activation(probT[:, u % 2, a * P:(a + n) * P], C.psum[:, 4 + G % 2, 0:n * P],
                                         ACT.Copy).then_inc(tcopied, 1)

            for at in unit_steps(act):
                if at(0):
                    copy(*at(0))
                if at(1):
                    expo(*at(1))


KP = CT + P + T + P


def window_attention(C, qr, kr, vt, ya):
    nc = C.nc
    q = C.slot(3, 2, 4, P)
    kl = C.slot(3, 2, NKV, 3 * P, at=1024)
    kc = C.slot(3, NKV, CT, at=1024 + 1536)
    vl = C.slot(3, 2, 3, P, at=1024 + 1536 + 512)
    vc = C.slot(3, 2, P, at=1024 + 1536 + 512 + 768)
    mask = C.slot(3, 2, 3 * P, at=4096)
    out = C.slot(3, 2, 4, P, at=4096 + 768)

    def setup_loads(sp, loaded):
        for g in range(NKV):
            for e in range(2):
                sp.dma_start(kc[64 * e:64 * e + 64, g, :], kr[64 * g:64 * g + 64, 0:CT]).then_inc(loaded, 16)
        sp.dma_start(vc, vt[0:CT, :].rearrange("(a p) n -> p a n", p=P)).then_inc(loaded, 16)

    def load(sp, t, j, loaded):
        sp.dma_start(q[:, j], qr[:, bass.ds(t * P, P)].rearrange("(a p) n -> p a n", p=P)).then_inc(loaded, 16)
        for g in range(NKV):
            for e in range(2):
                sp.dma_start(kl[64 * e:64 * e + 64, j, g, :],
                             kr[64 * g:64 * g + 64, bass.ds(t * P + CT, 3 * P)]).then_inc(loaded, 16)
        sp.dma_start(vl[:, j], vt[bass.ds(t * P + CT, 3 * P), :].rearrange("(a p) n -> p a n", p=P))\
            .then_inc(loaded, 16)
        sp.dma_start(mask[:, j, :], C.ins["k_band"][bass.ds(t, 1), :, :].rearrange("o p n -> (o p) n"))\
            .then_inc(loaded, 16)

    def units(j):
        us = []
        for h in range(NQ):
            g, e = h // (NQ // NKV), h % 2
            r = slice(64 * e, 64 * e + 64)
            us.append(dict(q=q[r, j, h // 2, :], n=5 * P, sink=h, mask=(mask[:, j, :], 0, 3 * P),
                           k=[(kl[r, j, g, :], 0), (kc[r, g, 0:P], 3 * P), (kc[r, g, P:CT], 4 * P)],
                           v=[vl[:, j, x, HD * g:HD * g + HD] for x in range(3)]
                           + [vc[:, x, HD * g:HD * g + HD] for x in range(2)],
                           out=out[r, j, h // 2, :], at=64 * e))
        return us

    attention(C, T // P, units, load, 7,
              lambda e, t, j: e.dma_start(ya[:, bass.ds(t * P, P)].rearrange("(a p) n -> p a n", p=P), out[:, j]),
              float(HD) ** -0.5, setup_loads, 5, sink=True, masked=True)


def latent_attention(C, qr, kn, krope, vt, tok):
    q = C.slot(3, 2, T, parts=QKD)
    k = C.slot(3, 2, T, at=2 * T, parts=QKD)
    v = C.slot(3, 2, T // P, HD, at=4 * T)
    out = C.slot(3, 2, T, at=5 * T, parts=HD)

    def load(sp, t, j, loaded):
        sp.dma_start(q[:, j, :], rows(qr, t, QKD)).then_inc(loaded, 16)
        sp.dma_start(k[0:QKN, j, :], rows(kn, t, QKN)).then_inc(loaded, 16)
        sp.dma_start(k[QKN:QKD, j, :], krope).then_inc(loaded, 16)
        sp.dma_start(v[:, j], vt[:, bass.ds(t * HD, HD)].rearrange("(a p) n -> p a n", p=P)).then_inc(loaded, 16)

    def units(j):
        us = []
        for b in range(T // P):
            n = (b + 1) * P
            us.append(dict(q=q[:, j, b * P:(b + 1) * P], n=n, mask=(C.mat("causal"), b * P, P),
                           k=[(k[:, j, a:a + w], a) for a, w in chunks(n)],
                           v=[v[:, j, x, :] for x in range(b + 1)], out=out[:, j, b * P:(b + 1) * P], at=0))
        return us

    attention(C, TH, units, load, 4,
              lambda e, t, j: e.dma_start(rows(tok, t, HD), out[:, j]),
              float(QKD) ** -0.5, masked=True)


def memory_attention(C, qm, km, vm, mem_out):
    q = C.slot(3, 2, 2, P)
    k = C.slot(3, 2, 256, at=512)
    v = C.slot(3, 2, 256, at=1024)
    out = C.slot(3, 2, 2, P, at=1536)

    def setup_loads(sp, loaded):
        sp.dma_start(k, km.rearrange("(a p) n -> p a n", p=P)).then_inc(loaded, 16)
        sp.dma_start(v, vm.rearrange("(a p) n -> p a n", p=P)).then_inc(loaded, 16)

    def load(sp, t, j, loaded):
        sp.dma_start(q[:, j], qm[:, bass.ds(t * P, P)].rearrange("(a p) n -> p a n", p=P)).then_inc(loaded, 16)

    def units(j):
        return [dict(q=q[64 * (h % 2):64 * (h % 2) + 64, j, h // 2, :], n=256,
                     k=[(k[64 * (h % 2):64 * (h % 2) + 64, h // 2, :], 0)],
                     v=[v[:, x, HD * h:HD * h + HD] for x in range(2)],
                     out=out[64 * (h % 2):64 * (h % 2) + 64, j, h // 2, :], at=64 * (h % 2))
                for h in range(MH)]

    attention(C, T // P, units, load, 1, lambda e, t, j: e.dma_start(
        mem_out[:, bass.ds(t * P, P)].rearrange("(a p) n -> p a n", p=P), out[:, j]),
              float(HD) ** -0.5, setup_loads, 2)


KAPPA = float(np.exp(-0.5))
NCH = ALL // CH
CC = CT // CH
SEGS = [(0, CT), (CT, T)]


def rwkv_prepare(C, rw, chunked, v_chunked, bonus, gate_in):
    nc, ins = C.nc, C.ins
    W, W4 = ALL, ALL + 4
    places = iter(range(0, 5 * SLOT, ALL + 8))

    def tile(parts=P):
        return C.slot(1, 1, W, at=next(places), parts=parts)[:, 0, :]

    raw = [C.slot(1, 1, W4, at=next(places))[:, 0, :] for _ in range(3)]
    cv = [tile() for _ in range(3)]
    kraw, rn, kk, sg, cum, w, y, e1, e2, e3, a, b = (tile() for _ in range(12))
    kd = [tile(), tile()]
    outs = [[tile() for _ in range(4)] for _ in range(2)]
    tail, starts = tile(64), tile()
    used = next(places)
    w2 = C.slot(1, 2, RW, at=used, parts=64)
    gate = e1
    r_, k_, v_ = cv
    sqk = y
    (padded, dstep, astep, pstep, wload, gate_out) = (
        C.sem(n) for n in ("padded", "dstep", "astep", "pstep", "wload", "gate_out"))
    loaded = [C.sem(f"loaded{x}") for x in range(3)]

    TAIL = [f"t{x}{s}{k}" for x in range(2) for s in range(2) for k in range(3)] + ["omka"]
    convs = [[f"c{x}{s}{k}" for s in range(2) for k in range(3)] for x in range(3)]
    DV = convs[0] + convs[1] + ["kraw"] + convs[2] + ["kmax", "krec", "kk"]
    for d in range(2):
        DV += [f"{n}{d}" for n in ("scan", "ct", "cc", "w", "y", "b", "am", "kd")] + ["ksum", "bon"] * d + \
              [f"{n}{d}" for n in ("A", "R", "B", "K")]
    DV += ["bonus"]
    AC = ["sg0", "sq", "sqrt", "a0", "e10", "e20", "e30", "sg1", "a1", "e11", "e21", "e31"]
    PEV = ["z0", "kk", "a0", "z1", "a1", "bon"]
    STORES = 10
    stored, before = C.storing(STORES * PAIRS)

    def dv(q, name):
        return len(TAIL) + q * len(DV) + DV.index(name) + 1

    def ac(q, name):
        return 2 + q * len(AC) + AC.index(name) + 1

    def pv(q, name):
        return q * len(PEV) + PEV.index(name) + 1

    def by_chunk(x):
        return x.rearrange("p (c n) -> p c n", n=CH)

    def bank(first, n=W):
        return C.psum[:, first:first + 3, :].rearrange("p a b -> p (a b)")[:, 0:n]

    with C.block() as block:
        @block.gpsimd
        def _(pool):
            for x in range(3):
                nc.gpsimd.memset(raw[x], 0.0).then_inc(padded, 1)
            for q in range(PAIRS):
                pool.wait_ge(dstep, dv(q, "c212"))
                pool.dma_start(v_chunked[:, :, q, :].rearrange("c p n -> p c n"), by_chunk(v_)).then_inc(stored, 16)
                for d in range(2):
                    for x, n in enumerate(("A", "R", "B", "K")):
                        pool.wait_ge(dstep, dv(q, f"{n}{d}"))
                        pool.dma_start(chunked[d, :, :, x, q, :].rearrange("c p n -> p c n"),
                                       by_chunk(outs[d][x])).then_inc(stored, 16)
                pool.wait_ge(dstep, dv(q, "bonus"))
                pool.dma_start(rows(bonus, q), rn[:, CT:W]).then_inc(stored, 16)
            pool.wait_ge(stored, 16 * STORES * PAIRS + before)

        @block.sync
        def _(sp):
            sp.dma_start(starts, ins["k_starts"]).then_inc(wload, 16)
            for d in range(2):
                sp.dma_start(w2[0:32, d, :], ins["decay_w2"][0, d, :, :]).then_inc(wload, 16)
                sp.dma_start(w2[32:64, d, :], ins["iclr_a2"][0, d, :, :]).then_inc(wload, 16)
            sp.wait_ge(padded, 3)
            for x, (r0, n) in enumerate([(3 * RW, 64), (3 * RW + 64, GL)]):
                for s, (a0, m) in enumerate(SEGS):
                    sp.dma_start(raw[x][0:n, a0 + 1 + s:a0 + 1 + s + m], rw[r0:r0 + n, a0:a0 + m])\
                      .then_inc(loaded[x], 16)
            for q in range(PAIRS):
                for x in range(3):
                    sp.wait_ge(dstep, len(TAIL) - 1 if q == 0 else dv(q - 1, f"c{x}12"))
                    for s, (a0, m) in enumerate(SEGS):
                        r0 = x * RW + q * P
                        sp.dma_start(raw[x][:, a0 + 1 + s:a0 + 1 + s + m], rw[r0:r0 + P, a0:a0 + m])\
                          .then_inc(loaded[x], 16)

        def conv(dve, x, s, k, src, dst, row, parts, step):
            a0, m = SEGS[s]
            i = src[0:parts, a0 + s + k:a0 + s + k + m]
            o = dst[0:parts, a0:a0 + m]
            c = C.par(f"conv{k}", row, parts)
            if step > 1:
                dve.wait_ge(dstep, step - 1)
            if k == 0:
                nc.vector.tensor_scalar(o, i, c, None, ALU.mult).then_inc(dstep, 1)
            else:
                nc.vector.scalar_tensor_tensor(o, i, c, o, ALU.mult, ALU.add).then_inc(dstep, 1)

        @block.vector
        def _(dve):
            n = 0
            for x in range(2):
                dve.wait_ge(loaded[x], 32)
                for s in range(2):
                    for k in range(3):
                        n += 1
                        conv(dve, x, s, k, raw[x], (tail, gate)[x], 12 + x, (64, GL)[x], n)
            nc.vector.tensor_scalar(C.omka[:, :], C.params[:, PARAM_ROWS["k_a"]:PARAM_ROWS["k_a"] + PAIRS], -1.0, 1.0,
                                    ALU.mult, ALU.add).then_inc(dstep, 1)
            dve.wait_ge(wload, 80)
            for q in range(PAIRS):
                def step(name, f, *args):
                    dve.wait_ge(dstep, dv(q, name) - 1)
                    f(*args).then_inc(dstep, 1)

                tt, ts, stt = nc.vector.tensor_tensor, nc.vector.tensor_scalar, nc.vector.scalar_tensor_tensor
                for x in range(3):
                    if x == 2:
                        step("kraw", ts, kraw, k_, C.par("k_k", q), None, ALU.mult)
                        if q > 0:
                            dve.wait_ge(stored, 16 * STORES * q + before)
                    dve.wait_ge(loaded[x], 32 * (q + 1) + (32 if x < 2 else 0))
                    for s in range(2):
                        for k in range(3):
                            conv(dve, x, s, k, raw[x], cv[x], 4 * x + q, P, dv(q, f"c{x}{s}{k}"))
                dve.wait_ge(pstep, pv(q, "kk"))
                step("kmax", ts, rn, bank(0), 1e-24, None, ALU.max)
                step("krec", nc.vector.reciprocal, rn, rn)
                dve.wait_ge(astep, ac(q, "sqrt"))
                step("kk", tt, kk, kraw, rn, ALU.mult)
                for d in range(2):
                    cumc, wc = by_chunk(cum), by_chunk(w)
                    dve.wait_ge(astep, ac(q, f"sg{d}"))
                    step(f"scan{d}", nc.vector.tensor_tensor_scan, cum, starts, sg, 0.0, ALU.mult, ALU.add)
                    step(f"ct{d}", nc.vector.tensor_copy, C.ends[:, 0, d, q, :], cumc[:, :, CH - 1])
                    step(f"cc{d}", nc.vector.tensor_copy, C.ends[:, 1, d, q, :], cumc[:, :, CH // 2 - 1])
                    step(f"w{d}", tt, wc, cumc, cumc[:, :, CH // 2 - 1:CH // 2].broadcast_to([P, NCH, CH]),
                         ALU.subtract)
                    step(f"y{d}", tt, y, w, sg, ALU.subtract)
                    dve.wait_ge(astep, ac(q, f"a{d}"))
                    step(f"b{d}", tt, b, kk, a, ALU.mult)
                    step(f"am{d}", ts, kd[d], a, C.par("k_a", q), C.omka[:, q:q + 1], ALU.mult, ALU.add)
                    step(f"kd{d}", tt, kd[d], kd[d], k_, ALU.mult)
                    if d == 1:
                        step("ksum", tt, kd[0][:, CT:W], kd[0][:, CT:W], kd[1][:, CT:W], ALU.add)
                        step("bon", stt, kd[0][:, CT:W], r_[:, CT:W], C.par("r_k", q), kd[0][:, CT:W], ALU.mult,
                             ALU.mult)
                    dve.wait_ge(astep, ac(q, f"e3{d}"))
                    eA, eR, eB = (e3, e2, e1) if d == 0 else (e1, e2, e3)
                    step(f"A{d}", tt, outs[d][0], kk, eA, ALU.mult)
                    step(f"R{d}", tt, outs[d][1], r_, eR, ALU.mult)
                    step(f"B{d}", tt, outs[d][2], b, eB, ALU.mult)
                    step(f"K{d}", tt, outs[d][3], kd[d], eB, ALU.mult)
                dve.wait_ge(pstep, pv(q, "bon"))
                step("bonus", tt, rn[:, CT:W], bank(0, T), v_[:, CT:W], ALU.mult)
            E, tot, mid = C.decay, C.ends[:, 0], C.ends[:, 1]
            last = dv(PAIRS - 1, "bonus")
            dve.wait_ge(dstep, last)
            nc.vector.memset(E[:, :, :, :], 0.0).then_inc(dstep, 1)
            nc.vector.tensor_tensor(tot, tot, mid, ALU.subtract).then_inc(dstep, 1)
            dve.wait_ge(dstep, last + 2)
            nc.vector.tensor_tensor(E[:, 0, :, 0:NCH - 1], tot[:, 0, :, 0:NCH - 1], mid[:, 0, :, 1:NCH], ALU.add)\
              .then_inc(dstep, 1)
            nc.vector.tensor_tensor(E[:, 1, :, 1:NCH], tot[:, 1, :, 0:NCH - 1], mid[:, 1, :, 1:NCH], ALU.add)\
              .then_inc(dstep, 1)
            nc.vector.tensor_tensor(E[:, 1, :, 0:1], tot[:, 1, :, NCH - 1:NCH], mid[:, 1, :, 0:1], ALU.add)\
              .then_inc(dstep, 1)

        @block.scalar
        def _(act):
            act.wait_ge(dstep, 6)
            nc.scalar.activation(tail[0:32, :], tail[0:32, :], ACT.Tanh).then_inc(astep, 1)
            act.wait_ge(dstep, 12)
            nc.scalar.activation(gate[0:GL, :], gate[0:GL, :], ACT.Sigmoid).then_inc(astep, 1)
            act.wait_ge(astep, 2)
            act.dma_start(gate_in, gate[0:GL, CT:W]).then_inc(gate_out, 16)
            act.wait_ge(gate_out, 16)
            def decays(q, d):
                act.wait_ge(pstep, pv(q, f"z{d}"))
                if d == 1 or q > 0:
                    act.wait_ge(dstep, dv(q, "y0") if d else dv(q - 1, "y1"))
                nc.scalar.activation(sg, bank(3), ACT.Sigmoid, bias=C.par("decay_w0", 4 * d + q)).then_inc(astep, 1)

            for q in range(PAIRS):
                decays(q, 0)
                act.wait_ge(dstep, dv(q, "kraw"))
                nc.scalar.activation(sqk, kraw, ACT.Square).then_inc(astep, 1)
                act.wait_ge(dstep, dv(q, "krec"))
                nc.scalar.activation(rn, rn, ACT.Sqrt).then_inc(astep, 1)
                for d in range(2):
                    if d == 1:
                        decays(q, 1)
                    act.wait_ge(pstep, pv(q, f"a{d}"))
                    if d == 1:
                        act.wait_ge(dstep, dv(q, "kd0"))
                    nc.scalar.activation(a, bank(0), ACT.Sigmoid, bias=C.par("iclr_a0", 4 * d + q)).then_inc(astep, 1)
                    act.wait_ge(dstep, dv(q, "K0") if d else dv(q, "y0"))
                    act.wait_ge(dstep, dv(q, f"y{d}"))
                    nc.scalar.activation(e1, w, ACT.Exp, scale=KAPPA).then_inc(astep, 1)
                    nc.scalar.activation(e2, y if d else w, ACT.Exp, scale=KAPPA if d else -KAPPA).then_inc(astep, 1)
                    nc.scalar.activation(e3, y, ACT.Exp, scale=-KAPPA).then_inc(astep, 1)
            act.wait_ge(dstep, dv(PAIRS - 1, "bonus") + 5)
            nc.scalar.activation(C.decay[:, :, :, :], C.decay[:, :, :, :], ACT.Exp, scale=-KAPPA)

        @block.tensor
        def _(pe):
            def product(first, lhsT, rhs, a0=0, n=W):
                for c, (a, m) in enumerate(chunks(n)):
                    mm = pe.matmul(C.psum[:, first + c, 0:m], lhsT, rhs[:, a0 + a:a0 + a + m], start=True, stop=True)
                mm.then_inc(pstep, 1)

            pe.wait_ge(wload, 80)
            for q in range(PAIRS):
                cols = slice(q * P, (q + 1) * P)
                pe.wait_ge(astep, ac(q - 1, "sg1") if q > 0 else 1)
                product(3, w2[0:32, 0, cols], tail[0:32, :])
                if q > 0:
                    pe.wait_ge(dstep, dv(q - 1, "bonus"))
                pe.wait_ge(astep, ac(q, "sq"))
                product(0, C.mat("headsum"), sqk)
                for d in range(2):
                    if d == 1:
                        pe.wait_ge(astep, ac(q, "sg0"))
                        product(3, w2[0:32, d, cols], tail[0:32, :])
                    pe.wait_ge(dstep, dv(q, "kmax"))
                    if d == 1:
                        pe.wait_ge(astep, ac(q, "a0"))
                    product(0, w2[32:64, d, cols], tail[32:64, :])
                pe.wait_ge(astep, ac(q, "a1"))
                pe.wait_ge(dstep, dv(q, "bon"))
                product(0, C.mat("headsum"), kd[0], CT, T)


def recurrence(C, chunked, v_chunked, yT):
    nc, ins = C.nc, C.ins
    NU = 2 * 2 * PAIRS
    at = [0]

    def tile(*shape):
        v = C.slot(1, *shape, at=at[0])
        at[0] += int(np.prod(shape))
        return v

    factors = tile(2, 2, 4 * PAIRS, CH)
    vals = tile(2, 2, PAIRS, CH)
    prods = tile(NU, 2, 2 * CH)
    XX = tile(NU, 2, CH)
    Wt = tile(NU, CH)
    toks = tile(3, 2, PAIRS, CH)
    W0s = tile(2, 2, PAIRS, HD)
    Us = tile(2, 2 * PAIRS, HD)
    S = tile(2, PAIRS, HD)
    corner = tile(2, LEVELS + 1, CH)
    keep_f = tile(2, 2 * CH)
    assert at[0] <= 4 * SLOT, at[0]
    keep = keep_f.bitcast(I32)
    names = ("consts", "cleared", "tok_turned", "tok_copied", "prod", "kept", "mprod", "m_used", "first",
             "xx", "w_ok", "zprod", "wprod", "w0p", "w0c", "up", "uc", "yp", "y_copied", "s_done", "s_new", "s_sum")
    (consts, cleared, tok_turned, tok_copied, prod, kept, mprod, m_used, first, xx, w_ok, zprod, wprod,
     w0p, w0c, up, uc, yp, y_copied, s_done, s_new, s_sum) = (C.sem(n) for n in names)
    loaded = C.pair("loaded")
    turn = C.sem("turn")
    NG = 4
    XL = (LEVELS + 1) * NG
    WL = LEVELS * NG

    def steps(eng):
        for s in range(CC):
            yield s, s, CC - 1 - s, s % 2, s // 2, None
        with eng.Fori(0, (NCH - CC) // 2) as i:
            for j in range(2):
                yield i * 2 + (j + CC), i * 2 + (j + CC), i * (-2) + (NCH - 1 - j), j, i + CC // 2, i * 2 + j

    def heads(d):
        for e in range(2):
            for q in range(PAIRS):
                yield 2 * q + e, 8 * d + 4 * e + q, q, slice(64 * e, 64 * e + 64)

    with C.block() as block:
        @block.gpsimd
        def _(pool):
            nc.gpsimd.memset(prods, 0.0).then_inc(cleared, 1)
            nc.gpsimd.memset(S, 0.0).then_inc(cleared, 1)

        @block.sync
        def _(sp):
            sp.dma_start(corner, ins["k_corner"].rearrange("p (a b c) -> p a b c", a=2, b=LEVELS + 1))\
              .then_inc(consts, 16)
            sp.dma_start(keep, ins["k_keep"].rearrange("d p n -> p d n")).then_inc(consts, 16)
            sp.sem_inc(s_done, 4)
            for s, fc, rc, j, m, _ in steps(sp):
                sp.wait_ge(s_done, s * 2 + 2)
                for d, c in enumerate((fc, rc)):
                    sp.dma_start(factors[:, j, d], chunked[d, bass.ds(c, 1), :, :, :, :]
                                 .rearrange("o p a q n -> (o p) (a q) n")).then_inc(loaded[j], 16)
                    sp.dma_start(vals[:, j, d], v_chunked[bass.ds(c, 1), :, :, :]
                                 .rearrange("o p q n -> (o p) q n")).then_inc(loaded[j], 16)

        @block.tensor
        def _(pe):
            for s, fc, rc, j, m, es in steps(pe):
                pe.wait_ge(loaded[j], (m + 1) * 64)
                n = 0
                for d in range(2):
                    for x in range(3):
                        pe.wait_ge(tok_copied, s * 6 + n + 1)
                        for q in range(PAIRS):
                            src = vals[:, j, d, q, :] if x == 2 else factors[:, j, d, (2 + x) * PAIRS + q, :]
                            mm = pe.transpose(C.psum[:, 6 + n % 2, q * CH:(q + 1) * CH], src, C.mat("ident"))
                        mm.then_inc(tok_turned, 1)
                        n += 1
                pe.wait_ge(s_new, s * 2 + 1)
                if es is not None:
                    pe.wait_ge(y_copied, es * 2 + 1)
                for d in range(2):
                    for h, u, q, r in heads(d):
                        pe.wait_ge(kept, s * NU + u + 1)
                        ar = factors[r, j, d, q:2 * PAIRS:PAIRS, :]
                        for x in range(2):
                            mm = pe.matmul(C.psum[:, u % 4, x * 2 * CH:(x + 1) * 2 * CH],
                                           factors[r, j, d, (2 + x) * PAIRS + q, :], ar, start=True, stop=True)
                        mm.then_inc(prod, 1)
                for g in range(NG):
                    pe.wait_ge(m_used, s * NG + g + 1)
                    for h, u, q, r in list(heads(g // 2))[4 * (g % 2):4 * (g % 2) + 4]:
                        mm = pe.matmul(C.psum[:, 4 + g % 2, (u % 4) * CH:(u % 4 + 1) * CH], factors[r, j, g // 2, q, :],
                                       factors[r, j, g // 2, 2 * PAIRS + q, :], start=True, stop=True)
                    mm.then_inc(mprod, 1)
                for lv in range(1, LEVELS + 1):
                    def corners(g):
                        pe.wait_ge(xx, s * XL + (lv - 1) * NG + g + 1)
                        pe.wait_ge(w_ok, s * WL + (lv - 1) * NG + g + 1)
                        for u in range(4 * g, 4 * g + 4):
                            mm = pe.matmul(C.psum[:, g % 2, (u % 4) * CH:(u % 4 + 1) * CH], prods[:, u, 0, 0:CH],
                                           XX[:, u, 0, :], start=True, stop=True)
                        mm.then_inc(wprod, 1)

                    def merge(g):
                        pe.wait_ge(w_ok, s * WL + (lv - 1) * NG + g + 3)
                        zb = C.psum[:, 2 + 2 * (g % 2):4 + 2 * (g % 2), :].rearrange("p a (b c) -> p (a b) c", c=CH)
                        for u in range(4 * g, 4 * g + 4):
                            if lv < LEVELS:
                                pe.matmul(zb[:, 2 * (u % 4), :], XX[:, u, 1, :], Wt[:, u, :], start=True, stop=True)
                            mm = pe.matmul(zb[:, 2 * (u % 4) + 1, :], Wt[:, u, :], XX[:, u, 1, :], start=True,
                                           stop=True)
                        mm.then_inc(zprod, 1)

                    for g in range(NG):
                        corners(g)
                        if g > 0:
                            merge(g - 1)
                    merge(NG - 1)
                pe.wait_ge(tok_copied, s * 6 + 8)
                pe.wait_ge(xx, s * XL + XL)
                for d in range(2):
                    for h, u, q, r in heads(d):
                        o = C.psum[:, 2 * d + h % 2, q * HD:(q + 1) * HD]
                        pe.matmul(o, factors[r, j, d, q, :], S[r, d, q, :], start=True, stop=False)
                        mm = pe.matmul(o, prods[:, u, 1, 0:CH],
                                       toks[:, 2, d, q, r.start:r.stop], start=False, stop=True)
                    mm.then_inc(w0p, 1)
                for d in range(2):
                    pe.wait_ge(w0c, s * 2 + d + 1)
                    for h, u, q, r in heads(d):
                        mm = pe.matmul(C.psum[:, 4 + d, h * HD:(h + 1) * HD], XX[:, u, 1, :], W0s[:, d, h % 2, q, :],
                                       start=True, stop=True)
                    mm.then_inc(up, 1)
                for d in range(2):
                    pe.wait_ge(uc, s * 2 + d + 1)
                    pe.sem_inc(turn, 1)
                    if es is not None:
                        for h, u, q, r in heads(d):
                            o = C.psum[r, d, q * CH:(q + 1) * CH]
                            pe.matmul(o, S[r, d, q, :], factors[r, j, d, PAIRS + q, :], start=True, stop=False)
                            pe.matmul(o, Us[:, d, h, :], prods[:, u, 0, CH:2 * CH], start=False, stop=False)
                            mm = pe.matmul(o, toks[:, 2, d, q, r.start:r.stop], prods[:, u, 1, CH:2 * CH],
                                           start=False, stop=True)
                        mm.then_inc(yp, 1)
                    for q in range(PAIRS):
                        o = C.psum[:, 2 + d, q * CH:(q + 1) * CH]
                        pe.matmul(o, toks[:, 0, d, q, :], Us[:, d, 2 * q:2 * q + 2, :].rearrange("p a b -> p (a b)"),
                                  start=True, stop=False)
                        mm = pe.matmul(o, toks[:, 1, d, q, :], toks[:, 2, d, q, :], start=False, stop=True)
                    mm.then_inc(s_done, 1)

        @block.scalar
        def _(act):
            act.sem_inc(tok_copied, 2)
            act.sem_inc(y_copied, 1)
            for s, fc, rc, j, m, es in steps(act):
                n = 0
                for d in range(2):
                    for x in range(3):
                        act.wait_ge(tok_turned, s * 6 + n + 1)
                        nc.scalar.activation(toks[:, x, d], C.psum[:, 6 + n % 2, :]
                                             .rearrange("p (q n) -> p q n", n=CH), ACT.Copy).then_inc(tok_copied, 1)
                        n += 1
                for d in range(2):
                    act.wait_ge(w0p, s * 2 + d + 1)
                    nc.scalar.activation(W0s[:, d], C.psum[:, 2 * d:2 * d + 2, 0:PAIRS * HD]
                                         .rearrange("p e (q v) -> p e q v", v=HD),
                                         ACT.Copy).then_inc(w0c, 1)
                for d in range(2):
                    act.wait_ge(up, s * 2 + d + 1)
                    nc.scalar.activation(Us[:, d], C.psum[:, 4 + d, :].rearrange("p (h v) -> p h v", v=HD),
                                         ACT.Copy, scale=-1.0).then_inc(uc, 1)
                if es is not None:
                    for d, c in enumerate((fc, rc)):
                        act.wait_ge(yp, es * 2 + d + 1)
                        nc.scalar.activation(yT[d][:, :, bass.ds((c - CC) * CH, CH)],
                                             C.psum[:, d, :].rearrange("p (q n) -> p q n", n=CH),
                                             ACT.Copy).then_inc(y_copied, 1)

        @block.vector
        def _(dve):
            dve.sem_inc(kept, 4)
            dve.sem_inc(m_used, 2)
            dve.sem_inc(w_ok, 2)
            dve.wait_ge(consts, 32)
            dve.wait_ge(cleared, 2)
            dve.sem_inc(s_new, 1)
            ident = C.mat("ident").unsqueeze(1).broadcast_to([P, 4, CH])
            for s, fc, rc, j, m, es in steps(dve):
                for u in range(NU):
                    dve.wait_ge(prod, s * NU + u + 1)
                    dve.sem_inc(turn, 1)
                    k2 = keep[:, u // 8, :].unsqueeze(1).broadcast_to([P, 2, 2 * CH])
                    nc.vector.copy_predicated(prods[:, u], k2, C.psum[:, u % 4, :]
                                              .rearrange("p (a b) -> p a b", a=2)).then_inc(kept, 1)
                for g in range(NG):
                    d, us = g // 2, slice(4 * g, 4 * g + 4)
                    c0 = corner[:, d, 0, :].unsqueeze(1).broadcast_to([P, 4, CH])
                    c0t = corner[:, 1 - d, 0, :].unsqueeze(1).broadcast_to([P, 4, CH])
                    dve.wait_ge(mprod, s * NG + g + 1)
                    nc.vector.tensor_tensor(XX[:, us, 0, :], C.psum[:, 4 + g % 2, :]
                                            .rearrange("p (a b) -> p a b", b=CH), c0, ALU.mult).then_inc(m_used, 1)
                    dve.wait_ge(kept, s * NU + 4 * g + 8)
                    nc.vector.tensor_tensor(XX[:, us, 1, :], prods[:, us, 0, 0:CH], c0t, ALU.mult).then_inc(first, 1)
                    dve.wait_ge(m_used, s * NG + g + 3)
                    nc.vector.tensor_tensor(XX[:, us, 0, :], ident, XX[:, us, 0, :], ALU.subtract).then_inc(first, 1)
                    dve.wait_ge(first, s * (2 * NG) + 2 * g + 1)
                    nc.vector.tensor_tensor(XX[:, us, 1, :], ident, XX[:, us, 1, :], ALU.subtract).then_inc(xx, 1)
                    dve.wait_ge(first, s * (2 * NG) + 2 * g + 2)
                for lv in range(1, LEVELS + 1):
                    def corners(g):
                        dve.wait_ge(wprod, s * WL + (lv - 1) * NG + g + 1)
                        c = corner[:, g // 2, lv, :].unsqueeze(1).broadcast_to([P, 4, CH])
                        nc.vector.tensor_tensor(Wt[:, 4 * g:4 * g + 4, :], C.psum[:, g % 2, :]
                                                .rearrange("p (a b) -> p a b", b=CH), c, ALU.mult).then_inc(w_ok, 1)

                    def merge(g):
                        dve.wait_ge(zprod, s * WL + (lv - 1) * NG + g + 1)
                        zb = C.psum[:, 2 + 2 * (g % 2):4 + 2 * (g % 2), :].rearrange("p a (b x c) -> p (a b) x c", x=2, c=CH)
                        us = slice(4 * g, 4 * g + 4)
                        x0 = 1 if lv == LEVELS else 0
                        dve.wait_ge(xx, s * XL + (lv - 1) * NG + g + 1)
                        nc.vector.tensor_tensor(XX[:, us, x0:2, :], XX[:, us, x0:2, :], zb[:, :, x0:2, :],
                                                ALU.subtract).then_inc(xx, 1)

                    for g in range(NG):
                        corners(g)
                        if g > 0:
                            merge(g - 1)
                    merge(NG - 1)
                for d, c in enumerate((fc, rc)):
                    dve.wait_ge(s_done, s * 2 + d + 1 + 4)
                    for e in range(2):
                        r = slice(64 * e, 64 * e + 64)
                        nc.vector.tensor_tensor(S[r, d], C.psum[r, 2 + d, :].rearrange("p (q n) -> p q n", n=CH)
                                                [:, :, 64 * e:64 * e + 64], S[r, d], ALU.add).then_inc(s_sum, 1)
                    dve.wait_ge(s_sum, s * 4 + 2 * d + 2)
                    dec = C.decay[:, d, :, bass.ds(c, 1)].broadcast_to([P, PAIRS, HD])
                    nc.vector.tensor_tensor(S[:, d], S[:, d], dec, ALU.mult).then_inc(s_new, 1)


def rwkv_output(C, yT, bonus, gate_in, out, slot):
    nc, ins = C.nc, C.ins
    g2 = C.slot(slot, 1, RW, parts=GL)[:, 0, :]
    sgate = C.slot(slot, 1, T, at=RW, parts=GL)[:, 0, :]
    bon = C.slot(slot, PAIRS, T, at=RW + T)
    sq = C.slot(slot + 1, 2, 512)
    rstd = C.slot(slot + 1, 2, 512, at=1024)
    loaded, dstep, astep, pstep = (C.sem(n) for n in ("loaded", "dstep", "astep", "pstep"))
    DV = ["sum", "center", "eps", "rec", "scale", "bias", "gate"]
    units = [(q, a) for q in range(PAIRS) for a in range(0, T, 512)]
    couples = [list(enumerate(units))[n:n + 2] for n in range(0, len(units), 2)]

    def dv(n, name):
        return n // 2 * 2 * len(DV) + 2 * DV.index(name) + n % 2 + 1

    def other(n, step):
        return n // 2 * 4 + 2 * step + n % 2 + 1

    with C.block() as block:
        @block.sync
        def _(sp):
            sp.dma_start(g2, ins["gate_g2"][0, :, :]).then_inc(loaded, 16)
            sp.dma_start(sgate, gate_in).then_inc(loaded, 16)
            sp.dma_start(bon, bonus.rearrange("(q p) n -> p q n", p=P)).then_inc(loaded, 16)

        @block.tensor
        def _(pe):
            pe.wait_ge(loaded, 48)
            for couple in couples:
                for n, (q, a) in couple:
                    pe.wait_ge(dstep, dv(n, "sum"))
                    pe.matmul(C.psum[:, n % 2, :], C.mat("headsum"), out[:, q, a:a + 512], start=True,
                              stop=True).then_inc(pstep, 1)
                for n, (q, a) in couple:
                    pe.matmul(C.psum[:, 4 + n % 2, :], g2[:, q * P:(q + 1) * P], sgate[:, a:a + 512], start=True,
                              stop=True)
                for n, (q, a) in couple:
                    pe.wait_ge(astep, other(n, 0))
                    pe.matmul(C.psum[:, 2 + n % 2, :], C.mat("headsum"), sq[:, n % 2], start=True,
                              stop=True).then_inc(pstep, 1)

        @block.scalar
        def _(act):
            for couple in couples:
                for n, (q, a) in couple:
                    act.wait_ge(dstep, dv(n, "center"))
                    nc.scalar.activation(sq[:, n % 2], out[:, q, a:a + 512], ACT.Square).then_inc(astep, 1)
                for n, (q, a) in couple:
                    act.wait_ge(dstep, dv(n, "rec"))
                    nc.scalar.activation(rstd[:, n % 2], rstd[:, n % 2], ACT.Sqrt).then_inc(astep, 1)

        @block.vector
        def _(dve):
            dve.wait_ge(loaded, 48)
            tt, ts, stt = nc.vector.tensor_tensor, nc.vector.tensor_scalar, nc.vector.scalar_tensor_tensor

            def step(couple, name, f, args):
                for n, (q, a) in couple:
                    if n // 2 or DV.index(name):
                        dve.wait_ge(dstep, max(dv(n, name) - 2, 1))
                    f(*args(n, q, out[:, q, a:a + 512], rstd[:, n % 2], slice(a, a + 512))).then_inc(dstep, 1)

            for couple in couples:
                last = couple[-1][0]
                step(couple, "sum", tt, lambda n, q, y, s, c: (y, yT[0][:, q, c], yT[1][:, q, c], ALU.add))
                dve.wait_ge(pstep, other(last, 0))
                step(couple, "center", stt, lambda n, q, y, s, c: (y, C.psum[:, n % 2, :], -1.0 / HD, y, ALU.mult,
                                                                  ALU.add))
                dve.wait_ge(pstep, other(last, 1))
                step(couple, "eps", ts, lambda n, q, y, s, c: (s, C.psum[:, 2 + n % 2, :], 1.0 / HD, LNX_EPS, ALU.mult,
                                                               ALU.add))
                step(couple, "rec", nc.vector.reciprocal, lambda n, q, y, s, c: (s, s))
                dve.wait_ge(astep, other(last, 1))
                step(couple, "scale", stt, lambda n, q, y, s, c: (y, y, C.par("lnx_w", q), s, ALU.mult, ALU.mult))
                step(couple, "bias", stt, lambda n, q, y, s, c: (y, y, C.par("lnx_b", q), bon[:, q, c], ALU.add,
                                                                ALU.add))
                step(couple, "gate", tt, lambda n, q, y, s, c: (y, y, C.psum[:, 4 + n % 2, :], ALU.mult))


def move(C, pairs):
    moved = C.sem("moved")
    with C.block() as block:
        @block.sync
        def _(sp):
            for dst, src in pairs:
                sp.dma_start(dst, src).then_inc(moved, 16)
            sp.wait_ge(moved, 16 * len(pairs))


def pad_keys(C, kraw, kr, vt):
    zero = C.slot(5, 1, P)[:, 0, :]
    cleared, stored = C.sem("cleared"), C.sem("stored")
    with C.block() as block:
        @block.gpsimd
        def _(pool):
            C.nc.gpsimd.memset(zero, 0.0).then_inc(cleared, 1)

        @block.sync
        def _(sp):
            sp.dma_start(kr[:, 0:CT], kraw[:, 0:CT]).then_inc(stored, 16)
            sp.wait_ge(cleared, 1)
            for a in (CT, CT + P + T):
                sp.dma_start(kr[:, a:a + P], zero).then_inc(stored, 16)
                sp.dma_start(vt[a:a + P, :], zero).then_inc(stored, 16)
            sp.wait_ge(stored, 80)

        @block.vector
        def _(dve):
            C.nc.vector.tensor_scalar(C.small[:, 8:8 + NQ], C.small[:, 0:NQ], -1.0, None, ALU.mult)


TWO_PI = 2.0 * np.pi
TP1 = 6.28125
TP2 = float(np.round((TWO_PI - TP1) * 2.0 ** 19) / 2.0 ** 19)
TP3 = float(TWO_PI - TP1 - TP2)
ROUND = 1.5 * 2.0 ** 23
PI_BELOW = 3.1415925


def position_tables(C, cos, sin, slot):
    nc, ins = C.nc, C.ins
    pi = C.slot(slot, 1, T, parts=QKD)[:, 0, :]
    ang, k, r = (C.slot(slot, 1, T, at=T * (1 + x), parts=QKD)[:, 0, :] for x in range(3))
    loaded, seq, done = C.sem("loaded"), C.sem("seq"), C.sem("done")
    with C.block() as block:
        @block.sync
        def _(sp):
            sp.dma_start(pi.bitcast(I32), ins["positions_2"].broadcast_to([QKD, T])).then_inc(loaded, 16)

        @block.vector
        def _(dve):
            n = [0]

            def step(f, *args):
                if n[0]:
                    dve.wait_ge(seq, n[0])
                f(*args).then_inc(seq, 1)
                n[0] += 1

            dve.wait_ge(loaded, 16)
            step(nc.vector.tensor_copy, ang, pi.bitcast(I32))
            step(nc.vector.tensor_scalar, ang, ang, C.mat("freq", QKD), None, ALU.mult)
            for x, (shift, out) in enumerate([(0.0, sin), (0.25, cos)]):
                step(nc.vector.tensor_scalar, k, ang, 1.0 / TWO_PI, shift, ALU.mult, ALU.add)
                step(nc.vector.tensor_scalar, k, k, ROUND, None, ALU.add)
                step(nc.vector.tensor_scalar, k, k, -ROUND, None, ALU.add)
                step(nc.vector.scalar_tensor_tensor, r, k, -TP1, ang, ALU.mult, ALU.add)
                step(nc.vector.scalar_tensor_tensor, r, k, -TP2, r, ALU.mult, ALU.add)
                step(nc.vector.scalar_tensor_tensor, r, k, -TP3, r, ALU.mult, ALU.add)
                step(nc.vector.tensor_scalar, r, r, shift * TWO_PI, PI_BELOW, ALU.add, ALU.min)
                step(nc.vector.tensor_scalar, out, r, -PI_BELOW, None, ALU.max)

        @block.scalar
        def _(act):
            act.wait_ge(seq, 18)
            nc.scalar.activation(sin, sin, ACT.Sin).then_inc(done, 1)
            nc.scalar.activation(cos, cos, ACT.Sin).then_inc(done, 1)


def silu_gate(C, y, gate, slot):
    nc = C.nc
    g = C.slot(slot, 2, T)
    s = C.slot(slot, 2, T, at=2 * T)
    loaded, sig, seq = C.pair("loaded"), C.sem("sig"), C.sem("seq")
    with C.block() as block:
        @block.sync
        def _(sp):
            for t in range(KD):
                if t >= 2:
                    sp.wait_ge(seq, 2 * (t - 1))
                sp.dma_start(g[:, t % 2], rows(gate, t)).then_inc(loaded[t % 2], 16)

        @block.scalar
        def _(act):
            for t in range(KD):
                act.wait_ge(loaded[t % 2], 16 * (t // 2 + 1))
                if t >= 2:
                    act.wait_ge(seq, 2 * (t - 1))
                nc.scalar.activation(s[:, t % 2], g[:, t % 2], ACT.Sigmoid).then_inc(sig, 1)

        @block.vector
        def _(dve):
            for t in range(KD):
                dve.wait_ge(loaded[t % 2], 16 * (t // 2 + 1))
                nc.vector.tensor_tensor(y[:, t, :], y[:, t, :], g[:, t % 2], ALU.mult).then_inc(seq, 1)
                dve.wait_ge(sig, t + 1)
                dve.wait_ge(seq, 2 * t + 1)
                nc.vector.tensor_tensor(y[:, t, :], y[:, t, :], s[:, t % 2], ALU.mult).then_inc(seq, 1)


def lru(C, u, y, slot):
    nc, ins = C.nc, C.ins
    NT = TW // P
    lam = C.small[:, 16:16 + NT]
    ex, sr, s2, acc, mx = (C.small[:, 22 + 6 * x:28 + 6 * x] for x in range(5))
    raw = C.slot(slot, 2, T + 4)
    xc, R, Ig, av, tv, rec = (C.slot(slot, 2, T, at=2 * (T + 4) + x * 2 * T) for x in range(6))
    blocks = C.slot(slot, 2, 2, P, at=2 * (T + 4) + 12 * T)
    cleared, dstep, astep, pstep = (C.sem(n) for n in ("cleared", "dstep", "astep", "pstep"))
    u_ready, w_ready = C.pair("u_ready"), C.pair("w_ready")
    CONV, MID, END = ["c0", "c1", "c2", "c3"], ["neg", "one", "rec", "sq", "gx"], ["gx2", "scan"]
    TERMS = 9
    N0 = 3 + 3 + 2 * TERMS + 4
    couples = [(t, t + 1) for t in range(0, NT, 2)]
    dve_order = [(t, s) for t in couples[0] for s in CONV]
    act_order = []
    for x, couple in enumerate(couples):
        dve_order += [(t, s) for t in couple for s in MID]
        dve_order += [(t, s) for t in (couples[x + 1] if x + 1 < len(couples) else ()) for s in CONV]
        dve_order += [(t, s) for t in couple for s in END]
        act_order += [(t, s) for t in couple for s in ("r", "i", "a", "t")] + [(t, "sqrt") for t in couple]

    def dv(t, name):
        return N0 + dve_order.index((t, name)) + 1

    def ac(t, name):
        return 1 + act_order.index((t, name)) + 1

    with C.block() as block:
        @block.gpsimd
        def _(pool):
            nc.gpsimd.memset(blocks, 0.0).then_inc(cleared, 1)
            nc.gpsimd.memset(raw, 0.0).then_inc(cleared, 1)

        @block.sync
        def _(sp):
            sp.wait_ge(cleared, 2)
            for t in range(NT):
                if t >= 2:
                    sp.wait_ge(dstep, dv(t - 2, "c3"))
                sp.dma_start(raw[:, t % 2, 3:3 + T], rows(u, t)).then_inc(u_ready[t % 2], 16)
                if t >= 2:
                    sp.wait_ge(pstep, t - 1)
                for x, w in enumerate(("lru_w_rgate_2", "lru_w_igate_2")):
                    for e in range(2):
                        sp.dma_start(blocks[64 * e:64 * e + 64, t % 2, x, 64 * e:64 * e + 64],
                                     ins[w][0, 2 * t + e, :, :]).then_inc(w_ready[t % 2], 16)

        @block.tensor
        def _(pe):
            for t in range(NT):
                pe.wait_ge(w_ready[t % 2], 64 * (t // 2 + 1))
                pe.wait_ge(dstep, dv(t, "c3"))
                if t > 1:
                    pe.wait_ge(astep, ac(t - 2, "i"))
                for x in range(2):
                    for c in range(2):
                        mm = pe.matmul(C.psum[:, 4 * (t % 2) + 2 * x + c, :], blocks[:, t % 2, x, :],
                                       xc[:, t % 2, c * 512:(c + 1) * 512],
                                       start=True, stop=True)
                mm.then_inc(pstep, 1)

        @block.scalar
        def _(act):
            act.wait_ge(dstep, 2)
            nc.scalar.activation(ex, mx, ACT.Exp, scale=-1.0).then_inc(astep, 1)
            act.wait_ge(dstep, N0)
            for t, name in act_order:
                b = t % 2
                ps = C.psum[:, 4 * b:4 * b + 4, :].rearrange("p (x a) b -> p x (a b)", x=2)
                if name == "r":
                    act.wait_ge(pstep, t + 1)
                    if t > 1:
                        act.wait_ge(dstep, dv(t - 2, "scan"))
                    nc.scalar.activation(R[:, b], ps[:, 0, :], ACT.Sigmoid, bias=C.par("lru_b_r", t)).then_inc(astep, 1)
                elif name == "i":
                    nc.scalar.activation(Ig[:, b], ps[:, 1, :], ACT.Sigmoid, bias=C.par("lru_b_i", t)).then_inc(astep, 1)
                elif name == "a":
                    act.wait_ge(astep, ac(t, "r"))
                    nc.scalar.activation(av[:, b], R[:, b], ACT.Exp, scale=lam[:, t:t + 1]).then_inc(astep, 1)
                elif name == "t":
                    nc.scalar.activation(tv[:, b], R[:, b], ACT.Tanh, scale=lam[:, t:t + 1]).then_inc(astep, 1)
                else:
                    act.wait_ge(dstep, dv(t, "sq"))
                    nc.scalar.activation(rec[:, b], rec[:, b], ACT.Sqrt).then_inc(astep, 1)

        @block.vector
        def _(dve):
            n = [0]
            tt, ts, stt = nc.vector.tensor_tensor, nc.vector.tensor_scalar, nc.vector.scalar_tensor_tensor

            def step(f, *args):
                if n[0]:
                    dve.wait_ge(dstep, n[0])
                f(*args).then_inc(dstep, 1)
                n[0] += 1

            lm = C.params[:, PARAM_ROWS["lru_lambda"]:PARAM_ROWS["lru_lambda"] + NT]
            step(ts, mx, lm, -1.0, None, ALU.mult)
            step(tt, mx, mx, lm, ALU.max)
            dve.wait_ge(astep, 1)
            step(ts, sr, ex, 2.0, None, ALU.add)
            step(nc.vector.reciprocal, sr, sr)
            step(tt, sr, sr, ex, ALU.mult)
            step(tt, s2, sr, sr, ALU.mult)
            for i in range(TERMS):
                c = 1.0 / (2 * (TERMS - 1 - i) + 1)
                step(tt, acc, acc if i else s2, s2, ALU.mult)
                step(ts, acc, acc, 1.0 if i else 0.0, c, ALU.mult, ALU.add)
            step(stt, acc, acc, 2.0, sr, ALU.mult, ALU.mult)
            step(ts, mx, lm, -1.0, 0.0, ALU.mult, ALU.max)
            step(tt, acc, acc, mx, ALU.add)
            step(ts, lam, acc, -8.0, None, ALU.mult)
            assert n[0] == N0
            for t, name in dve_order:
                b = t % 2
                x, i, r, v = xc[:, b], Ig[:, b], rec[:, b], tv[:, b]
                if name in CONV:
                    k = CONV.index(name)
                    w, shifted = C.par("lru_conv", 6 * k + t), raw[:, b, k:k + T]
                    if k == 0:
                        dve.wait_ge(u_ready[b], 16 * (t // 2 + 1))
                        if t > 1:
                            dve.wait_ge(pstep, t - 1)
                        step(ts, x, shifted, w, C.par("lru_conv_b", t), ALU.mult, ALU.add)
                    else:
                        step(stt, x, shifted, w, x, ALU.mult, ALU.add)
                elif name == "neg":
                    dve.wait_ge(astep, ac(t, "t"))
                    step(ts, v, v, -2.0, 2e-30, ALU.mult, ALU.max)
                elif name == "one":
                    step(ts, r, v, 0.5, 1.0, ALU.mult, ALU.add)
                elif name == "rec":
                    step(nc.vector.reciprocal, r, r)
                elif name == "sq":
                    step(tt, r, r, v, ALU.mult)
                elif name == "gx":
                    step(tt, i, i, x, ALU.mult)
                elif name == "gx2":
                    dve.wait_ge(astep, ac(t, "sqrt"))
                    step(tt, i, i, r, ALU.mult)
                else:
                    step(nc.vector.tensor_tensor_scan, y[:, t, :], av[:, b], i, 0.0, ALU.mult, ALU.add)


def block_kernel(nc, ins, out, stop=None):
    with ExitStack() as ctx:
        C = Core(nc, ctx, ins, out)
        C.ends = ctx.enter_context(nc.sbuf_tensor("ends", [P, 2, 2, PAIRS, NCH], F32))
        C.decay = ctx.enter_context(nc.sbuf_tensor("decay", [P, 2, PAIRS, NCH], F32))
        C.omka = ctx.enter_context(nc.sbuf_tensor("omka", [P, PAIRS], F32))
        full, full_r = C.slot, C.slot_r
        w_in = ins["w_in"][0, :, :]

        with C.stage():
            setup(C)
        mod = lambda part, v: (lambda k: C.mod[:, part * KD + k, v:v + 1])
        gain = lambda n: (lambda k: C.gain[:, n, k:k + 1])
        par = lambda name, j=0: (lambda k: C.par(name, j + k))

        xT, cT = full(0, KD, T), full(1, KD, CT)
        at_h = 2 * SLOT + SLOT // 4
        hT = full(0, KD, ALL, at=at_h)
        h_hi, h_lo = full_r(1, KD, ALL), full_r(3.5, KD, ALL)
        memT = full(5.5, KD, 256)
        with C.together():
            turn_in(C, ins["x"][0, :, :], xT, T, D, 0, 5)
            turn_in(C, ins["ctx"][0, :, :], cT, CT, D, 0, 5.25)
            turn_in(C, ins["mem_2"][0, :, :], memT, 256, D, 0, 4.5)
            modulation(C)

        km = [C.scratch(f"km{l}", 256, 256) for l in range(2)]
        vm = [C.scratch(f"vm{l}", 256, 256) for l in range(2)]
        with C.together():
            norm(C, cT, hT[:, :, 0:CT], CT, KD, 5.25, gain(1), mod(0, 1))
            norm(C, xT, hT[:, :, CT:ALL], T, KD, 5.75, gain(0), mod(0, 0))
            for l in range(2):
                linear_tok(C, memT, ins["w_mem_kv_2"][l, :, 256:512], 256, KD, 2, (4.5625, 4.875)[l], vm[l])
            mem_r = [full_r(s, KD, 256) for s in (1.25, 1.5)]
            linears(C, [job(ins["w_mem_kv_2"][l, :, :], 2, *mem_r, KD, n_tok=256, dram=km[l]) for l in range(2)], 3.5,
                    splits=[(memT, *mem_r)])

        qraw, qr = C.scratch("qraw", AW, T), C.scratch("qr", AW, T)
        kraw, kr = C.scratch("kraw", P, ALL), C.scratch("kr", P, KP)
        vt = C.scratch("vt", KP, P)
        rw = C.scratch("rw", 3 * RW + DL + IL + GL, ALL)
        gates = C.scratch("gates", 2 * D, T)
        cols = lambda c0: w_in[:, c0:]
        with C.together():
            linear_tok(C, hT, w_in[:, C_V:C_V + P], P, KD, ALL // P, 4.75, vt, row=lambda t: t + (t >= CT // P))
            hh = dict(hi=h_hi, lo=h_lo, kt=KD)
            linears(C, [job(cols(C_Q), AW // P, **hh, tok0=CT, dram=qraw),
                        job(cols(C_K), 1, **hh, n_tok=ALL, dram=kraw),
                        job(cols(C_R), 3 * RW // P, **hh, n_tok=ALL, dram=rw),
                        job(cols(C_HW), 1, **hh, n_tok=ALL, width=DL + IL, dram=rw[3 * RW:3 * RW + DL + IL, :]),
                        job(cols(C_HG), 1, **hh, n_tok=ALL, width=GL, dram=rw[3 * RW + DL + IL:, :]),
                        job(cols(C_G), 2 * D // P, **hh, tok0=CT, dram=gates, func=ACT.Sigmoid)],
                    SLOTS - (6 * KD * P + 2 * ALL) / SLOT, splits=[(hT, h_hi, h_lo)])

        ya = C.scratch("ya", AW, T)
        axial = full(4, 2, T)
        with C.together():
            pad_keys(C, kraw, kr, vt)
            move(C, [(axial, ins["k_axial"].rearrange("a p n -> p a n"))])
        with C.together():
            rotate(C, qraw, qr, AW // P, P, T, C.mat("rot"), axial[:, 0, :], axial[:, 1, :], 5)
            rotate(C, kraw[:, CT:ALL], None, 1, P, T, C.mat("rot"), axial[:, 0, :], axial[:, 1, :], 4.25,
                   dst_rows=lambda t: kr[:, CT + P:CT + P + T])
        with C.stage():
            window_attention(C, qr, kr, vt, ya)

        chunked = C.scratch("chunked", 2, NCH, P, 4, PAIRS, CH)
        v_chunked = C.scratch("v_chunked", NCH, P, PAIRS, CH)
        bonus, gate_in = C.scratch("bonus", RW, T), C.scratch("gate_in", GL, T)
        with C.stage():
            rwkv_prepare(C, rw, chunked, v_chunked, bonus, gate_in)
        yT = [full(5, PAIRS, T), full(5, PAIRS, T, at=PAIRS * T)]
        with C.stage():
            recurrence(C, chunked, v_chunked, yT)
        yr, yaT = full(1, PAIRS, T), full(1, PAIRS, T, at=PAIRS * T)
        with C.together():
            rwkv_output(C, yT, bonus, gate_in, yr, 2)
            move(C, [(yaT, ya.rearrange("(k p) n -> p k n", p=P))])

        merged, x1 = full(3, KD, T), full(1, KD, T)
        with C.stage():
            yr_r, ya_r = ([full_r(s, PAIRS, T, at=at) for s in (2, 4)] for at in (0, PAIRS * T))
            linears(C, [job(ins["w_branch_attn"][0, :, :], KD, *ya_r, AW // P, mul=gates[0:D, :], res=merged),
                        job(ins["w_branch_rwkv"][0, :, :], KD, *yr_r, RW // P, mul=gates[D:2 * D, :], add=merged,
                            res=merged)],
                    5, kind="combine", splits=[(yaT, *ya_r), (yr, *yr_r)])
        with C.stage():
            m_r = [full_r(s, KD, T) for s in (2, 4)]
            linears(C, [job(ins["w_out"][0, :, :], KD, *m_r, KD, col=2 * KD, add=xT, res=x1)], 5, kind="combine",
                    splits=[(merged, *m_r)])

        h2 = full(2, KD, T)
        with C.stage():
            norm(C, x1, h2, T, KD, 5, gain(2), mod(3, 0))
        h2_r, hid = [full_r(s, KD, T) for s in (3, 4)], [full_r(s, KD, T) for s in (0, 2)]
        with C.stage():
            split(C, h2, *h2_r)
        with C.stage():
            linears(C, [jb for p in range(DFF // D) for jb in (
                job(ins["w_mlp_up"][0, :, p * D:], KD, *h2_r, KD, res=hid, kind="sqrelu"),
                job(ins["w_mlp_down"][0, p * D:(p + 1) * D, :], KD, *hid, KD, col=5 * KD, add=x1, res=x1,
                    kind="combine", own=True))], 5)
        h = full(0, KD, T)
        with C.stage():
            norm(C, x1, h, T, KD, 5, par("norm_f_g"))

        y2, mixed = full(1, KD, T), full(2, KD, T)
        gate = [C.scratch(f"gate{l}", D, T) for l in range(2)]
        qm = [C.scratch(f"qm{l}", 256, T) for l in range(2)]
        mem_out = [C.scratch(f"mem_out{l}", 256, T) for l in range(2)]

        def finish_layer(l, before):
            with C.together():
                if before:
                    move(C, before)
                memory_attention(C, qm[l], km[l], vm[l], mem_out[l])
            with C.stage():
                move(C, [(y2[:, TW // P:KD, :], mem_out[l].rearrange("(k p) n -> p k n", p=P))])
            with C.stage():
                silu_gate(C, y2, gate[l], 3)
            with C.stage():
                y_r = [full_r(s, KD, T) for s in (4, 5)]
                linears(C, [job(ins["w_out_2"][l, :, :], KD, *y_r, KD, add=h, scale=ALPHA, res=mixed)], 3,
                        kind="combine", splits=[(y2, *y_r)])
            with C.stage():
                norm(C, mixed, h, T, KD, 5, par("ln_g", 8 * l), par("ln_b", 8 * l), center=True)

        wm = ins["mla_w_in_2"][0, :, :]
        z = full(1, 5, T)
        kr96, krot = C.scratch("kr96", QKD, T), C.scratch("krot", QKD, T)
        q96, q96r = C.scratch("q96", TH * QKD, T), C.scratch("q96r", TH * QKD, T)
        kn, v2, tok = C.scratch("kn", TH * QKN, T), C.scratch("v2", T, TW), C.scratch("tok", TW, T)
        c_g = QL + KVL + QKR
        hr = [full_r(s, KD, T) for s in (2, 3)]
        with C.stage():
            linears(C, [job(wm, 5, *hr, KD, res=z),
                        job(wm[:, QL + KVL - QKN:], 1, *hr, KD, width=QKD, dram=kr96),
                        job(wm[:, c_g:], KD, *hr, KD, dram=gate[0]),
                        job(wm[:, c_g + D:], 2, *hr, KD, dram=qm[0])], 4, splits=[(h, *hr)])
        zq, zk = z[:, 0:3, :], z[:, 3:5, :]
        cos, sin = (full(5, 1, T, at=x * T, parts=QKD)[:, 0, :] for x in range(2))
        with C.together():
            norm(C, zq, zq, T, 3, 2, par("q_norm"))
            norm(C, zk, zk, T, 2, 2.5, par("kv_norm"))
            position_tables(C, cos, sin, 3)
        wkv = ins["mla_w_ukv_2"][0, :, :]
        def values(k):
            return wkv[k * P:(k + 1) * P, :].rearrange("p (h c) -> p h c", c=QKN + HD)[:, :, QKN:]

        def keys_of_two_heads(t, b):
            return [(b[:, :, e * QKN:(e + 1) * QKN], wkv[:, bass.ds(t * (2 * (QKN + HD)) + e * (QKN + HD), QKN)]
                     .rearrange("(k p) n -> p k n", p=P)) for e in range(2)]

        with C.together():
            linear_tok(C, zk, values, TW, 2, T // P, 5.25, v2, w_view=lambda b: b.rearrange("p (h c) -> p h c", c=HD))
            z_hi, z_lo = full_r(2, 5, T), full_r(4, 5, T)
            linears(C, [job(ins["mla_w_uq_2"][0, :, :], TH * QKD // P, z_hi[:, 0:3, :], z_lo[:, 0:3, :], 3, dram=q96),
                        job(None, TH * QKN // P, z_hi[:, 3:5, :], z_lo[:, 3:5, :], 2, dram=kn,
                            w_view=keys_of_two_heads, w_parts=2)], 3, splits=[(z, z_hi, z_lo)])
        with C.together():
            rotate(C, q96, q96r, TH, QKD, T, C.mat("rot_mla", QKD), cos, sin, 4)
            rotate(C, kr96, krot, 1, QKD, T, C.mat("rot_mla", QKD), cos, sin, 3)
        with C.stage():
            latent_attention(C, q96r, kn, krot[QKN:QKD, :], v2, tok)
        finish_layer(0, [(y2[:, 0:TW // P, :], tok.rearrange("(k p) n -> p k n", p=P))])

        wl = ins["lru_w_in_2"][0, :, :]
        u = C.scratch("u", TW, T)
        with C.stage():
            linears(C, [job(wl, TW // P, *hr, KD, dram=u),
                        job(wl[:, TW:], KD, *hr, KD, dram=gate[1]),
                        job(wl[:, TW + D:], 2, *hr, KD, dram=qm[1])], 4, splits=[(h, *hr)])
        with C.stage():
            lru(C, u, y2, 3)
        finish_layer(1, [])
        with C.stage():
            turn_out(C, h, out[0, :, :], T, 5)


_INS = ["x", "c", "ctx", "c_ctx", "w_ada", "b_ada", "norm1_g", "w_in", "sink", "conv_w", "decay_w0", "decay_w2",
        "iclr_a0", "iclr_a2", "gate_g2", "k_k", "k_a", "r_k", "lnx_w", "lnx_b", "w_branch_attn", "w_branch_rwkv",
        "w_out", "norm2_g", "w_mlp_up", "w_mlp_down", "norm_f_g", "mem_2", "positions_2", "mla_w_in_2",
        "mla_q_norm_2", "mla_w_uq_2", "mla_kv_norm_2", "mla_w_ukv_2", "lru_w_in_2", "lru_conv_w_2",
        "lru_conv_b_2", "lru_w_rgate_2", "lru_b_rgate_2", "lru_w_igate_2", "lru_b_igate_2", "lru_lambda_2",
        "w_mem_kv_2", "w_out_2", "ln_g_2", "ln_b_2"]


def kernel(**inputs):
    import concourse.bacc as bacc
    from concourse.bass_utils import run_bass_kernel_spmd as run

    nc = bacc.Bacc("TRN2", target_bir_lowering=False, num_devices=1)
    arrays, ins = {}, {}
    given = {n: np.ascontiguousarray(inputs[n]) for n in _INS}
    given.update(shape_constants())
    for name, a in given.items():
        arrays[f"in_{name}"] = a
        ins[name] = nc.dram_tensor(f"in_{name}", a.shape, mybir.dt.from_np(a.dtype), kind="ExternalInput").ap()
    out = nc.dram_tensor("out_0", (1, T, D), F32, kind="ExternalOutput").ap()
    block_kernel(nc, ins, out)
    r = run(nc, [arrays], core_ids=[0])
    return r.results[0]["out_0"]
```
